# Optimizing a Trainium2 kernel written in Bass

```python
import jax, jax.numpy as jnp
from jax import lax
import numpy as np

D_MODEL = 1024
BATCH = 1
SEQ = 1024
DEPTH = 1

ROPE_THETA = 500000.0
NORM_EPS = 1e-5
NEG_INF = -1e30
POS_INF = 1e30
Q_BLOCK = 128

MLA_HEADS = 8
MLA_NOPE_DIM = 64
MLA_ROPE_DIM = 32
MLA_V_DIM = 64
MLA_Q_RANK = 256
MLA_KV_RANK = 128

NSA_HEADS = 8
NSA_KV_HEADS = 2
NSA_GROUP = NSA_HEADS // NSA_KV_HEADS
NSA_HEAD_DIM = 64
NSA_ROPE_DIM = NSA_HEAD_DIM // 4
CMP_BLOCK = 32
CMP_STRIDE = 16
CMP_HIDDEN = 2 * NSA_HEAD_DIM
SEL_BLOCK = 64
N_SEL = 16
N_LOCAL_SEL = 2
WINDOW = 512
NSA_Q_BLOCK = 64

MIX_WIDTH = MLA_HEADS * MLA_V_DIM + NSA_HEADS * NSA_HEAD_DIM
NSA_KV_WIDTH = NSA_KV_HEADS * NSA_HEAD_DIM
IN_SPLITS = (MLA_Q_RANK, MLA_KV_RANK, MLA_ROPE_DIM, NSA_HEADS * NSA_HEAD_DIM) + (NSA_KV_WIDTH,) * 6 + (3 * NSA_HEADS,)
IN_COLS = sum(IN_SPLITS)

N_EXPERTS = 32
TOP_K = 4
D_FF = D_MODEL
SWIGLU_LIMIT = 7.0
SWIGLU_ALPHA = 1.702
MOE_BLOCK = 128

kernel_name = 'hybrid_mla_nsa_moe_layer'

def rms_norm(x, g):
    xf = x.astype(jnp.float32)
    y = xf * lax.rsqrt(jnp.mean(xf * xf, axis=-1, keepdims=True) + NORM_EPS)
    return (y * g.astype(jnp.float32)).astype(x.dtype)

def rope_cos_sin(pos, rot_dim):
    inv_freq = ROPE_THETA ** (-jnp.arange(0, rot_dim, 2, dtype=jnp.float32) / rot_dim)
    ang = pos.astype(jnp.float32)[..., None] * inv_freq
    return jnp.cos(ang), jnp.sin(ang)

def apply_rope(x, cos, sin):
    half = cos.shape[-1]
    c = cos[:, :, None, :].astype(x.dtype)
    s = sin[:, :, None, :].astype(x.dtype)
    x1, x2, rest = x[..., :half], x[..., half:2 * half], x[..., 2 * half:]
    return jnp.concatenate([x1 * c - x2 * s, x2 * c + x1 * s, rest], axis=-1)

def masked_softmax(s, mask):
    return jax.nn.softmax(jnp.where(mask, s, NEG_INF), axis=-1)

def mla_mixer(q_lat, kv_lat, k_pe, cos, sin, q_norm, w_q_up, kv_norm, w_kv_up):
    B, S, _ = q_lat.shape
    q = (rms_norm(q_lat, q_norm) @ w_q_up).reshape(B, S, MLA_HEADS, MLA_NOPE_DIM + MLA_ROPE_DIM)
    kv = (rms_norm(kv_lat, kv_norm) @ w_kv_up).reshape(B, S, MLA_HEADS, MLA_NOPE_DIM + MLA_V_DIM)
    k_nope, v = kv[..., :MLA_NOPE_DIM], kv[..., MLA_NOPE_DIM:]
    q = jnp.concatenate([q[..., :MLA_NOPE_DIM], apply_rope(q[..., MLA_NOPE_DIM:], cos, sin)], axis=-1)
    k_pe = apply_rope(k_pe[:, :, None, :], cos, sin)
    k = jnp.concatenate([k_nope, jnp.broadcast_to(k_pe, (B, S, MLA_HEADS, MLA_ROPE_DIM))], axis=-1)
    scale = (MLA_NOPE_DIM + MLA_ROPE_DIM) ** -0.5
    k_pos = jnp.arange(S)

    def block(i):
        q0 = i * Q_BLOCK
        qb = lax.dynamic_slice_in_dim(q, q0, Q_BLOCK, axis=1)
        s = jnp.einsum('bqhd,bkhd->bhqk', qb, k).astype(jnp.float32) * scale
        q_pos = q0 + jnp.arange(Q_BLOCK)
        p = masked_softmax(s, k_pos[None, :] <= q_pos[:, None])
        return jnp.einsum('bhqk,bkhd->bqhd', p.astype(v.dtype), v)

    o = lax.map(block, jnp.arange(S // Q_BLOCK))
    return jnp.moveaxis(o, 0, 1).reshape(B, S, MLA_HEADS * MLA_V_DIM)

def compress(kv, pos_emb, w1, w2):
    S = kv.shape[1]
    n_cmp = (S - CMP_BLOCK) // CMP_STRIDE + 1
    idx = jnp.arange(n_cmp)[:, None] * CMP_STRIDE + jnp.arange(CMP_BLOCK)[None, :]
    blocks = kv[:, idx] + pos_emb[:, None, :]
    hid = jax.nn.silu(jnp.einsum('bnlgd,ldh->bngh', blocks, w1))
    return hid @ w2

def nsa_mixer(q, k_c, v_c, k_s, v_s, k_w, v_w, gate_logits, pos, cos, sin, cmp_pos, cmp_w1, cmp_w2):
    B, S, _ = q.shape
    G, Hg, dh = NSA_KV_HEADS, NSA_GROUP, NSA_HEAD_DIM
    scale = dh ** -0.5
    q = apply_rope(q.reshape(B, S, NSA_HEADS, dh), cos, sin).reshape(B, S, G, Hg, dh)
    kv_shape = (B, S, G, dh)
    k_c, v_c, k_s, v_s, k_w, v_w = [t.reshape(kv_shape) for t in (k_c, v_c, k_s, v_s, k_w, v_w)]
    k_s = apply_rope(k_s, cos, sin)
    k_w = apply_rope(k_w, cos, sin)
    t = jnp.arange(S)

    n_cmp = (S - CMP_BLOCK) // CMP_STRIDE + 1
    cmp_start = jnp.arange(n_cmp) * CMP_STRIDE
    cmp_end = cmp_start + CMP_BLOCK - 1
    kc = compress(k_c, cmp_pos[0], cmp_w1[0], cmp_w2[0])
    vc = compress(v_c, cmp_pos[1], cmp_w1[1], cmp_w2[1])
    ccos, csin = rope_cos_sin(pos[:, cmp_end], NSA_ROPE_DIM)
    kc = apply_rope(kc, ccos, csin)
    s_cmp = jnp.einsum('bsghd,bngd->bghsn', q, kc).astype(jnp.float32) * scale
    p_cmp = masked_softmax(s_cmp, cmp_end[None, :] <= t[:, None]) * (t >= CMP_BLOCK - 1)[:, None]
    o_cmp = jnp.einsum('bghsn,bngd->bsghd', p_cmp.astype(vc.dtype), vc)

    n_sel = S // SEL_BLOCK
    j = jnp.arange(n_sel)
    overlap = ((cmp_start[:, None] < (j[None, :] + 1) * SEL_BLOCK)
               & (cmp_start[:, None] + CMP_BLOCK > j[None, :] * SEL_BLOCK)).astype(jnp.float32)
    imp = jnp.einsum('bghsn,nj->bgsj', p_cmp, overlap)
    cur = (t // SEL_BLOCK)[:, None]
    forced = (j[None, :] == 0) | ((j[None, :] <= cur) & (j[None, :] > cur - N_LOCAL_SEL))
    imp = jnp.where(forced, POS_INF, jnp.where(j[None, :] <= cur, imp, NEG_INF))
    k_top = min(N_SEL, n_sel)
    _, sel_idx = lax.top_k(imp, k_top)

    ks_blocks = k_s.reshape(B, n_sel, SEL_BLOCK, G, dh).transpose(0, 3, 1, 2, 4)
    vs_blocks = v_s.reshape(B, n_sel, SEL_BLOCK, G, dh).transpose(0, 3, 1, 2, 4)
    gather = jax.vmap(jax.vmap(lambda blk, ix: blk[ix]))
    k_w_pad = jnp.pad(k_w, ((0, 0), (WINDOW, 0), (0, 0), (0, 0)))
    v_w_pad = jnp.pad(v_w, ((0, 0), (WINDOW, 0), (0, 0), (0, 0)))
    n_keys_sel = k_top * SEL_BLOCK

    def block(i):
        q0 = i * NSA_Q_BLOCK
        qb = lax.dynamic_slice_in_dim(q, q0, NSA_Q_BLOCK, axis=1)
        q_pos = q0 + jnp.arange(NSA_Q_BLOCK)
        ib = lax.dynamic_slice_in_dim(sel_idx, q0, NSA_Q_BLOCK, axis=2)
        kg = gather(ks_blocks, ib).reshape(B, G, NSA_Q_BLOCK, n_keys_sel, dh)
        vg = gather(vs_blocks, ib).reshape(B, G, NSA_Q_BLOCK, n_keys_sel, dh)
        key_pos = (ib[..., None] * SEL_BLOCK + jnp.arange(SEL_BLOCK)).reshape(B, G, NSA_Q_BLOCK, n_keys_sel)
        s_sel = jnp.einsum('bqghd,bgqkd->bghqk', qb, kg).astype(jnp.float32) * scale
        p_sel = masked_softmax(s_sel, (key_pos <= q_pos[:, None])[:, :, None])
        o_sel = jnp.einsum('bghqk,bgqkd->bqghd', p_sel.astype(vg.dtype), vg)
        kwb = lax.dynamic_slice_in_dim(k_w_pad, q0, NSA_Q_BLOCK + WINDOW, axis=1)
        vwb = lax.dynamic_slice_in_dim(v_w_pad, q0, NSA_Q_BLOCK + WINDOW, axis=1)
        w_pos = q0 - WINDOW + jnp.arange(NSA_Q_BLOCK + WINDOW)
        w_mask = ((w_pos[None, :] <= q_pos[:, None]) & (w_pos[None, :] > q_pos[:, None] - WINDOW)
                  & (w_pos[None, :] >= 0))
        s_win = jnp.einsum('bqghd,bkgd->bghqk', qb, kwb).astype(jnp.float32) * scale
        p_win = masked_softmax(s_win, w_mask)
        o_win = jnp.einsum('bghqk,bkgd->bqghd', p_win.astype(vwb.dtype), vwb)
        return o_sel, o_win

    o_sel, o_win = lax.map(block, jnp.arange(S // NSA_Q_BLOCK))
    o_sel = jnp.moveaxis(o_sel, 0, 1).reshape(B, S, G, Hg, dh)
    o_win = jnp.moveaxis(o_win, 0, 1).reshape(B, S, G, Hg, dh)
    gates = jax.nn.sigmoid(gate_logits.astype(jnp.float32)).reshape(B, S, G, Hg, 3).astype(q.dtype)
    o = gates[..., 0:1] * o_cmp + gates[..., 1:2] * o_sel + gates[..., 2:3] * o_win
    return o.reshape(B, S, NSA_HEADS * dh)

def moe_ffn(h, router_w, router_b, w1, b1, w2, b2):
    B, S, D = h.shape
    xt = h.reshape(-1, D)
    N = xt.shape[0]
    logits = (xt @ router_w + router_b).astype(jnp.float32)
    top_val, top_idx = lax.top_k(logits, TOP_K)
    gate = jax.nn.softmax(top_val, axis=-1)
    flat_e = top_idx.reshape(-1)
    flat_tok = jnp.repeat(jnp.arange(N, dtype=jnp.int32), TOP_K)
    order = jnp.argsort(flat_e)
    se, stok, sgate = flat_e[order], flat_tok[order], gate.reshape(-1)[order]
    counts = jnp.bincount(flat_e, length=N_EXPERTS)
    padded = ((counts + MOE_BLOCK - 1) // MOE_BLOCK) * MOE_BLOCK
    start = jnp.cumsum(counts) - counts
    pend = jnp.cumsum(padded)
    pstart = pend - padded
    dest = pstart[se] + (jnp.arange(N * TOP_K) - start[se])
    n_blocks = -(-(N * TOP_K) // MOE_BLOCK) + N_EXPERTS
    n_rows = n_blocks * MOE_BLOCK
    row_tok = jnp.zeros((n_rows,), jnp.int32).at[dest].set(stok)
    row_gate = jnp.zeros((n_rows,), xt.dtype).at[dest].set(sgate.astype(xt.dtype))
    block_expert = jnp.minimum(jnp.searchsorted(pend, jnp.arange(n_blocks) * MOE_BLOCK, side='right'),
                               N_EXPERTS - 1)

    def expert_block(args):
        tok, e, g = args
        hcat = xt[tok] @ w1[e] + b1[e]
        a = jnp.minimum(hcat[:, :D_FF], SWIGLU_LIMIT)
        up = jnp.clip(hcat[:, D_FF:], -SWIGLU_LIMIT, SWIGLU_LIMIT)
        glu = a * jax.nn.sigmoid(SWIGLU_ALPHA * a)
        return (((up + 1.0) * glu) @ w2[e] + b2[e]) * g[:, None]

    y = lax.map(expert_block, (row_tok.reshape(n_blocks, MOE_BLOCK), block_expert,
                               row_gate.reshape(n_blocks, MOE_BLOCK)))
    out = jax.ops.segment_sum(y.reshape(n_rows, D), row_tok, num_segments=N)
    return out.reshape(B, S, D)

def setup_inputs(seed: int = 0) -> dict:
    key = jax.random.key(seed)
    ks = jax.random.split(key, 24)
    f32 = jnp.float32
    L = DEPTH

    def normal(k, shape, scale):
        return jax.random.normal(k, shape, f32) * scale

    def gain(k, shape):
        return 1.0 + 0.02 * jax.random.normal(k, shape, f32)

    x = normal(ks[0], (BATCH, SEQ, D_MODEL), 1.0)
    positions = (jnp.arange(SEQ, dtype=jnp.int32)[None, :]
                 + jax.random.randint(ks[1], (BATCH, 1), 0, 1024, dtype=jnp.int32))
    return {
        'x': x,
        'positions': positions,
        'attn_norm': gain(ks[2], (L, D_MODEL)),
        'w_in': normal(ks[3], (L, D_MODEL, IN_COLS), D_MODEL ** -0.5),
        'mla_q_norm': gain(ks[4], (L, MLA_Q_RANK)),
        'mla_w_q_up': normal(ks[5], (L, MLA_Q_RANK, MLA_HEADS * (MLA_NOPE_DIM + MLA_ROPE_DIM)), MLA_Q_RANK ** -0.5),
        'mla_kv_norm': gain(ks[6], (L, MLA_KV_RANK)),
        'mla_w_kv_up': normal(ks[7], (L, MLA_KV_RANK, MLA_HEADS * (MLA_NOPE_DIM + MLA_V_DIM)), MLA_KV_RANK ** -0.5),
        'nsa_cmp_pos': normal(ks[8], (L, 2, CMP_BLOCK, NSA_HEAD_DIM), 0.1),
        'nsa_cmp_w1': normal(ks[9], (L, 2, CMP_BLOCK, NSA_HEAD_DIM, CMP_HIDDEN), (CMP_BLOCK * NSA_HEAD_DIM) ** -0.5),
        'nsa_cmp_w2': normal(ks[10], (L, 2, CMP_HIDDEN, NSA_HEAD_DIM), CMP_HIDDEN ** -0.5),
        'w_out': normal(ks[11], (L, MIX_WIDTH, D_MODEL), MIX_WIDTH ** -0.5),
        'ffn_norm': gain(ks[12], (L, D_MODEL)),
        'router_w': normal(ks[13], (L, D_MODEL, N_EXPERTS), D_MODEL ** -0.5),
        'router_b': normal(ks[14], (L, N_EXPERTS), 0.01),
        'moe_w1': normal(ks[15], (L, N_EXPERTS, D_MODEL, 2 * D_FF), D_MODEL ** -0.5),
        'moe_b1': normal(ks[16], (L, N_EXPERTS, 2 * D_FF), 0.02),
        'moe_w2': normal(ks[17], (L, N_EXPERTS, D_FF, D_MODEL), D_FF ** -0.5),
        'moe_b2': normal(ks[18], (L, N_EXPERTS, D_MODEL), 0.02),
        'final_norm': gain(ks[19], (D_MODEL,)),
    }

def reference(x, positions, attn_norm, w_in, mla_q_norm, mla_w_q_up, mla_kv_norm, mla_w_kv_up,
              nsa_cmp_pos, nsa_cmp_w1, nsa_cmp_w2, w_out, ffn_norm, router_w, router_b,
              moe_w1, moe_b1, moe_w2, moe_b2, final_norm):
    cos_mla, sin_mla = rope_cos_sin(positions, MLA_ROPE_DIM)
    cos_nsa, sin_nsa = rope_cos_sin(positions, NSA_ROPE_DIM)
    split_at = np.cumsum(IN_SPLITS)[:-1].tolist()
    h = x
    for l in range(DEPTH):
        u = rms_norm(h, attn_norm[l])
        (q_lat, kv_lat, k_pe, q_nsa, k_c, v_c, k_s, v_s, k_w, v_w, g_nsa) = jnp.split(u @ w_in[l], split_at, axis=-1)
        o_mla = mla_mixer(q_lat, kv_lat, k_pe, cos_mla, sin_mla,
                          mla_q_norm[l], mla_w_q_up[l], mla_kv_norm[l], mla_w_kv_up[l])
        o_nsa = nsa_mixer(q_nsa, k_c, v_c, k_s, v_s, k_w, v_w, g_nsa, positions, cos_nsa, sin_nsa,
                          nsa_cmp_pos[l], nsa_cmp_w1[l], nsa_cmp_w2[l])
        h = h + jnp.concatenate([o_mla, o_nsa], axis=-1) @ w_out[l]
        h = h + moe_ffn(rms_norm(h, ffn_norm[l]), router_w[l], router_b[l],
                        moe_w1[l], moe_b1[l], moe_w2[l], moe_b2[l])
    return rms_norm(h, final_norm)


_drawn_inputs = setup_inputs


def setup_inputs(seed=0):
    import zlib

    import numpy as np

    out = dict(_drawn_inputs(seed))
    spreads = {}
    factors = {'mla_q_norm': 4.176,
     'mla_kv_norm': 3.027,
     'moe_b1': 5.156,
     'moe_b2': 5.945,
     'final_norm': 22.744,
     'router_b': 3.167,
     'nsa_cmp_pos': 2.846}
    for name, (base, spread) in spreads.items():
        noise = np.random.default_rng([zlib.crc32(name.encode()), seed]).standard_normal(out[name].shape)
        drawn = base * np.exp(spread * noise) if base else spread * noise
        out[name] = __import__('jax').numpy.asarray(drawn.astype(out[name].dtype))
    for name, factor in factors.items():
        out[name] = (out[name] * factor).astype(out[name].dtype)
    return out
```

```python
from contextlib import ExitStack

import numpy as np

import concourse.bass as bass
from concourse import mybir
from concourse.alu_op_type import AluOpType as ALU

F32 = mybir.dt.float32
BF16 = mybir.dt.bfloat16
I32 = mybir.dt.int32
U32 = mybir.dt.uint32
ACT = mybir.ActivationFunctionType
AX_X = mybir.AxisListType.X
AX_XY = mybir.AxisListType.XY

P = 128
SEQ, D = 1024, 1024
NT, KT = SEQ // P, D // P
EPS = 1e-5
NEG = -1e30
THETA = 500000.0

H_MLA, NOPE, ROPE, V_DIM = 8, 64, 32, 64
QK_MLA = NOPE + ROPE
Q_RANK, KV_RANK = 256, 128
H_NSA, G_NSA, DH, ROPE_N = 8, 2, 64, 16
CMP_BLOCK, CMP_STRIDE, CMP_HID = 32, 16, 128
N_CMP = (SEQ - CMP_BLOCK) // CMP_STRIDE + 1
WINDOW = 512
WT = WINDOW // P
KVW = G_NSA * DH
IN_COLS = Q_RANK + KV_RANK + ROPE + H_NSA * DH + 6 * KVW + 3 * H_NSA
C_Q, C_KV = 0, Q_RANK
C_PE = C_KV + KV_RANK
C_QN = C_PE + ROPE
C_KC = C_QN + H_NSA * DH
C_KW = C_KC + 4 * KVW
NF = ROPE // 2 + ROPE_N // 2

NE, TOPK, DFF = 32, 4, 1024
LIMIT, ALPHA = 7.0, 1.702
CAP = 192
VARIANTS = (128, 144, 160, 176, CAP)
MORE = (SEQ - 1) // CAP
MAX_ITEMS = P
DUMP = 256
FC = 8
DC = 4

TWO_PI = 2.0 * np.pi
C1 = 6.28125
C2 = float(np.float32(np.round((TWO_PI - C1) * 2.0 ** 20) / 2.0 ** 20))
C3 = float(TWO_PI - C1 - C2)
ROUND = 12582912.0
PI_IN = 3.1415925


class Steps:

    def __init__(self, sem, base=0):
        self.sem, self.base, self.n = sem, base, 0

    def mark(self, ins):
        ins.then_inc(self.sem, 1)
        self.n += 1
        return ins

    def wait(self, eng):
        eng.wait_ge(self.sem, self.base + self.n)


def hold(eng, sem, value, passed):
    eng.wait_ge(sem, value)
    eng.sem_inc(passed, 1)


def frequencies():
    def inv(rot):
        return np.float32(THETA ** (-np.arange(0, rot, 2) / rot))
    return [float(f) for f in np.concatenate([inv(ROPE), inv(ROPE_N)])]


class Mem:

    def __init__(self, nc, ctx, sems=None):
        self.nc, self.ctx, self.sems = nc, ctx, sems

    def sb(self, name, shape, dt=F32):
        return self.ctx.enter_context(self.nc.sbuf_tensor(name, shape, dt))

    def ps(self, name, shape, dt=F32):
        return self.ctx.enter_context(self.nc.psum_tensor(name, shape, dt))

    def sem(self, name):
        self.sems.append(self.nc.alloc_semaphore(name=name))
        return self.sems[-1]


def constants(nc, C, a):
    with ExitStack() as ctx:
        M = Mem(nc, ctx, C["sems"])
        rows = M.sb("rows", [19, P])
        rows_b1 = M.sb("rows_b1", [P, 4, P])
        rows_b2 = M.sb("rows_b2", [P, 2, P])
        pos_i = M.sb("pos_i", [NT, P], I32)
        pos_r = M.sb("pos_r", [NT, P])
        posc_i = M.sb("posc_i", [N_CMP, 1], I32)
        posp = M.sb("posp", [P, NT + 1])
        freq = M.sb("freq", [P, NF])
        ang = M.sb("ang", [P, NT + 1, NF])
        turns = M.sb("turns", [P, 2, NT + 1, NF])
        red = M.sb("red", [P, 2, NT + 1, NF])
        ones_f = M.sb("ones_f", [P, P])
        it_i = M.sb("it_i", [P, CAP], I32)
        pS = [M.ps(f"pc{i}", [P, 4, P]) for i in range(4)]
        ld_rows, ld_b, ld_pos, ld_posc = M.sem("c_rows"), M.sem("c_b"), M.sem("c_pos"), M.sem("c_posc")
        masks, fr, tr, own = M.sem("c_masks"), M.sem("c_freq"), M.sem("c_tr"), M.sem("c_own")
        zeroed, table, ev = M.sem("c_zero"), M.sem("c_table"), M.sem("c_ev")
        block = ctx.enter_context(nc.Block())

        @block.sync
        def _(sp):
            for r0, name, n in ((0, "attn_norm", 8), (8, "mla_q_norm", 2), (10, "mla_kv_norm", 1),
                                (11, "ffn_norm", 8)):
                sp.dma_start(rows[r0:r0 + n, :], a[name].rearrange("l (k p) -> (l k) p", p=P)).then_inc(ld_rows, 16)
            sp.dma_start(pos_i[:], a["positions"].rearrange("b (t p) -> (b t) p", p=P)).then_inc(ld_pos, 16)
            ends = a["positions"].rearrange("b (n s) -> (b n) s", s=CMP_STRIDE)[1:1 + N_CMP, CMP_STRIDE - 1:CMP_STRIDE]
            sp.dma_start(posc_i[:], ends, allow_slow_non_contiguous=True).then_inc(ld_posc, 16)
            sp.dma_start(rows_b1[:], a["moe_b1"].rearrange("l (g e) (m p) -> (l e m) g p", g=4, p=P)
                         ).then_inc(ld_b, 16)
            sp.dma_start(rows_b2[:], a["moe_b2"].rearrange("l (g e) (m p) -> (l e m) g p", g=2, p=P)
                         ).then_inc(ld_b, 16)
            sp.dma_start(C["rb"][:], a["router_b"].rearrange("l e -> e l"),
                         allow_slow_non_contiguous=True).then_inc(ld_b, 16)
            sp.wait_ge(ld_b, 48)

        @block.gpsimd
        def _(pool):
            pool.memset(C["ident"][:], 0.0).then_inc(zeroed, 1)
            pool.memset(C["ident_b"][:], 0.0).then_inc(zeroed, 1)
            pool.memset(C["causal"][:], 0.0).then_inc(zeroed, 1)
            pool.memset(C["far"][:], 0.0).then_inc(zeroed, 1)
            pool.memset(C["cmp_mask"][:], 0.0).then_inc(zeroed, 1)
            pool.memset(C["before"][:], 1.0).then_inc(zeroed, 1)
            pool.memset(C["ones_b"][:], 1.0).then_inc(zeroed, 1)
            pool.memset(C["late"][:], 1.0).then_inc(zeroed, 1)
            for j, f in enumerate(frequencies()):
                pool.memset(freq[:, j:j + 1], f).then_inc(fr, 1)
            pool.wait_ge(zeroed, 8)
            for t in ("ident", "ident_b"):
                pool.affine_select(out=C[t][:], in_=C[t][:], compare_op=ALU.not_equal, fill=1.0, base=0,
                                   pattern=[[-1, P]], channel_multiplier=1).then_inc(masks, 1)
            pool.affine_select(out=C["causal"][:], in_=C["causal"][:], compare_op=ALU.is_ge, fill=NEG, base=0,
                               pattern=[[-1, P]], channel_multiplier=1).then_inc(masks, 1)
            pool.affine_select(out=C["far"][:], in_=C["far"][:], compare_op=ALU.is_gt, fill=NEG, base=0,
                               pattern=[[1, P]], channel_multiplier=-1).then_inc(masks, 1)
            pool.affine_select(out=C["cmp_mask"][:], in_=C["cmp_mask"][:], compare_op=ALU.is_ge, fill=NEG,
                               base=-(CMP_BLOCK - 1), pattern=[[P, NT], [-CMP_STRIDE, 64]],
                               channel_multiplier=1).then_inc(masks, 1)
            pool.affine_select(out=C["before"][:], in_=C["before"][:], compare_op=ALU.is_gt, fill=0.0, base=0,
                               pattern=[[1, P]], channel_multiplier=-1).then_inc(masks, 1)
            pool.affine_select(out=C["late"][:], in_=C["late"][:], compare_op=ALU.is_ge, fill=0.0,
                               base=-(CMP_BLOCK - 1), pattern=[[0, 1]], channel_multiplier=1).then_inc(masks, 1)
            pool.iota(C["iota_i"][:], [[1, CAP]], base=0, channel_multiplier=0).then_inc(masks, 1)
            pool.iota(C["iota_p_i"][:], [[0, 1]], base=0, channel_multiplier=1).then_inc(masks, 1)
            pool.iota(C["iota_t_i"][:], [[1, NT]], base=0, channel_multiplier=0).then_inc(masks, 1)
            pool.wait_ge(masks, 10)

        @block.tensor
        def _(pe):
            pe.wait_ge(masks, 10)
            pe.wait_ge(ld_rows, 64)
            pe.wait_ge(own, 1)
            nc.tensor.transpose(pS[0][:, 0, 0:19], rows[:], C["ident"][0:19, 0:19])
            nc.tensor.transpose(pS[0][:, 1, 0:NT], pos_r[:], C["ident"][0:NT, 0:NT]).then_inc(tr, 1)
            pe.wait_ge(ld_b, 48)
            for g in range(4):
                nc.tensor.transpose(pS[1][:, g, :], rows_b1[:, g, :], C["ident"][:])
            for g in range(2):
                last = nc.tensor.transpose(pS[2][:, g, :], rows_b2[:, g, :], C["ident"][:])
            last.then_inc(tr, 1)

        @block.vector
        def _(dve):
            S = Steps(own)
            dve.wait_ge(ld_pos, 16)
            S.mark(nc.vector.tensor_copy(pos_r[:], pos_i[:]))
            S.mark(nc.vector.memset(posp[:], 0.0))
            dve.wait_ge(ld_posc, 16)
            S.wait(dve)
            S.mark(nc.vector.tensor_copy(posp[0:N_CMP, NT:NT + 1], posc_i[:]))
            dve.wait_ge(tr, 1)
            S.mark(nc.vector.tensor_copy(C["vec"][:], pS[0][:, 0, 0:19]))
            S.mark(nc.vector.tensor_copy(posp[:, 0:NT], pS[0][:, 1, 0:NT]))
            dve.wait_ge(masks, 10)
            S.mark(nc.vector.tensor_copy(C["iota"][:], C["iota_i"][:]))
            S.mark(nc.vector.tensor_copy(C["iota_p"][:], C["iota_p_i"][:]))
            S.mark(nc.vector.tensor_copy(C["iota_t"][:], C["iota_t_i"][:]))
            dve.wait_ge(tr, 2)
            S.mark(nc.vector.tensor_copy(C["b1"][:], pS[1][:]))
            S.mark(nc.vector.tensor_copy(C["b2"][:], pS[2][:, 0:2, :]))
            dve.wait_ge(fr, NF)
            S.wait(dve)
            S.mark(nc.vector.tensor_tensor(ang[:], posp[:].unsqueeze(2).to_broadcast([P, NT + 1, NF]),
                                           freq[:].unsqueeze(1).to_broadcast([P, NT + 1, NF]), ALU.mult))
            S.wait(dve)
            S.mark(nc.vector.tensor_scalar(turns[:, 0], ang[:], 1.0 / TWO_PI, None, ALU.mult))
            S.mark(nc.vector.tensor_scalar(turns[:, 1], ang[:], 1.0 / TWO_PI, 0.25, ALU.mult, ALU.add))
            for k in (ROUND, -ROUND):
                S.wait(dve)
                S.mark(nc.vector.tensor_scalar(turns[:], turns[:], k, None, ALU.add))
            S.wait(dve)
            for j in range(2):
                S.mark(nc.vector.scalar_tensor_tensor(red[:, j], turns[:, j], -C1, ang[:], ALU.mult, ALU.add))
            for k in (C2, C3):
                S.wait(dve)
                S.mark(nc.vector.scalar_tensor_tensor(red[:], turns[:], -k, red[:], ALU.mult, ALU.add))
            S.wait(dve)
            S.mark(nc.vector.tensor_scalar(red[:, 1], red[:, 1], float(np.pi / 2), None, ALU.add))
            S.wait(dve)
            S.mark(nc.vector.tensor_scalar(red[:], red[:], PI_IN, -PI_IN, ALU.min, ALU.max))
            S.wait(dve)
            dve.sem_inc(table, 1)

        @block.scalar
        def _(act):
            act.wait_ge(table, 1)
            nc.scalar.activation(C["trig"][:], red[:], ACT.Sin).then_inc(ev, 1)
            act.wait_ge(ev, 1)


def rope(nc, dve, S, x, heads, r0, half, sin, cos, t1, t2):
    p = x.shape[0]
    n = p, heads, 2, half
    xr = x[:, :, r0:r0 + 2 * half].rearrange("p h (two f) -> p h two f", two=2)
    c = cos.unsqueeze(1).unsqueeze(1).to_broadcast([*n])
    s = sin.unsqueeze(1).to_broadcast([p, heads, half])
    S.wait(dve)
    S.mark(nc.vector.tensor_tensor(t1, xr, c, ALU.mult))
    S.mark(nc.vector.tensor_tensor(t2[:, :, 0, :], xr[:, :, 1, :], s, ALU.mult))
    S.mark(nc.vector.tensor_tensor(t2[:, :, 1, :], xr[:, :, 0, :], s, ALU.mult))
    S.wait(dve)
    S.mark(nc.vector.tensor_tensor(xr[:, :, 0, :], t1[:, :, 0, :], t2[:, :, 0, :], ALU.subtract))
    S.mark(nc.vector.tensor_tensor(xr[:, :, 1, :], t1[:, :, 1, :], t2[:, :, 1, :], ALU.add))


PROJ = ((C_Q, C_QN), (C_KC, C_KW), (C_KW, IN_COLS), (C_QN, C_KC))
PROJ_ACT, PROJ_DVE = 12, 14


def project(nc, C, R, a):
    with ExitStack() as ctx:
        M = Mem(nc, ctx, C["sems"])
        w_in = M.sb("w_in", [P, KT, IN_COLS])
        x_t = M.sb("x_t", [P, D])
        xs = M.sb("xs", [P, D])
        junk = M.sb("junk", [P, D], BF16)
        uT = M.sb("uT", [P, KT, P])
        lat = M.sb("lat", [P, Q_RANK + KV_RANK])
        stage = M.sb("stage", [P, 12, DH])
        raw = M.sb("raw", [P, 4, 2, DH])
        ss, rec, rstd = M.sb("ss", [P, 1]), M.sb("rec", [P, 1]), M.sb("rstd", [P, 1])
        ss2, rec2, rstd2 = M.sb("ss2", [P, 2]), M.sb("rec2", [P, 2]), M.sb("rstd2", [P, 2])
        t1, t2 = M.sb("t1", [P, 12, 2, 8]), M.sb("t2", [P, 12, 2, 8])
        t3, t4 = M.sb("t3", [P, 1, 2, 16]), M.sb("t4", [P, 1, 2, 16])
        pe_t = M.sb("pe_t", [P, 1, ROPE])
        sig = M.sb("sig", [P, 1])
        pX = [M.ps(f"pX{i}", [P, 4, P]) for i in range(2)]
        pJ = [M.ps(f"pJ{i}", [P, 512]) for i in range(4)]
        pY = [M.ps(f"pY{i}", [P, 4, P]) for i in range(2)]
        w_loaded = [M.sem(f"p_w{i}") for i in range(4)]
        x_loaded, xs_ready, x_turned, u_ready = (M.sem("p_" + s) for s in ("x", "xs", "xt", "u"))
        sq_ready, rec_ready = M.sem("p_sq"), M.sem("p_rec")
        lsq_ready, lrec_ready = M.sem("p_lsq"), M.sem("p_lrec")
        product, copied, lat_ready, roped = (M.sem("p_" + s) for s in ("prod", "copied", "lat", "roped"))
        y_turned, y_dve, y_act = M.sem("p_yt"), M.sem("p_yd"), M.sem("p_ya")
        own_act, own_dve, passed = M.sem("p_oa"), M.sem("p_od"), M.sem("p_passed")
        zero, gates_ready = M.sem("p_zero"), M.sem("p_gates")
        block = ctx.enter_context(nc.Block())
        x_rows = a["x"].rearrange("b (t p) d -> (b t) p d", p=P)
        w_rows = a["w_in"].rearrange("l (k p) c -> (l p) k c", p=P)

        @block.sync
        def _(sp):
            sp.dma_start(x_t[:], x_rows[0]).then_inc(x_loaded, 16)
            for i in (0, 1, 2, 3):
                c0, c1 = PROJ[i]
                sp.dma_start(w_in[:, :, c0:c1], w_rows[:, :, c0:c1]).then_inc(w_loaded[i], 16)
            with sp.Fori(1, NT) as t:
                sp.wait_ge(xs_ready, t)
                sp.dma_start(x_t[:], x_rows[bass.ds(t, 1)].rearrange("a p d -> (a p) d")).then_inc(x_loaded, 16)

        @block.gpsimd
        def _(pool):
            pool.memset(R["nsaT"][64:96, :, :], 0.0).then_inc(zero, 1)
            pool.wait_ge(zero, 1)

        @block.tensor
        def _(pe):
            def turn_x(t, first=False):
                pe.wait_ge(xs_ready, t + 1)
                if not first:
                    pe.wait_ge(u_ready, 2 * t)
                for k in range(KT):
                    last = nc.tensor.transpose(pX[k // 4][:, k % 4, :], xs[:, k * P:(k + 1) * P], C["ident"][:])
                    if k % 4 == 3:
                        last.then_inc(x_turned, 1)

            def products(t, first=False):
                pe.wait_ge(u_ready, 2 * t + 2)
                for i, (c0, c1) in enumerate(PROJ):
                    if first:
                        pe.wait_ge(w_loaded[i], 16)
                    else:
                        pe.wait_ge(copied, 4 * t - 3 + i)
                    for k in range(KT):
                        last = nc.tensor.matmul(pJ[i][:, 0:c1 - c0], uT[:, k, :], w_in[:, k, c0:c1],
                                                start=(k == 0), stop=(k == KT - 1))
                    last.then_inc(product, 1)
                    if i == 0 and not first:
                        turn_y(t - 1)

            def turn_y(t):
                pe.wait_ge(lat_ready, t + 1)
                pe.wait_ge(y_dve, 3 * t + 1)
                for k in range(3):
                    last = nc.tensor.transpose(pY[0][:, k, :], lat[:, k * P:(k + 1) * P], C["ident"][:])
                last.then_inc(y_turned, 1)
                hold(pe, roped, t + 1, passed)
                for g in range(3):
                    if g == 1:
                        hold(pe, y_dve, 3 * t + 2, passed)
                    else:
                        hold(pe, y_act, 2 * t + 1 + g // 2, passed)
                    for j in range(4):
                        last = nc.tensor.transpose(pY[(g + 1) % 2][0:DH, j, :], stage[:, 4 * g + j, :], C["ident"][:])
                    last.then_inc(y_turned, 1)
                pe.wait_ge(y_dve, 3 * t + 3)
                for j in range(4):
                    last = nc.tensor.transpose(pY[0][:, j, :], raw[:, j].rearrange("p r d -> p (r d)"), C["ident"][:])
                last.then_inc(y_turned, 1)

            pe.sem_inc(y_dve, 1)
            pe.sem_inc(y_act, 1)
            turn_x(0, True)
            products(0, True)
            with pe.Fori(1, NT) as t:
                turn_x(t)
                products(t)
            turn_y(NT - 1)

        @block.scalar
        def _(act):
            def before(t, S, first=False):
                act.wait_ge(x_loaded, 16 * t + 16)
                nc.scalar.activation(junk[:], x_t[:], ACT.Square, accum_out=ss[:]).then_inc(sq_ready, 1)
                act.wait_ge(rec_ready, t + 1)
                S.mark(nc.scalar.activation(rstd[:], rec[:], ACT.Sqrt))
                if not first:
                    act.wait_ge(x_turned, 2 * t)
                S.wait(act)
                nc.scalar.activation(xs[:], x_t[:], ACT.Copy, scale=rstd[:]).then_inc(xs_ready, 1)

            def after(t, S, first=False):
                act.wait_ge(product, 4 * t + 1)
                if not first:
                    act.wait_ge(y_turned, 5 * t)
                S.mark(nc.scalar.activation(junk[:, 0:Q_RANK], pJ[0][:, 0:Q_RANK], ACT.Square,
                                            accum_out=ss2[:, 0:1]))
                S.wait(act)
                nc.scalar.activation(junk[:, 0:KV_RANK], pJ[0][:, C_KV:C_PE], ACT.Square,
                                     accum_out=ss2[:, 1:2]).then_inc(lsq_ready, 1)
                if not first:
                    act.wait_ge(roped, t)
                S.mark(nc.scalar.activation(pe_t[:, 0, :], pJ[0][:, C_PE:C_QN], ACT.Copy))
                act.wait_ge(lrec_ready, t + 1)
                S.mark(nc.scalar.activation(rstd2[:], rec2[:], ACT.Sqrt))
                S.wait(act)
                S.mark(nc.scalar.activation(lat[:, 0:Q_RANK], pJ[0][:, 0:Q_RANK], ACT.Copy, scale=rstd2[:, 0:1]))
                S.mark(nc.scalar.activation(lat[:, Q_RANK:], pJ[0][:, C_KV:C_PE], ACT.Copy, scale=rstd2[:, 1:2]))
                S.wait(act)
                act.sem_inc(lat_ready, 1)
                act.sem_inc(copied, 1)
                act.wait_ge(product, 4 * t + 2)
                S.mark(nc.scalar.activation(
                    raw[:], pJ[1][:, 0:2 * KVW].rearrange("p (j d) -> p j d", d=DH).unsqueeze(2)
                    .to_broadcast([P, 4, 2, DH]), ACT.Copy))
                S.mark(nc.scalar.activation(stage[:, 8:10, :].rearrange("p j d -> p (j d)"),
                                            pJ[1][:, 2 * KVW:3 * KVW], ACT.Copy))
                S.mark(nc.scalar.activation(R["v_s"][:, bass.ds(t, 1), :].rearrange("p a c -> p (a c)"),
                                            pJ[1][:, 3 * KVW:4 * KVW], ACT.Copy))
                S.wait(act)
                act.sem_inc(copied, 1)
                act.wait_ge(product, 4 * t + 3)
                S.mark(nc.scalar.activation(stage[:, 10:12, :].rearrange("p j d -> p (j d)"),
                                            pJ[2][:, 0:KVW], ACT.Copy))
                S.mark(nc.scalar.activation(R["v_w"][:, bass.ds(t, 1), :].rearrange("p a c -> p (a c)"),
                                            pJ[2][:, KVW:2 * KVW], ACT.Copy))
                S.mark(nc.scalar.activation(R["gates"][:, bass.ds(t, 1), :].rearrange("p a c -> p (a c)"),
                                            pJ[2][:, 2 * KVW:2 * KVW + 3 * H_NSA], ACT.Copy))
                S.wait(act)
                act.sem_inc(copied, 1)
                act.wait_ge(product, 4 * t + 4)
                nc.scalar.activation(stage[:, 0:8, :].rearrange("p j d -> p (j d)"), pJ[3][:], ACT.Copy
                                     ).then_inc(copied, 1)

            def from_y(t):
                for n, g in enumerate((0, 2)):
                    act.wait_ge(y_turned, 5 * t + 2 + 2 * n)
                    nc.scalar.activation(R["nsaT"][0:DH, 4 * g:4 * g + 4, bass.ds(t * P, P)],
                                         pY[1][0:DH], ACT.Copy).then_inc(y_act, 1)

            S = Steps(own_act)
            before(0, S, True)
            before(1, S)
            after(0, S, True)
            from_y(0)
            n0 = S.n
            with act.Fori(1, NT - 1) as t:
                S = Steps(own_act, (t - 1) * PROJ_ACT + n0)
                before(t + 1, S)
                after(t, S)
                from_y(t)
            assert S.n == PROJ_ACT, S.n
            S = Steps(own_act, (NT - 2) * PROJ_ACT + n0)
            after(NT - 1, S)
            from_y(NT - 1)
            S.wait(act)
            S.mark(nc.scalar.activation(R["gates"][:], R["gates"][:], ACT.Sigmoid))
            S.wait(act)
            nc.scalar.activation(R["gates"][:, 0, 0:3 * H_NSA:3], R["gates"][:, 0, 0:3 * H_NSA:3], ACT.Copy,
                                 scale=C["late"][:]).then_inc(gates_ready, 1)
            act.wait_ge(gates_ready, 1)

        @block.vector
        def _(dve):
            def reciprocal(S, out, x, n):
                S.mark(nc.vector.tensor_scalar(out, x, 1.0 / n, EPS, ALU.mult, ALU.add))
                S.wait(dve)
                return nc.vector.reciprocal(out, out)

            def before(t, S):
                dve.wait_ge(sq_ready, t + 1)
                reciprocal(S, rec[:], ss[:], D).then_inc(rec_ready, 1)

            def turned(t, first=False):
                for i in range(2):
                    dve.wait_ge(x_turned, 2 * t + 1 + i)
                    if i == 0 and not first:
                        dve.wait_ge(product, 4 * t)
                    nc.vector.tensor_tensor(uT[:, 4 * i:4 * i + 4, :], pX[i][:],
                                            C["vec"][:, 4 * i:4 * i + 4].unsqueeze(2).to_broadcast([P, 4, P]),
                                            ALU.mult).then_inc(u_ready, 1)

            def latents(t, S):
                dve.wait_ge(lsq_ready, t + 1)
                for i, n in enumerate((Q_RANK, KV_RANK)):
                    S.mark(nc.vector.tensor_scalar(rec2[:, i:i + 1], ss2[:, i:i + 1], 1.0 / n, EPS,
                                                   ALU.mult, ALU.add))
                S.wait(dve)
                nc.vector.reciprocal(rec2[:], rec2[:]).then_inc(lrec_ready, 1)
                dve.wait_ge(lat_ready, t + 1)
                sin, cos = (C["trig"][:, j, bass.ds(t, 1), :].rearrange("p a f -> p (a f)") for j in (0, 1))
                rope(nc, dve, S, pe_t[:], 1, 0, ROPE // 2, sin[:, 0:16], cos[:, 0:16], t3[:], t4[:])
                S.wait(dve)
                S.mark(nc.vector.tensor_copy(R["k_pe"][:, bass.ds(t, 1), :], pe_t[:]))

            def heads(t, S):
                sin, cos = (C["trig"][:, j, bass.ds(t, 1), :].rearrange("p a f -> p (a f)") for j in (0, 1))
                dve.wait_ge(copied, 4 * t + 4)
                rope(nc, dve, S, stage[:], 12, 0, ROPE_N // 2, sin[:, 16:24], cos[:, 16:24], t1[:], t2[:])
                S.wait(dve)
                dve.sem_inc(roped, 1)

            def from_y(t, S):
                dve.wait_ge(y_turned, 5 * t + 1)
                nc.vector.tensor_tensor(R["latT"][:, :, bass.ds(t * P, P)], pY[0][:, 0:3, :],
                                        C["vec"][:, 8:11].unsqueeze(2).to_broadcast([P, 3, P]),
                                        ALU.mult).then_inc(y_dve, 1)
                dve.wait_ge(y_turned, 5 * t + 3)
                nc.vector.tensor_copy(R["nsaT"][0:DH, 4:8, bass.ds(t * P, P)], pY[0][0:DH]).then_inc(y_dve, 1)
                dve.wait_ge(y_turned, 5 * t + 5)
                nc.vector.tensor_copy(R["rawT"][:, :, bass.ds(t * P, P)], pY[0][:]).then_inc(y_dve, 1)

            S = Steps(own_dve)
            before(0, S)
            turned(0, True)
            before(1, S)
            latents(0, S)
            turned(1)
            heads(0, S)
            from_y(0, S)
            n0 = S.n
            with dve.Fori(1, NT - 1) as t:
                S = Steps(own_dve, (t - 1) * PROJ_DVE + n0)
                before(t + 1, S)
                latents(t, S)
                turned(t + 1)
                heads(t, S)
                from_y(t, S)
            assert S.n == PROJ_DVE, S.n
            S = Steps(own_dve, (NT - 2) * PROJ_DVE + n0)
            latents(NT - 1, S)
            heads(NT - 1, S)
            from_y(NT - 1, S)


def compress(nc, C, R, a):
    LP = CMP_BLOCK // 2
    with ExitStack() as ctx:
        M = Mem(nc, ctx, C["sems"])
        w1 = M.sb("cw1", [P, 2, LP, CMP_HID])
        w2 = M.sb("cw2", [P, 2, DH])
        pos = M.sb("cpos", [2 * LP, 2 * DH])
        posT = M.sb("cposT", [P, 2, LP])
        blocks = M.sb("cblocks", [P, 2, LP, G_NSA, N_CMP])
        sg, hid = M.sb("csg", [P, 2, G_NSA * N_CMP]), M.sb("chid", [P, 2, G_NSA * N_CMP])
        kc = M.sb("ckc", [64, G_NSA, DH])
        t1, t2 = M.sb("ct1", [64, G_NSA, 2, 8]), M.sb("ct2", [64, G_NSA, 2, 8])
        pH = [M.ps(f"cpH{i}", [P, 512]) for i in range(2)]
        pO, pT = M.ps("cpO", [64, 4, DH]), M.ps("cpT", [P, 4, P])
        ld, ldp, turned, posT_ready = M.sem("cc_ld"), M.sem("cc_ldp"), M.sem("cc_turned"), M.sem("cc_posT")
        built, hid_ready, sg_ready, silu = M.sem("cc_built"), M.sem("cc_hid"), M.sem("cc_sg"), M.sem("cc_silu")
        out_ready, own, kc_ready, kc_turned = M.sem("cc_out"), M.sem("cc_own"), M.sem("cc_kc"), M.sem("cc_kct")
        zero, zero2 = M.sem("cc_zero"), M.sem("cc_zero2")
        block = ctx.enter_context(nc.Block())

        @block.sync
        def _(sp):
            sp.dma_start(pos[:], a["nsa_cmp_pos"].rearrange("l c (lp two) d -> (l c lp) (two d)", two=2)
                         ).then_inc(ldp, 16)
            for c in range(2):
                sp.dma_start(w1[:, c], a["nsa_cmp_w1"][0, c].rearrange("(lp two) d h -> (two d) lp h", two=2)
                             ).then_inc(ld, 16)
            sp.dma_start(w2[:], a["nsa_cmp_w2"].rearrange("l c h d -> (l h) c d")).then_inc(ld, 16)
            sp.wait_ge(ld, 48)

        def windows(c, g):
            half = []
            for two in range(2):
                src = R["rawT"][64 * two:64 * two + 64, 2 * c + g, :]
                v = bass.AP(tensor=src.tensor, offset=src.offset + two,
                            ap=[list(src.ap[0]), [2, LP], [CMP_STRIDE, N_CMP]])
                half.append(v)
            return half

        def build(eng, c):
            for g in range(G_NSA):
                for two, v in enumerate(windows(c, g)):
                    h = slice(64 * two, 64 * two + 64)
                    eng.tensor_tensor(blocks[h, c, :, g, :], v,
                                      posT[h, c, :].unsqueeze(2).to_broadcast([64, LP, N_CMP]),
                                      ALU.add).then_inc(built, 1)

        @block.gpsimd
        def _(pool):
            for t in (kc, R["kcT"], R["v_c"]):
                pool.memset(t[:], 0.0).then_inc(zero, 1)
            pool.wait_ge(zero, 3)
            pool.sem_inc(zero2, 1)

        @block.vector
        def _(dve):
            S = Steps(own)
            dve.wait_ge(turned, 1)
            nc.vector.tensor_copy(posT[:], pT[:, 0, 0:2 * LP].rearrange("p (c l) -> p c l", c=2)
                                  ).then_inc(posT_ready, 1)
            dve.wait_ge(posT_ready, 1)
            build(nc.vector, 0)
            build(nc.vector, 1)
            for c in range(2):
                dve.wait_ge(sg_ready, c + 1)
                nc.vector.tensor_tensor(hid[:, c, :], pH[c][:, 0:G_NSA * N_CMP], sg[:, c, :], ALU.mult
                                        ).then_inc(silu, 1)
            dve.wait_ge(zero2, 1)
            dve.wait_ge(out_ready, 1)
            S.mark(nc.vector.tensor_copy(kc[0:N_CMP], pO[0:N_CMP, 0:2, :]))
            rope(nc, dve, S, kc[0:N_CMP], G_NSA, 0, ROPE_N // 2, C["trig"][0:N_CMP, 0, NT, 16:24],
                 C["trig"][0:N_CMP, 1, NT, 16:24], t1[0:N_CMP], t2[0:N_CMP])
            S.wait(dve)
            nc.vector.tensor_copy(R["v_c"][0:N_CMP], pO[0:N_CMP, 2:4, :]).then_inc(kc_ready, 1)
            dve.wait_ge(kc_turned, 1)
            nc.vector.tensor_copy(R["kcT"][0:DH], pT[0:DH, 1:3, 0:64]).then_inc(kc_ready, 1)
            dve.wait_ge(kc_ready, 2)

        @block.scalar
        def _(act):
            for c in range(2):
                act.wait_ge(hid_ready, c + 1)
                nc.scalar.activation(sg[:, c, :], pH[c][:, 0:G_NSA * N_CMP], ACT.Sigmoid).then_inc(sg_ready, 1)

        @block.tensor
        def _(pe):
            pe.wait_ge(ldp, 16)
            nc.tensor.transpose(pT[:, 0, 0:2 * LP], pos[:], C["ident"][0:2 * LP, 0:2 * LP]).then_inc(turned, 1)
            pe.wait_ge(ld, 48)
            for c in range(2):
                pe.wait_ge(built, 4 * c + 4)
                for lp in range(LP):
                    last = nc.tensor.matmul(pH[c][:, 0:G_NSA * N_CMP], w1[:, c, lp, :],
                                            blocks[:, c, lp].rearrange("p g n -> p (g n)"),
                                            start=(lp == 0), stop=(lp == LP - 1))
                last.then_inc(hid_ready, 1)
            pe.wait_ge(silu, 2)
            for c in range(2):
                for g in range(G_NSA):
                    last = nc.tensor.matmul(pO[0:N_CMP, 2 * c + g, :], hid[:, c, g * N_CMP:(g + 1) * N_CMP],
                                            w2[:, c, :], start=True, stop=True)
            last.then_inc(out_ready, 1)
            pe.wait_ge(kc_ready, 1)
            for g in range(G_NSA):
                last = nc.tensor.transpose(pT[0:DH, 1 + g, 0:64], kc[:, g, :], C["ident"][0:64, 0:64])
            last.then_inc(kc_turned, 1)


QG = 4
LAG = 3


class Unit:

    def __init__(self, kind, pair, qg, head, i):
        self.kind, self.pair, self.qg, self.head, self.i = kind, pair, qg, head, i
        if kind == "win":
            self.k0 = max(0, i - WT)
            w = (i + 1 - self.k0) * P
            self.spans = [(0, w, 0), ((WT + 1) * P, (WT + 1) * P + 64, 1)]
            pieces = [(P * j, P, self.k0 + j) for j in range(i + 1 - self.k0)] + [((WT + 1) * P, 64, None)]
        else:
            self.k0 = 0
            w = (i + 1) * P
            self.spans = [(0, w, 0)]
            pieces = [(P * j, P, j) for j in range(i + 1)]
        self.width = w
        self.banks = [pieces[j:j + 4] for j in range(0, len(pieces), 4)]


def plan(kinds, pairs):
    units, first, groups = [], [], []
    for pair in range(pairs):
        for qg in range(NT // QG):
            for kind in kinds:
                for i in range(QG * qg, QG * qg + QG):
                    for head in range(2):
                        first.append(sum(len(u.banks) for u in units))
                        units.append(Unit(kind, pair, qg, head, i))
                groups.append((len(units) - 1, kind, pair, qg))
    return units, first, groups


def value_tiles(kind, qg):
    q0, q1 = QG * qg, QG * qg + QG
    if kind == "win":
        return [(k, max(k, q0), min(k + WT + 1, q1)) for k in range(max(0, q0 - WT), q1)]
    return [(k, max(k, q0), q1) for k in range(q1)]


class Attention:

    def __init__(self, nc, M, C, R, name, kinds, pairs, prep, gated):
        self.nc, self.C, self.R, self.kinds, self.gated = nc, C, R, kinds, gated
        self.units, self.first, self.groups = plan(kinds, pairs)
        self.OUTS = 2 * pairs
        self.U, self.NG = len(self.units), len(self.groups)
        self.prep = prep
        banks = prep + sum(len(u.banks) for u in self.units)
        assert banks % 2 == 0 and self.U % 4 == 0 and prep % 2 == 0
        self.half = banks // 2
        self.probs = M.sb(name + "probs", [P, 4, SEQ])
        self.probsT = M.sb(name + "probsT", [P, 2, NT, QG * P])
        self.negmax = M.sb(name + "negmax", [P, 4, 2])
        self.sums = M.sb(name + "sums", [P, 4, 2])
        self.weight = M.sb(name + "weight", [P, 4, 2])
        self.pS = [M.ps(f"{name}pS{i}", [P, SEQ]) for i in range(2)]
        self.pT = [M.ps(f"{name}pT{i}", [P, 4, P]) for i in range(2)]
        self.pO = [M.ps(f"{name}pO{i}", [P, QG * P]) for i in range(2)]
        s = lambda x: M.sem(name + x)
        self.staged = s("staged")
        self.scored, self.maxed, self.exped, self.inverted = s("scored"), s("maxed"), s("exped"), s("inv")
        self.scaled = s("scaled")
        self.bank_turned = [s("bt0"), s("bt1")]
        self.bank_read = [s("br0"), s("br1")]
        self.valued, self.out_read = s("valued"), s("outd")
        self.passed = s("passed")

    FREE_BANK, FREE_SCORES, FREE_OUT, FREE_VALUED, NO_BANK = 1, 2, 2, 1, 1

    def start(self, pe):
        for b in range(2):
            pe.sem_inc(self.bank_read[b], self.FREE_BANK)
            pe.sem_inc(self.bank_turned[b], self.NO_BANK)
        pe.sem_inc(self.exped, self.FREE_SCORES)
        pe.sem_inc(self.out_read, self.FREE_OUT)
        pe.sem_inc(self.valued, self.FREE_VALUED)

    def wait_bank(self, pe, it, seq):
        pe.wait_ge(self.bank_read[seq % 2], it * self.half + seq // 2 + self.FREE_BANK)

    def wait_turned(self, eng, it, seq):
        eng.wait_ge(self.bank_turned[seq % 2], it * self.half + seq // 2 + 1 + self.NO_BANK)

    def scores(self, pe, it, n):
        nc, C, u, pS = self.nc, self.C, self.units[n], self.pS[n % 2]
        pe.wait_ge(self.exped, it * self.U + n + 1)
        q = self.queries(u)
        for c0 in range(0, u.width, 512):
            c1 = min(c0 + 512, u.width)
            diag = u.width - P >= c0 and u.width - P < c1
            far = u.kind == "win" and u.i >= WT and c0 == 0
            nc.tensor.matmul(pS[:, c0:c1], q, self.keys(u, u.k0 * P + c0, u.k0 * P + c1), start=True,
                             stop=not (diag or far))
            if far:
                nc.tensor.matmul(pS[:, 0:P], C["ident_b"][:], C["far"][:], start=False, stop=not diag)
            if diag:
                last = nc.tensor.matmul(pS[:, u.width - P:u.width], C["ident_b"][:], C["causal"][:],
                                        start=False, stop=True)
        if u.kind == "win":
            c0 = (WT + 1) * P
            nc.tensor.matmul(pS[:, c0:c0 + 64], q, self.keys(u, None, None), start=True, stop=False)
            last = nc.tensor.matmul(pS[:, c0:c0 + 64], C["ident_b"][:], C["cmp_mask"][:, u.i, :],
                                    start=False, stop=True)
        last.then_inc(self.scored, 1)

    def turn(self, pe, it, n):
        nc, u = self.nc, self.units[n]
        pe.wait_ge(self.scaled, it * self.U + n + 1)
        for j, pieces in enumerate(u.banks):
            seq = self.prep + self.first[n] + j
            self.wait_bank(pe, it, seq)
            if pieces[0][1] != P:
                pe.sem_inc(self.passed, 1)
            for k, (col, rows, _) in enumerate(pieces):
                last = nc.tensor.transpose(self.pT[seq % 2][0:rows, k, :], self.probs[:, n % 4, col:col + rows],
                                           self.C["ident"][:])
            last.then_inc(self.bank_turned[seq % 2], 1)

    def values(self, pe, it, g):
        nc, (n, kind, pair, qg) = self.nc, self.groups[g]
        opening, closing = kind == self.kinds[0], kind == self.kinds[-1]
        seqs = self.prep + self.first[n] + len(self.units[n].banks)
        for b in range(2):
            pe.wait_ge(self.bank_read[b], it * self.half + (seqs + 1 - b) // 2 + self.FREE_BANK)
        if opening:
            pe.wait_ge(self.out_read, self.OUTS * it + 2 * pair + qg - 1 + self.FREE_OUT)
        tiles = value_tiles(kind, qg)
        for j, (k, i0, i1) in enumerate(tiles):
            c0, c1 = (i0 - QG * qg) * P, (i1 - QG * qg) * P
            end = closing and kind != "win" and j == len(tiles) - 1
            for h in range(2):
                last = nc.tensor.matmul(self.pO[qg][64 * h:64 * h + 64, c0:c1], self.value(kind, k, h),
                                        self.probsT[:, h, k, c0:c1], start=opening and j == 0, stop=end)
        if kind == "win":
            for h in range(2):
                last = nc.tensor.matmul(self.pO[qg][64 * h:64 * h + 64, :], self.value("cmp", 0, h),
                                        self.cmpT[:, h, :], start=False, stop=True)
        last.then_inc(self.valued, 1)

    def tensor(self, pe, it):
        for s in range(self.U + LAG + 1):
            if LAG <= s < self.U + LAG:
                self.turn(pe, it, s - LAG)
            if s < self.U:
                self.scores(pe, it, s)
            for g, (n, *_) in enumerate(self.groups):
                if n == s - LAG - 1:
                    self.values(pe, it, g)

    def read_banks(self, eng, copy, it, n, parity):
        u = self.units[n]
        group = next(g for g, (m, *_) in enumerate(self.groups) if n <= m)
        for j, pieces in enumerate(u.banks):
            seq = self.prep + self.first[n] + j
            if seq % 2 != parity:
                continue
            eng.wait_ge(self.valued, it * self.NG + group + self.FREE_VALUED)
            self.wait_turned(eng, it, seq)
            c = (u.i % QG) * P
            full = [x for x in pieces if x[1] == P]
            k0 = full[0][2] if full else 0
            if full:
                last = copy(self.probsT[:, u.head, k0:k0 + len(full), c:c + P], self.pT[seq % 2][:, 0:len(full), :])
            if len(full) < len(pieces):
                last = copy(self.cmpT[0:64, u.head, c:c + P], self.pT[seq % 2][0:64, len(full), :])
            last.then_inc(self.bank_read[seq % 2], 1)

    def scalar(self, act, it, out_tile):
        nc = self.nc
        for s in range(self.U + LAG + 2):
            if LAG <= s < self.U + LAG:
                self.read_banks(act, nc.scalar.copy, it, s - LAG, 0)
            for g, (n, kind, pair, qg) in enumerate(self.groups):
                if n == s - LAG - 2 and kind == self.kinds[-1]:
                    act.wait_ge(self.valued, it * self.NG + g + 1 + self.FREE_VALUED)
                    nc.scalar.copy(out_tile(pair)[:, :, qg * QG * P:(qg + 1) * QG * P].rearrange("p a q -> p (a q)"),
                                   self.pO[qg][:]).then_inc(self.out_read, 1)
            if s < self.U:
                act.wait_ge(self.maxed, it * self.U + s + 1)
                if s >= 4:
                    self.wait_turned(act, it, self.prep + self.first[s - 4] + len(self.units[s - 4].banks) - 1)
                else:
                    for b in range(2):
                        act.wait_ge(self.bank_turned[b], it * self.half + self.NO_BANK)
                for c0, c1, k in self.units[s].spans:
                    last = nc.scalar.activation(self.probs[:, s % 4, c0:c1], self.pS[s % 2][:, c0:c1], ACT.Exp,
                                                bias=self.negmax[:, s % 4, k:k + 1],
                                                accum_out=self.sums[:, s % 4, k:k + 1])
                last.then_inc(self.exped, 1)

    def vector(self, dve, it):
        nc = self.nc
        for s in range(self.U + LAG):
            if s >= LAG:
                self.read_banks(dve, nc.vector.tensor_copy, it, s - LAG, 1)
            if s < self.U:
                dve.wait_ge(self.scored, it * self.U + s + 1)
                for c0, c1, k in self.units[s].spans:
                    last = nc.vector.tensor_reduce(self.negmax[:, s % 4, k:k + 1], self.pS[s % 2][:, c0:c1],
                                                   AX_X, ALU.max, negate=True)
                last.then_inc(self.maxed, 1)
            if 1 <= s <= self.U:
                n = s - 1
                u, w = self.units[n], self.weight[:, n % 4, 0:len(self.units[n].spans)]
                dve.wait_ge(self.exped, it * self.U + n + 1 + self.FREE_SCORES)
                nc.vector.reciprocal(w, self.sums[:, n % 4, 0:len(u.spans)]).then_inc(self.inverted, 1)
                if self.gated:
                    dve.wait_ge(self.inverted, 2 * (it * self.U + n) + 1)
                    gate = [1] if u.kind == "sel" else [2, 0]
                    for k, br in enumerate(gate):
                        last = nc.vector.tensor_tensor(w[:, k:k + 1], w[:, k:k + 1],
                                                       self.gate(u, br), ALU.mult)
                    last.then_inc(self.inverted, 1)
                    dve.wait_ge(self.inverted, 2 * (it * self.U + n) + 2)
                else:
                    dve.wait_ge(self.inverted, it * self.U + n + 1)
                for c0, c1, k in u.spans:
                    last = nc.vector.tensor_scalar(self.probs[:, n % 4, c0:c1], self.probs[:, n % 4, c0:c1],
                                                   w[:, k:k + 1], None, ALU.mult)
                last.then_inc(self.scaled, 1)


def mla(nc, C, R, a):
    scale = QK_MLA ** -0.5
    ROPES = 5
    with ExitStack() as ctx:
        M = Mem(nc, ctx, C["sems"])
        A = Attention(nc, M, C, R, "m_", ("mla",), 1, NT, False)
        wq = M.sb("m_wq", [P, Q_RANK // P, 2 * QK_MLA])
        wkv = M.sb("m_wkv", [P, 2 * (NOPE + V_DIM)])
        stage = M.sb("m_stage", [P, 2, 4, QK_MLA])
        qkT = M.sb("m_qkT", [QK_MLA, 4, SEQ])
        v = M.sb("m_v", [P, NT, 2, V_DIM])
        t1, t2 = M.sb("m_t1", [P, 2, 2, 16]), M.sb("m_t2", [P, 2, 2, 16])
        loaded, product, copied, roped, own = (M.sem("m_" + s) for s in ("ld", "prod", "copied", "roped", "own"))
        A.queries = lambda u: qkT[:, u.head, u.i * P:(u.i + 1) * P]
        A.keys = lambda u, c0, c1: qkT[:, 2 + u.head, c0:c1]
        A.value = lambda kind, k, h: v[:, k, h, :]
        PAIRS = H_MLA // 2
        block = ctx.enter_context(nc.Block())

        @block.sync
        def _(sp):
            def load(it):
                sp.dma_start(wq[:], a["mla_w_q_up"].rearrange("l (k p) (a c) -> (l p) k a c", p=P, a=PAIRS)
                             [:, :, bass.ds(it, 1), :].rearrange("p k a c -> p k (a c)")).then_inc(loaded, 16)
                sp.dma_start(wkv[:], a["mla_w_kv_up"].rearrange("l p (a c) -> (l p) a c", a=PAIRS)
                             [:, bass.ds(it, 1), :].rearrange("p a c -> p (a c)")).then_inc(loaded, 16)
            load(0)
            with sp.Fori(1, PAIRS) as it:
                sp.wait_ge(product, NT * it)
                load(it)

        @block.tensor
        def _(pe):
            A.start(pe)
            pe.sem_inc(copied, 1)
            with pe.Fori(0, PAIRS) as it:
                pe.wait_ge(loaded, 32 * it + 32)
                pe.wait_ge(A.exped, it * A.U + A.FREE_SCORES)
                for j in range(NT + 1):
                    if j < NT:
                        b = A.pS[j % 2]
                        pe.wait_ge(copied, NT * it + max(j - 1, 0) + 1)
                        for k in range(Q_RANK // P):
                            nc.tensor.matmul(b[:, 0:2 * QK_MLA], R["latT"][:, k, j * P:(j + 1) * P], wq[:, k, :],
                                             start=(k == 0), stop=(k == Q_RANK // P - 1))
                        nc.tensor.matmul(b[:, 512:768], R["latT"][:, 2, j * P:(j + 1) * P], wkv[:],
                                         start=True, stop=True).then_inc(product, 1)
                    if j >= 1:
                        pe.wait_ge(roped, NT * it + j)
                        A.wait_bank(pe, it, j - 1)
                        for k in range(4):
                            last = nc.tensor.transpose(A.pT[(j - 1) % 2][0:QK_MLA, k, :], stage[:, (j - 1) % 2, k, :],
                                                       C["ident"][:])
                        last.then_inc(A.bank_turned[(j - 1) % 2], 1)
                for b in range(2):
                    pe.wait_ge(A.bank_read[b], it * A.half + NT // 2 + A.FREE_BANK)
                A.tensor(pe, it)

        @block.scalar
        def _(act):
            with act.Fori(0, PAIRS) as it:
                for j in range(NT):
                    b = A.pS[j % 2]
                    act.wait_ge(product, NT * it + j + 1)
                    if j >= 2:
                        A.wait_turned(act, it, j - 2)
                    nc.scalar.activation(stage[:, j % 2, 0:2, :].rearrange("p h c -> p (h c)"), b[:, 0:2 * QK_MLA],
                                         ACT.Copy, scale=scale).then_inc(copied, 1)
                    if j % 2 == 0 and j >= 2:
                        A.wait_turned(act, it, j - 2)
                        nc.scalar.copy(qkT[:, :, (j - 2) * P:(j - 1) * P], A.pT[0][0:QK_MLA]).then_inc(A.bank_read[0], 1)
                A.wait_turned(act, it, NT - 2)
                nc.scalar.copy(qkT[:, :, (NT - 2) * P:(NT - 1) * P], A.pT[0][0:QK_MLA]).then_inc(A.bank_read[0], 1)
                A.scalar(act, it, lambda pair: R["mixT"][:, bass.ds(it, 1), :])

        @block.vector
        def _(dve):
            with dve.Fori(0, PAIRS) as it:
                S = Steps(own, it * ROPES * NT)
                for j in range(NT):
                    b = A.pS[j % 2]
                    dve.wait_ge(product, NT * it + j + 1)
                    if j >= 2:
                        A.wait_turned(dve, it, j - 2)
                    nc.vector.tensor_copy(stage[:, j % 2, 2:4, 0:NOPE],
                                          b[:, 512:768].rearrange("p (h c) -> p h c", h=2)[:, :, 0:NOPE])
                    nc.vector.tensor_copy(v[:, j], b[:, 512:768].rearrange("p (h c) -> p h c", h=2)[:, :, NOPE:])
                    nc.vector.tensor_copy(stage[:, j % 2, 2:4, NOPE:],
                                          R["k_pe"][:, j:j + 1, :].to_broadcast([P, 2, ROPE]))
                    dve.wait_ge(copied, NT * it + j + 2)
                    rope(nc, dve, S, stage[:, j % 2, 0:2, :], 2, NOPE, ROPE // 2, C["trig"][:, 0, j, 0:16],
                         C["trig"][:, 1, j, 0:16], t1[:], t2[:])
                    S.wait(dve)
                    dve.sem_inc(roped, 1)
                    if j % 2 == 1 and j >= 3:
                        A.wait_turned(dve, it, j - 2)
                        nc.vector.tensor_copy(qkT[:, :, (j - 2) * P:(j - 1) * P], A.pT[1][0:QK_MLA]
                                              ).then_inc(A.bank_read[1], 1)
                assert S.n == ROPES * NT
                A.wait_turned(dve, it, NT - 1)
                nc.vector.tensor_copy(qkT[:, :, (NT - 1) * P:], A.pT[1][0:QK_MLA]).then_inc(A.bank_read[1], 1)
                A.vector(dve, it)


def nsa(nc, C, R):
    PER_G = H_NSA // G_NSA // 2
    with ExitStack() as ctx:
        M = Mem(nc, ctx, C["sems"])
        A = Attention(nc, M, C, R, "n_", ("sel", "win"), PER_G, 0, True)
        A.cmpT = M.sb("n_cmpT", [P, 2, QG * P])
        q = M.sb("n_q", [96, 2 * PER_G, SEQ])
        k = M.sb("n_k", [96, 2, SEQ])
        kc = M.sb("n_kc", [96, 64])
        v = M.sb("n_v", [P, 2, NT, DH])
        vc = M.sb("n_vc", [P, DH])
        gp = M.sb("n_g", [P, NT, 6 * PER_G])
        q_staged, k_staged, v_staged, g_staged, zero, copied, passed = (
            M.sem("n_" + s) for s in ("q", "k", "v", "g", "z", "copied", "n_passed"))
        A.queries = lambda u: q[:, 2 * u.pair + u.head, u.i * P:(u.i + 1) * P]
        A.keys = lambda u, c0, c1: kc[:] if c0 is None else k[:, 0 if u.kind == "sel" else 1, c0:c1]
        A.value = lambda kind, t, h: vc[:] if kind == "cmp" else v[:, 0 if kind == "sel" else 1, t, :]
        A.gate = lambda u, br: gp[:, u.i, 6 * u.pair + 3 * u.head + br:6 * u.pair + 3 * u.head + br + 1]
        block = ctx.enter_context(nc.Block())

        @block.gpsimd
        def _(pool):
            pool.memset(A.cmpT[64:128], 0.0).then_inc(zero, 1)
            pool.wait_ge(zero, 1)
            pool.memset(vc[64:128], 0.0).then_inc(zero, 1)
            pool.wait_ge(zero, 2)
            with pool.Fori(0, G_NSA) as g:
                pool.wait_ge(A.valued, g * A.NG + A.FREE_VALUED)
                pool.tensor_copy(v[:, 0], R["v_s"][:, :, bass.ds(g * DH, DH)]).then_inc(copied, 1)
                pool.wait_ge(copied, 2 * g + 1)
                pool.tensor_copy(v[:, 1], R["v_w"][:, :, bass.ds(g * DH, DH)]).then_inc(copied, 1)
                pool.wait_ge(copied, 2 * g + 2)
                pool.tensor_copy(vc[0:64].rearrange("p (a d) -> p a d", a=1), R["v_c"][:, bass.ds(g, 1), :]
                                 ).then_inc(v_staged, 1)

        @block.tensor
        def _(pe):
            A.start(pe)
            pe.wait_ge(zero, 2)
            with pe.Fori(0, G_NSA) as g:
                pe.wait_ge(k_staged, g + 1)
                pe.wait_ge(v_staged, g + 1)
                hold(pe, q_staged, g + 1, passed)
                A.tensor(pe, g)

        @block.scalar
        def _(act):
            with act.Fori(0, G_NSA) as g:
                act.wait_ge(A.valued, g * A.NG + A.FREE_VALUED)
                for h in range(2 * PER_G):
                    last = nc.scalar.activation(q[:, h:h + 1, :], R["nsaT"][:, bass.ds(2 * PER_G * g + h, 1), :],
                                                ACT.Copy, scale=DH ** -0.5)
                last.then_inc(q_staged, 1)
                A.scalar(act, g, lambda pair: R["mixT"][:, bass.ds(PER_G * g + pair + H_MLA // 2, 1), :])

        @block.vector
        def _(dve):
            with dve.Fori(0, G_NSA) as g:
                dve.wait_ge(A.valued, g * A.NG + A.FREE_VALUED)
                nc.vector.tensor_copy(k[:, 0:1, :], R["nsaT"][:, bass.ds(g + 8, 1), :])
                nc.vector.tensor_copy(k[:, 1:2, :], R["nsaT"][:, bass.ds(g + 10, 1), :])
                nc.vector.tensor_copy(kc[:].rearrange("p (a n) -> p a n", a=1), R["kcT"][:, bass.ds(g, 1), :]
                                      ).then_inc(k_staged, 1)
                nc.vector.tensor_copy(gp[:], R["gates"][:, :, bass.ds(g * (6 * PER_G), 6 * PER_G)]).then_inc(g_staged, 1)
                dve.wait_ge(g_staged, g + 1)
                A.vector(dve, g)


def route(nc, C, R, W, a):
    with ExitStack() as ctx:
        M = Mem(nc, ctx, C["sems"])
        w_out = M.sb("r_wout", [P, KT, D])
        rw = M.sb("r_rw", [P, KT, NE])
        g_ffn = M.sb("r_gffn", [P, D])
        mix = M.sb("r_mix", [P, KT, P])
        x_t, h_t, hn_t = M.sb("r_x", [P, D]), M.sb("r_h", [P, D]), M.sb("r_hn", [P, D])
        junk = M.sb("r_junk", [P, D], BF16)
        hnT = M.sb("r_hnT", [P, KT, P])
        lgT = M.sb("r_lgT", [NE, P])
        lg = M.sb("r_lg", [P, NT, NE])
        ss, rec, rstd = M.sb("r_ss", [P, 1]), M.sb("r_rec", [P, 1]), M.sb("r_rstd", [P, 1])
        top, top_i = M.sb("r_top", [P, NT, 8]), M.sb("r_topi", [P, NT, 8], U32)
        top_f, e4 = M.sb("r_topf", [P, NT, TOPK]), M.sb("r_e4", [P, NT, TOPK])
        se = M.sb("r_se", [P, NT])
        hot = w_out[:, 0, :].rearrange("p (t k e) -> p t k e", t=NT, k=TOPK)
        zeros = w_out[:, 1, :]
        took, took_b = M.sb("r_took", [P, NT, NE]), M.sb("r_tookb", [P, NT, NE], BF16)
        gate, rest = (w_out[:, 2, i * NT * NE:(i + 1) * NT * NE].rearrange("p (t e) -> p t e", t=NT) for i in (0, 1))
        cnt, more, cum, cum2 = (M.sb("r_" + s, [P, NE]) for s in ("cnt", "more", "cum", "cum2"))
        sel, one = M.sb("r_sel", [P, NE]), M.sb("r_one", [P, 8])
        items, items_i = M.sb("r_items", [P, 4]), M.sb("r_itemsi", [P, 4], I32)
        pM = M.ps("r_pM", [P, D])
        pX = [M.ps(f"r_pX{i}", [P, 4, P]) for i in range(2)]
        pR, pL = M.ps("r_pR", [NE, P]), M.ps("r_pL", [P, NE])
        pP, pC = M.ps("r_pP", [P, NT, NE]), M.ps("r_pC", [P, NE])
        s = lambda x: M.sem("r_" + x)
        wld, rld, x_in, mixed, product = s("wld"), s("rld"), s("xin"), s("mixed"), s("prod")
        summed, sq, rec_r, rstd_r, normed = s("sum"), s("sq"), s("rec"), s("rstd"), s("norm")
        h_out, hn_out, turned, x0_read, x1_read = s("hout"), s("hnout"), s("turned"), s("x0"), s("x1")
        lt, lt_ready, l_turned, l_read = s("lt"), s("ltr"), s("lturn"), s("lread")
        zero, z_out, own, e_in, e_out, took_r, posd = s("z"), s("zout"), s("own"), s("ein"), s("eout"), s("took"), s("pos")
        tab_ready, tab_out, tab_in, passed = s("tabr"), s("tabo"), s("tabi"), s("passed")
        block = ctx.enter_context(nc.Block())
        x_rows = a["x"].rearrange("b (t p) d -> (b t) p d", p=P)
        tiles = lambda dram: dram[0:SEQ].rearrange("(t p) d -> t p d", p=P)
        one_of = lambda v, t: v[bass.ds(t, 1)].rearrange("a p d -> (a p) d")

        @block.sync
        def _(sp):
            sp.dma_start(x_t[:], x_rows[0]).then_inc(x_in, 16)
            sp.dma_start(w_out[:], a["w_out"].rearrange("l (k p) d -> (l p) k d", p=P)).then_inc(wld, 16)
            sp.dma_start(rw[:], a["router_w"].rearrange("l (k p) e -> (l p) k e", p=P)).then_inc(rld, 16)
            sp.dma_start(g_ffn[:], a["ffn_norm"].to_broadcast([P, D])).then_inc(rld, 16)
            W.load(sp, 0, first=True)
            with sp.Fori(1, NT) as t:
                sp.wait_ge(summed, t)
                sp.dma_start(x_t[:], one_of(x_rows, t)).then_inc(x_in, 16)
            sp.wait_ge(zero, 1)
            for d in (R["acc"], R["hn"]):
                for i in range(DUMP // P):
                    sp.dma_start(d[SEQ + i * P:SEQ + (i + 1) * P, :], zeros).then_inc(z_out, 16)
            sp.wait_ge(z_out, 16 * 2 * DUMP // P)
            sp.wait_ge(tab_ready, 1)
            sp.dma_start(R["table"], items_i[:]).then_inc(tab_out, 16)
            sp.wait_ge(tab_out, 16)
            sp.dma_start(W.tab[:].rearrange("p n c -> p (n c)"),
                         R["table"].rearrange("(a n) c -> a (n c)", a=1).to_broadcast([P, MAX_ITEMS * 4])
                         ).then_inc(tab_in, 16)
            sp.wait_ge(tab_in, 16)

        @block.gpsimd
        def _(pool):
            def stage(t):
                pool.tensor_copy(mix[:], R["mixT"][:, :, bass.ds(t * P, P)]).then_inc(mixed, 1)
            stage(0)
            with pool.Fori(1, NT) as t:
                pool.wait_ge(product, 2 * t)
                stage(t)

        @block.tensor
        def _(pe):
            def half(t, i, first=False):
                if i == 0:
                    pe.wait_ge(mixed, t + 1)
                    if not first:
                        pe.wait_ge(summed, t)
                for k in range(KT):
                    last = nc.tensor.matmul(pM[:, i * 512:(i + 1) * 512], mix[:, k, :],
                                            w_out[:, k, i * 512:(i + 1) * 512], start=(k == 0), stop=(k == KT - 1))
                last.then_inc(product, 1)

            def turn(t):
                pe.wait_ge(normed, t + 1)
                for k in range(KT):
                    if k == 0:
                        pe.wait_ge(x0_read, t + 1)
                    if k == 4:
                        pe.wait_ge(x1_read, t + 1)
                    last = nc.tensor.transpose(pX[k // 4][:, k % 4, :], hn_t[:, k * P:(k + 1) * P], C["ident"][:])
                    if k % 4 == 3:
                        last.then_inc(turned, 1)

            def router(t):
                pe.wait_ge(x0_read, t + 2)
                pe.wait_ge(x1_read, t + 2)
                for k in range(KT):
                    last = nc.tensor.matmul(pR[:], rw[:, k, :], hnT[:, k, :], start=(k == 0), stop=(k == KT - 1))
                last.then_inc(lt, 1)
                pe.wait_ge(lt_ready, t + 1)
                hold(pe, l_read, t + 1, passed)
                nc.tensor.transpose(pL[:], lgT[:], C["ident"][0:NE, 0:NE]).then_inc(l_turned, 1)

            for q in (x0_read, x1_read, l_read):
                pe.sem_inc(q, 1)
            pe.wait_ge(wld, 16)
            pe.wait_ge(rld, 32)
            half(0, 0, True)
            half(0, 1, True)
            with pe.Fori(1, NT) as t:
                half(t, 0)
                turn(t - 1)
                half(t, 1)
                router(t - 1)
            turn(NT - 1)
            router(NT - 1)
            pe.wait_ge(took_r, 1)
            for t in range(NT):
                for j in range(t):
                    nc.tensor.matmul(pP[:, t, :], C["ones_b"][:], took_b[:, j, :], start=(j == 0), stop=False)
                nc.tensor.matmul(pP[:, t, :], C["before"][:], took_b[:, t, :], start=(t == 0), stop=True)
            for j in range(NT):
                last = nc.tensor.matmul(pC[:], C["ones_b"][:], took_b[:, j, :], start=(j == 0), stop=(j == NT - 1))
            last.then_inc(posd, 1)

        @block.scalar
        def _(act):
            with act.Fori(0, NT) as t:
                act.wait_ge(summed, t + 1)
                act.dma_start(one_of(tiles(R["acc"]), t), h_t[:]).then_inc(h_out, 16)
                nc.scalar.activation(junk[:], h_t[:], ACT.Square, accum_out=ss[:]).then_inc(sq, 1)
                act.wait_ge(rec_r, t + 1)
                nc.scalar.activation(rstd[:], rec[:], ACT.Sqrt).then_inc(rstd_r, 1)
                act.wait_ge(normed, t + 1)
                act.dma_start(one_of(tiles(R["hn"]), t), hn_t[:]).then_inc(hn_out, 16)
                act.wait_ge(turned, 2 * t + 1)
                nc.scalar.copy(hnT[:, 0:4, :], pX[0][:]).then_inc(x0_read, 1)
                act.wait_ge(lt, t + 1)
                nc.scalar.activation(lgT[:], pR[:], ACT.Identity, bias=C["rb"][:]).then_inc(lt_ready, 1)
            act.wait_ge(e_in, 1)
            nc.scalar.activation(e4[:], e4[:], ACT.Exp).then_inc(e_out, 1)
            act.wait_ge(h_out, 16 * NT)
            act.wait_ge(hn_out, 16 * NT)

        @block.vector
        def _(dve):
            def tile(t, first=False):
                dve.wait_ge(x_in, 16 * t + 16)
                dve.wait_ge(product, 2 * t + 2)
                if not first:
                    dve.wait_ge(h_out, 16 * t)
                nc.vector.tensor_tensor(h_t[:], pM[:], x_t[:], ALU.add).then_inc(summed, 1)
                dve.wait_ge(sq, t + 1)
                nc.vector.tensor_scalar(rec[:], ss[:], 1.0 / D, EPS, ALU.mult, ALU.add).then_inc(own, 1)
                dve.wait_ge(own, t + 1)
                nc.vector.reciprocal(rec[:], rec[:]).then_inc(rec_r, 1)
                dve.wait_ge(rstd_r, t + 1)
                if not first:
                    dve.wait_ge(hn_out, 16 * t)
                    dve.wait_ge(turned, 2 * t)
                nc.vector.scalar_tensor_tensor(hn_t[:], h_t[:], rstd[:], g_ffn[:], ALU.mult, ALU.mult
                                               ).then_inc(normed, 1)
                dve.wait_ge(turned, 2 * t + 2)
                nc.vector.tensor_copy(hnT[:, 4:8, :], pX[1][:]).then_inc(x1_read, 1)
                dve.wait_ge(l_turned, t + 1)
                nc.vector.tensor_copy(lg[:, bass.ds(t, 1), :].rearrange("p a e -> p (a e)"), pL[:]
                                      ).then_inc(l_read, 1)

            dve.wait_ge(rld, 32)
            tile(0, True)
            with dve.Fori(1, NT) as t:
                tile(t)
            S = Steps(own, NT)
            dve.wait_ge(l_read, NT + 1)
            V = nc.vector
            V.memset(zeros, 0.0).then_inc(zero, 1)
            B = lambda x, n: x.to_broadcast(n)
            full = [P, NT, TOPK, NE]
            for t in range(NT):
                S.mark(V.max(top[:, t, :], lg[:, t, :]))
            S.wait(dve)
            V.tensor_tensor(e4[:], top[:, :, 0:TOPK], B(top[:, :, 0:1], [P, NT, TOPK]), ALU.subtract
                            ).then_inc(e_in, 1)
            for t in range(NT):
                S.mark(V.max_index(top_i[:, t, :], top[:, t, :], lg[:, t, :]))
            S.wait(dve)
            S.mark(V.tensor_copy(top_f[:], top_i[:, :, 0:TOPK]))
            S.wait(dve)
            for t in range(NT):
                S.mark(V.tensor_tensor(hot[:, t], B(top_f[:, t, :].unsqueeze(2), [P, TOPK, NE]),
                                       B(C["iota"][:, 0:NE].unsqueeze(1), [P, TOPK, NE]), ALU.is_equal))
            S.wait(dve)
            S.mark(V.tensor_reduce(took[:], hot.rearrange("p t k e -> p t e k"), AX_X, ALU.add))
            S.wait(dve)
            V.tensor_copy(took_b[:], took[:]).then_inc(took_r, 1)
            dve.wait_ge(e_out, 1)
            S.mark(V.tensor_reduce(se[:], e4[:], AX_X, ALU.add))
            S.wait(dve)
            S.mark(V.reciprocal(se[:], se[:]))
            S.wait(dve)
            S.mark(V.tensor_tensor(e4[:], e4[:], B(se[:].unsqueeze(2), [P, NT, TOPK]), ALU.mult))
            S.wait(dve)
            for t in range(NT):
                S.mark(V.tensor_tensor(hot[:, t], hot[:, t], B(e4[:, t, :].unsqueeze(2), [P, TOPK, NE]), ALU.mult))
            S.wait(dve)
            S.mark(V.tensor_reduce(gate, hot.rearrange("p t k e -> p t e k"), AX_X, ALU.add))
            S.mark(V.tensor_copy(W.facts[:, :, :, 0], B(C["iota_p"][:].unsqueeze(2), [P, NT, NE])))
            S.mark(V.tensor_copy(W.facts[:, :, :, 1], B(C["iota_t"][:].unsqueeze(2), [P, NT, NE])))
            S.mark(V.memset(W.facts[:, :, :, 2], 1.0))
            S.wait(dve)
            S.mark(V.tensor_copy(W.facts[:, :, :, 3], gate))
            S.wait(dve)
            S.mark(V.tensor_tensor(rest, gate, W.facts[:, :, :, 3], ALU.subtract))
            S.wait(dve)
            S.mark(V.tensor_copy(W.facts[:, :, :, 4], rest))
            S.wait(dve)
            S.mark(V.tensor_tensor(rest, rest, W.facts[:, :, :, 4], ALU.subtract))
            S.wait(dve)
            S.mark(V.tensor_copy(W.facts[:, :, :, 5], rest))
            dve.wait_ge(posd, 1)
            S.mark(V.scalar_tensor_tensor(W.place[:], pP[:], 1.0, took[:], ALU.add, ALU.mult))
            S.mark(V.tensor_copy(cnt[:], pC[:]))
            S.wait(dve)
            S.mark(V.tensor_scalar(W.place[:], W.place[:], -1.0, None, ALU.add))
            S.mark(V.tensor_scalar(more[:], cnt[:], float(CAP), None, ALU.is_gt))
            for j in range(2, MORE + 1):
                S.wait(dve)
                S.mark(V.scalar_tensor_tensor(more[:], cnt[:], float(CAP * j), more[:], ALU.is_gt, ALU.add))
            src, dst, other = more, cum, cum2
            for d in (1, 2, 4, 8, 16):
                S.wait(dve)
                S.mark(V.tensor_copy(dst[:, 0:d], src[:, 0:d]))
                S.mark(V.tensor_tensor(dst[:, d:], src[:, d:], src[:, 0:NE - d], ALU.add))
                src, dst, other = dst, other, dst
            cumul = src
            S.wait(dve)
            S.mark(V.tensor_scalar(one[:, 0:1], C["iota_p"][:], float(-NE), None, ALU.add))
            S.wait(dve)
            S.mark(V.tensor_scalar(sel[:], cumul[:], one[:, 0:1], None, ALU.is_le))
            S.wait(dve)
            S.mark(V.tensor_reduce(one[:, 1:2], sel[:], AX_X, ALU.add))
            S.mark(V.tensor_tensor(sel[:], sel[:], cumul[:], ALU.mult))
            S.wait(dve)
            S.mark(V.tensor_reduce(one[:, 2:3], sel[:], AX_X, ALU.max))
            S.mark(V.tensor_scalar(one[:, 1:2], one[:, 1:2], float(NE - 1), None, ALU.min))
            S.wait(dve)
            S.mark(V.tensor_tensor(one[:, 3:4], one[:, 0:1], one[:, 2:3], ALU.subtract))
            S.mark(V.tensor_scalar(one[:, 4:5], C["iota_p"][:], float(NE), None, ALU.is_ge))
            S.wait(dve)
            S.mark(V.tensor_scalar(one[:, 3:4], one[:, 3:4], float(CAP), float(CAP), ALU.mult, ALU.add))
            S.mark(V.tensor_tensor(one[:, 5:6], one[:, 1:2], C["iota_p"][:], ALU.subtract))
            S.wait(dve)
            S.mark(V.tensor_tensor(items[:, 3:4], one[:, 3:4], one[:, 4:5], ALU.mult))
            S.mark(V.tensor_tensor(one[:, 5:6], one[:, 5:6], one[:, 4:5], ALU.mult))
            S.wait(dve)
            S.mark(V.tensor_tensor(items[:, 0:1], one[:, 5:6], C["iota_p"][:], ALU.add))
            S.wait(dve)
            S.mark(V.tensor_scalar(sel[:], C["iota"][:, 0:NE], items[:, 0:1], None, ALU.is_equal))
            S.wait(dve)
            S.mark(V.tensor_tensor(sel[:], sel[:], cnt[:], ALU.mult))
            S.wait(dve)
            S.mark(V.tensor_reduce(one[:, 6:7], sel[:], AX_X, ALU.add))
            S.mark(V.tensor_scalar(items[:, 2:3], cumul[:, NE - 1:NE], float(NE), None, ALU.add))
            S.wait(dve)
            S.mark(V.tensor_tensor(items[:, 1:2], one[:, 6:7], items[:, 3:4], ALU.subtract))
            S.wait(dve)
            V.tensor_copy(items_i[:], items[:]).then_inc(tab_ready, 1)
            dve.wait_ge(tab_in, 16)
            S.mark(V.tensor_copy(W.tab_f[:], W.tab[:, :, 3]))
            S.wait(dve)


class Weights:

    def __init__(self, nc, M, a):
        self.a = a
        self.w1 = [M.sb(f"w1_{c}", [P, KT, 2, P]) for c in range(FC)]
        self.w2 = [M.sb(f"w2_{c}", [P, DFF // P, D // DC]) for c in range(DC)]
        self.tab = M.sb("tab", [P, MAX_ITEMS, 4], I32)
        self.tab_f = M.sb("tab_f", [P, MAX_ITEMS])
        self.facts = M.sb("facts", [P, NT, NE, 6], BF16)
        self.place = M.sb("place", [P, NT, NE])
        self.w1_in = [M.sem(f"w1in{c}") for c in range(FC)]
        self.w2_in = [M.sem(f"w2in{c}") for c in range(DC)]
        self.up_done, self.down_done = M.sem("up_done"), M.sem("down_done")

    def load(self, sp, n, e=0, first=False):
        w1 = self.a["moe_w1"].rearrange("l e (k p) (two c f) -> c (l e) two p k f", p=P, two=2, f=P)
        w2 = self.a["moe_w2"].rearrange("l e (k p) (c d) -> c (l e) p k d", p=P, c=DC)
        for c in range(FC):
            if not first:
                sp.wait_ge(self.up_done, FC * (n - 1) + c + 1)
            for two in range(2):
                sp.dma_start(self.w1[c][:, :, two, :], w1[c, bass.ds(e, 1), two].rearrange("a p k f -> (a p) k f")
                             ).then_inc(self.w1_in[c], 16)
        for c in range(DC):
            if not first:
                sp.wait_ge(self.down_done, DC * (n - 1) + c + 1)
            sp.dma_start(self.w2[c][:], w2[c, bass.ds(e, 1)].rearrange("a p k d -> (a p) k d")
                         ).then_inc(self.w2_in[c], 16)


def experts(nc, C, R, W):
    with ExitStack() as ctx:
        M = Mem(nc, ctx, C["sems"])
        place_e, facts_e = M.sb("e_place", [P, NT]), M.sb("e_facts", [P, NT, 6], BF16)
        onehot = M.sb("e_onehot", [P, NT, CAP], BF16)
        iota8 = C["iota"]
        told = M.sb("e_told", [P, 2, 6])
        tmp = M.sb("e_tmp", [P, 4, 2])
        dump = M.sb("e_dump", [P, 2])
        idx_next, idx = M.sb("e_idxn", [P, 2], I32), M.sb("e_idx", [P, 2], I32)
        gate_next, gate = M.sb("e_gaten", [P, 2]), M.sb("e_gate", [P, 2])
        x0, x1 = M.sb("e_x0", [P, D]), M.sb("e_x1", [64, D])
        xT = M.sb("e_xT", [P, KT, CAP])
        b1, b2 = M.sb("e_b1", [P, 2 * FC]), M.sb("e_b2", [P, KT])
        g1, g2, up = M.sb("e_g1", [P, 2, CAP]), M.sb("e_g2", [P, 2, CAP]), M.sb("e_up", [P, 2, CAP])
        sg = M.sb("e_sg", [P, 2, CAP])
        hT = M.sb("e_hT", [P, FC, CAP])
        yT = M.sb("e_yT", [P, KT, CAP])
        y0, y1 = M.sb("e_y0", [P, D]), M.sb("e_y1", [64, D])
        pH = [M.ps(f"e_pH{i}", [P, 2, 256]) for i in range(2)]
        pY = [M.ps(f"e_pY{i}", [P, 2, 256]) for i in range(2)]
        pX = [M.ps(f"e_pX{i}", [P, 4, P]) for i in range(2)]
        pD = M.ps("e_pD", [P, 2, 8])
        s = lambda x: M.sem("e_" + x)
        cleared, picked, told_ready, idx_ready = s("clr"), s("picked"), s("told"), s("idx")
        gathered, cur_ready = [s("ga0"), s("ga1")], s("cur")
        bank_turned, bank_read = [s("bt0"), s("bt1")], [s("br0"), s("br1")]
        h_read, lin_ready, sg_ready, h_ready = s("hread"), s("lin"), s("sg"), s("h")
        yT_ready, scat, scattered = s("yT"), [s("sc0"), s("sc1")], s("scattered")
        own_d, own_a, b_staged, passed = s("od"), s("oa"), s("bst"), s("passed")
        block = ctx.enter_context(nc.Block())
        PER, FREE = 4, 1

        def seq_late(n):
            return 2 + PER * n

        def seq_x(n):
            return 3 + PER * n

        def seq_early(n):
            return 5 + PER * n

        def n_items(eng):
            return eng.value_load(W.tab[0:1, 0, 2:3], min_val=NE, max_val=NE + SEQ * TOPK // CAP)

        def expert(eng, n):
            return eng.value_load(W.tab[0:1, bass.ds(n, 1), 0:1].rearrange("p a c -> p (a c)"),
                                  min_val=0, max_val=NE - 1)

        @block.sync
        def _(sp):
            last = n_items(sp)
            with sp.Fori(1, last) as n:
                W.load(sp, n, expert(sp, n))

        @block.gpsimd
        def _(pool):
            def gather(i):
                hold(pool, idx_ready, i + 1, passed)
                pool.indirect_dma_start(x0[:], None, R["hn"], bass.IndirectOffsetOnAxis(idx_next[:, 0:1], 0)
                                        ).then_inc(gathered[0], 16)
                pool.indirect_dma_start(x1[:], None, R["hn"], bass.IndirectOffsetOnAxis(idx_next[0:64, 1:2], 0)
                                        ).then_inc(gathered[1], 16)
            for t in (told, xT, hT, yT, y0, y1, gate, idx_next):
                pool.memset(t[:], 0.0 if t is not idx_next else 0).then_inc(cleared, 1)
            last = n_items(pool)
            gather(0)
            def scatter(n):
                for b in range(2):
                    hold(pool, bank_read[b], seq_late(n) + 1 + FREE, passed)
                pool.indirect_dma_start(R["acc"], bass.IndirectOffsetOnAxis(idx[:, 0:1], 0), y0[:], None,
                                        compute_op=ALU.add).then_inc(scat[0], 16)
                pool.indirect_dma_start(R["acc"], bass.IndirectOffsetOnAxis(idx[0:64, 1:2], 0), y1[:], None,
                                        compute_op=ALU.add).then_inc(scat[1], 16)
                for b in range(2):
                    pool.wait_ge(scat[b], 16 * n + 16)
                pool.sem_inc(scattered, 1)

            with pool.Fori(0, last) as n:
                scatter(n)
                gather(n + 1)
            scatter(last)
            for b in range(2):
                pool.wait_ge(gathered[b], 16)

        @block.tensor
        def _(pe):
            def pick(i):
                pe.wait_ge(picked, i + 1)
                for j, rows in enumerate((P, 64)):
                    for t in range(NT):
                        last = nc.tensor.matmul(pD[0:rows, j, 0:6], onehot[:, t, j * P:j * P + rows],
                                                facts_e[:, t, :], start=(t == 0), stop=(t == NT - 1))
                last.then_inc(told_ready, 1)

            def turn_x(i, seq, steps):
                for j in steps:
                    if j == 0:
                        for b in range(2):
                            pe.wait_ge(gathered[b], 16 * i + 16)
                    pe.wait_ge(bank_read[j % 2], seq + j // 2 + FREE)
                    for m in range(2):
                        k = 2 * j + m
                        room = pX[j % 2][:, 2 * m:2 * m + 2, :].rearrange("p a q -> p (a q)")
                        nc.tensor.transpose(room[:, 0:P], x0[:, k * P:(k + 1) * P], C["ident"][:])
                        last = nc.tensor.transpose(room[:, P:CAP], x1[:, k * P:(k + 1) * P], C["ident"][0:64, 0:64])
                    last.then_inc(bank_turned[j % 2], 1)

            def turn_y(n, c):
                if c < 2:
                    pe.wait_ge(yT_ready, DC * n + c + 1 + 2)
                    pe.wait_ge(bank_read[c % 2], seq_early(n) + FREE)
                else:
                    pe.wait_ge(yT_ready, DC * n + c + 1 + 2 - DC)
                    pe.wait_ge(bank_read[c % 2], seq_late(n) + FREE)
                for m in range(2):
                    nc.tensor.transpose(pX[c % 2][:, m, :], yT[:, 2 * c + m, 0:P], C["ident"][:])
                    last = nc.tensor.transpose(pX[c % 2][0:64, 2 + m, :], yT[:, 2 * c + m, P:CAP], C["ident"][:])
                last.then_inc(bank_turned[c % 2], 1)

            def item(n, N):
                for b in range(2):
                    pe.wait_ge(bank_read[b], PER * n + 1 + FREE)
                for c in range(FC):
                    pe.wait_ge(W.w1_in[c], 32 * n + 32)
                    pe.wait_ge(h_read, FC * n + c + 1)
                    for two in range(2):
                        for k in range(KT):
                            last = nc.tensor.matmul(pH[c % 2][:, two, 0:N], W.w1[c][:, k, two, :], xT[:, k, 0:N],
                                                    start=(k == 0), stop=(k == KT - 1))
                    last.then_inc(W.up_done, 1)
                    if c == 0:
                        turn_y(n, 2)
                        turn_y(n, 3)
                    if c == 4:
                        pick(n + 1)
                for c in range(DC):
                    pe.wait_ge(W.w2_in[c], 16 * n + 16)
                    pe.wait_ge(yT_ready, DC * n + c + 1)
                    steps = [(k, m) for m in range(2) for k in range(DFF // P)]
                    if c == 0:
                        steps.sort(key=lambda s: s[0] == DFF // P - 1)
                    for k, m in steps:
                        if c == 0 and m == 0:
                            pe.wait_ge(h_ready, FC * n + k + 1)
                        last = nc.tensor.matmul(pY[c % 2][:, m, 0:N], W.w2[c][:, k, m * P:(m + 1) * P],
                                                hT[:, k, 0:N], start=(k, m) == steps[0], stop=(k, m) == steps[-1])
                    last.then_inc(W.down_done, 1)
                    if c < 2:
                        turn_x(n + 1, seq_x(n), (2 * c, 2 * c + 1))
                    if c == 2:
                        turn_y(n, 0)
                        turn_y(n, 1)

            def choose(n, left, variants):
                if len(variants) == 1:
                    item(n, variants[0])
                    return
                with pe.If(left <= variants[0]):
                    item(n, variants[0])
                with pe.Else():
                    choose(n, left, variants[1:])

            for b in range(2):
                pe.sem_inc(bank_read[b], FREE)
            pe.sem_inc(h_read, 2)
            pe.sem_inc(yT_ready, 2)
            pe.wait_ge(cleared, 8 + 4)
            last = n_items(pe)
            pick(0)
            turn_x(0, 0, range(4))
            for b in range(2):
                pe.wait_ge(bank_read[b], 2 + FREE)
            with pe.Fori(0, last) as n:
                left = pe.value_load(W.tab[0:1, bass.ds(n, 1), 1:2].rearrange("p a c -> p (a c)"),
                                     min_val=-SEQ * 64, max_val=SEQ)
                choose(n, left, VARIANTS)
            turn_y(last, 2)
            turn_y(last, 3)

        @block.scalar
        def _(act):
            def stage_b2(i):
                e = expert(act, i)
                nc.scalar.copy(b2[:], C["b2"][:, bass.ds(e * KT, KT)]).then_inc(own_a, 1)

            def read_x(seq, steps=(0, 2)):
                for j in steps:
                    act.wait_ge(bank_turned[0], seq + j // 2 + 1)
                    nc.scalar.copy(xT[:, 2 * j:2 * j + 2, :],
                                   pX[0][:].rearrange("p (m a) q -> p m (a q)", m=2)[:, :, 0:CAP]
                                   ).then_inc(bank_read[0], 1)

            act.wait_ge(cleared, 8 + 4)
            stage_b2(0)
            last = n_items(act)
            read_x(0)
            def results(n, c):
                seq = seq_early(n) if c < 2 else seq_late(n)
                act.wait_ge(bank_turned[0], seq + 1)
                nc.scalar.activation(y0[:, 2 * c * P:(2 * c + 2) * P], pX[0][:, 0:2, :].rearrange("p a q -> p (a q)"),
                                     ACT.Copy, scale=gate[:, 0:1])
                nc.scalar.activation(y1[:, 2 * c * P:(2 * c + 2) * P],
                                     pX[0][0:64, 2:4, :].rearrange("p a q -> p (a q)"),
                                     ACT.Copy, scale=gate[0:64, 1:2]).then_inc(bank_read[0], 1)

            with act.Fori(0, last) as n:
                for c in range(FC):
                    act.wait_ge(lin_ready, FC * n + c + 1)
                    nc.scalar.activation(sg[:, c % 2], g1[:, c % 2], ACT.Sigmoid, scale=ALPHA).then_inc(sg_ready, 1)
                    if c == 0:
                        results(n, 2)
                act.wait_ge(own_a, n + 1)
                for c in range(DC):
                    act.wait_ge(W.down_done, DC * n + c + 1)
                    for m in range(2):
                        k = 2 * c + m
                        ins = nc.scalar.activation(yT[:, k, :], pY[c % 2][:, m, 0:CAP], ACT.Identity,
                                                   bias=b2[:, k:k + 1])
                    ins.then_inc(yT_ready, 1)
                    if c < 2:
                        read_x(seq_x(n), (2 * c,))
                    if c == 2:
                        act.wait_ge(cur_ready, n + 1)
                        results(n, 0)
                act.wait_ge(yT_ready, DC * (n + 1) + 2)
                stage_b2(n + 1)
            results(last, 2)

        @block.vector
        def _(dve):
            V = nc.vector
            B = lambda x, n: x.to_broadcast(n)
            OWN = 3 * FC + 2 + 6

            def prepare(i):
                e = expert(dve, i)
                V.tensor_scalar(place_e[:].unsqueeze(2), W.place[:, :, bass.ds(e, 1)],
                                W.tab_f[:, bass.ds(i, 1)], None, ALU.subtract).then_inc(b_staged, 1)
                V.tensor_copy(facts_e[:].unsqueeze(2), W.facts[:, :, bass.ds(e, 1), :])
                dve.wait_ge(b_staged, 2 * i + 1)
                for t in range(NT):
                    ins = V.tensor_scalar(onehot[:, t, :], C["iota"][:], place_e[:, t:t + 1], None, ALU.is_equal)
                ins.then_inc(picked, 1)

            def stage_b1(i):
                e = expert(dve, i)
                V.tensor_copy(b1[:], C["b1"][:, bass.ds(e * (2 * FC), 2 * FC)]).then_inc(b_staged, 1)

            def addresses(i, S):
                dve.wait_ge(told_ready, i + 1)
                S.mark(V.tensor_copy(told[:, 0, :], pD[:, 0, 0:6]))
                S.mark(V.tensor_copy(told[0:64, 1, :], pD[0:64, 1, 0:6]))
                S.wait(dve)
                S.mark(V.tensor_scalar(tmp[:, 0], told[:, :, 2], -1.0, 1.0, ALU.mult, ALU.add))
                S.mark(V.scalar_tensor_tensor(tmp[:, 1], told[:, :, 1], float(P), told[:, :, 0], ALU.mult, ALU.add))
                S.mark(V.tensor_tensor(tmp[:, 2], told[:, :, 3], told[:, :, 4], ALU.add))
                S.wait(dve)
                S.mark(V.tensor_tensor(tmp[:, 0], tmp[:, 0], dump[:], ALU.mult))
                V.tensor_tensor(gate_next[:], tmp[:, 2], told[:, :, 5], ALU.add)
                S.wait(dve)
                V.tensor_tensor(idx_next[:], tmp[:, 0], tmp[:, 1], ALU.add).then_inc(idx_ready, 1)

            def read_x(seq):
                for j in (1, 3):
                    dve.wait_ge(bank_turned[1], seq + j // 2 + 1)
                    V.tensor_copy(xT[:, 2 * j:2 * j + 2, :],
                                  pX[1][:].rearrange("p (m a) q -> p m (a q)", m=2)[:, :, 0:CAP]
                                  ).then_inc(bank_read[1], 1)

            for ps in (*pH, *pY):
                V.memset(ps[:], 0.0).then_inc(cleared, 1)
            dve.wait_ge(cleared, 8 + 4)
            S = Steps(own_d)
            S.mark(V.tensor_scalar(dump[:, 0:1], C["iota_p"][:], float(SEQ), None, ALU.add))
            S.mark(V.tensor_scalar(dump[:, 1:2], C["iota_p"][:], float(SEQ + P), None, ALU.add))
            S.wait(dve)
            prepare(0)
            stage_b1(0)
            addresses(0, S)
            S.mark(V.tensor_copy(idx[:], dump[:]))
            S.wait(dve)

            def results(n, c):
                seq = seq_early(n) if c < 2 else seq_late(n)
                dve.wait_ge(bank_turned[1], seq + 1)
                V.tensor_scalar(y0[:, 2 * c * P:(2 * c + 2) * P], pX[1][:, 0:2, :].rearrange("p a q -> p (a q)"),
                                gate[:, 0:1], None, ALU.mult)
                V.tensor_scalar(y1[:, 2 * c * P:(2 * c + 2) * P], pX[1][0:64, 2:4, :].rearrange("p a q -> p (a q)"),
                                gate[0:64, 1:2], None, ALU.mult).then_inc(bank_read[1], 1)

            last = n_items(dve)
            read_x(0)
            n0 = S.n
            with dve.Fori(0, last) as n:
                S = Steps(own_d, n * OWN + n0)
                dve.wait_ge(b_staged, 2 * n + 2)
                for c in range(FC):
                    dve.wait_ge(W.up_done, FC * n + c + 1)
                    S.mark(V.tensor_scalar(g1[:, c % 2], pH[c % 2][:, 0, 0:CAP], b1[:, c:c + 1], LIMIT, ALU.add, ALU.min))
                    V.tensor_scalar(up[:, c % 2], pH[c % 2][:, 1, 0:CAP], b1[:, FC + c:FC + c + 1], LIMIT,
                                    ALU.add, ALU.min).then_inc(h_read, 1)
                    V.drain().then_inc(lin_ready, 1)
                    dve.wait_ge(lin_ready, FC * n + c + 1)
                    S.mark(V.tensor_scalar(up[:, c % 2], up[:, c % 2], -LIMIT, 1.0, ALU.max, ALU.add))
                    dve.wait_ge(sg_ready, FC * n + c + 1)
                    S.mark(V.tensor_tensor(g2[:, c % 2], g1[:, c % 2], sg[:, c % 2], ALU.mult))
                    S.wait(dve)
                    V.tensor_tensor(hT[:, c, :], g2[:, c % 2], up[:, c % 2], ALU.mult).then_inc(h_ready, 1)
                    if c == 0:
                        results(n, 3)
                    if c == 1:
                        prepare(n + 1)
                    if c == 5:
                        dve.wait_ge(scattered, n + 1)
                        dve.wait_ge(bank_read[0], seq_late(n) + 1 + FREE)
                        dve.wait_ge(idx_ready, n + 1)
                        for b in range(2):
                            dve.wait_ge(gathered[b], 16 * n + 16)
                        S.mark(V.tensor_copy(idx[:], idx_next[:]))
                        S.mark(V.tensor_copy(gate[:], gate_next[:]))
                        S.wait(dve)
                        dve.sem_inc(cur_ready, 1)
                        addresses(n + 1, S)
                stage_b1(n + 1)
                read_x(seq_x(n))
                dve.wait_ge(cur_ready, n + 1)
                results(n, 1)
            results(last, 3)
            assert S.n == OWN, S.n


def final(nc, C, R, a, out):
    HALVES = NT // 2
    with ExitStack() as ctx:
        M = Mem(nc, ctx, C["sems"])
        h = M.sb("f_h", [P, NT, D])
        g = M.sb("f_g", [P, D])
        junk = M.sb("f_junk", [P, NT, D], BF16)
        ss, rec, rstd = M.sb("f_ss", [P, NT]), M.sb("f_rec", [P, NT]), M.sb("f_rstd", [P, NT])
        h_in = [M.sem(f"f_in{t}") for t in range(NT)]
        g_in, sq, own, rec_r, rstd_r, done, stored = (M.sem("f_" + s) for s in ("g", "sq", "own", "rec", "rstd", "done", "st"))
        block = ctx.enter_context(nc.Block())
        acc = R["acc"][0:SEQ].rearrange("(t p) d -> t p d", p=P)
        res = out.rearrange("b (t p) d -> (b t) p d", p=P)

        @block.sync
        def _(sp):
            sp.dma_start(g[:], a["final_norm"].rearrange("(l d) -> l d", l=1).to_broadcast([P, D])).then_inc(g_in, 16)
            for t in range(NT):
                sp.dma_start(h[:, t, :], acc[t]).then_inc(h_in[t], 16)
            for t in range(NT):
                sp.wait_ge(done, t + 1)
                sp.dma_start(res[t], h[:, t, :]).then_inc(stored, 16)
            sp.wait_ge(stored, 16 * NT)

        @block.scalar
        def _(act):
            for t in range(NT):
                act.wait_ge(h_in[t], 16)
                nc.scalar.activation(junk[:, t], h[:, t, :], ACT.Square, accum_out=ss[:, t:t + 1]).then_inc(sq, 1)
                if t >= 1:
                    act.wait_ge(rec_r, t)
                    nc.scalar.activation(rstd[:, t - 1:t], rec[:, t - 1:t], ACT.Sqrt).then_inc(rstd_r, 1)
            act.wait_ge(rec_r, NT)
            nc.scalar.activation(rstd[:, NT - 1:], rec[:, NT - 1:], ACT.Sqrt).then_inc(rstd_r, 1)

        @block.vector
        def _(dve):
            dve.wait_ge(g_in, 16)
            for t in range(NT + 1):
                if t < NT:
                    dve.wait_ge(sq, t + 1)
                    nc.vector.tensor_scalar(rec[:, t:t + 1], ss[:, t:t + 1], 1.0 / D, EPS, ALU.mult, ALU.add
                                            ).then_inc(own, 1)
                    dve.wait_ge(own, t + 1)
                    nc.vector.reciprocal(rec[:, t:t + 1], rec[:, t:t + 1]).then_inc(rec_r, 1)
                if t >= 1:
                    dve.wait_ge(rstd_r, t)
                    nc.vector.scalar_tensor_tensor(h[:, t - 1, :], h[:, t - 1, :], rstd[:, t - 1:t], g[:],
                                                   ALU.mult, ALU.mult).then_inc(done, 1)


def layer(nc, a, out, upto=None, debug=None):
    R = {k: nc.dram_tensor(k, (SEQ + DUMP, D), F32, kind="Internal").ap() for k in ("acc", "hn")}
    R["table"] = nc.dram_tensor("table", (MAX_ITEMS, 4), I32, kind="Internal").ap()
    with ExitStack() as whole:
        M = Mem(nc, whole)
        C = {
            "sems": [],
            "ident": M.sb("ident", [P, P]), "ident_b": M.sb("ident_b", [P, P], BF16),
            "causal": M.sb("causal", [P, P], BF16), "far": M.sb("far", [P, P], BF16),
            "cmp_mask": M.sb("cmp_mask", [P, NT, 64], BF16), "before": M.sb("before", [P, P], BF16),
            "ones_b": M.sb("ones_b", [P, P], BF16), "late": M.sb("late", [P, 1]),
            "iota_i": M.sb("iota_i", [P, CAP], I32), "iota": M.sb("iota", [P, CAP]),
            "iota_p_i": M.sb("iota_p_i", [P, 1], I32), "iota_p": M.sb("iota_p", [P, 1]),
            "iota_t_i": M.sb("iota_t_i", [P, NT], I32), "iota_t": M.sb("iota_t", [P, NT]),
            "vec": M.sb("vec", [P, 19]), "b1": M.sb("b1", [P, NE * 2 * FC]), "b2": M.sb("b2", [P, NE * KT]),
            "rb": M.sb("rb", [NE, 1]), "trig": M.sb("trig", [P, 2, NT + 1, NF]),
        }
        constants(nc, C, a)
        with ExitStack() as early:
            M = Mem(nc, early)
            R["mixT"] = M.sb("mixT", [P, KT, SEQ])
            with ExitStack() as heads:
                M = Mem(nc, heads)
                R["latT"] = M.sb("latT", [P, 3, SEQ])
                R["nsaT"] = M.sb("nsaT", [96, 12, SEQ])
                R["v_s"], R["v_w"] = M.sb("v_s", [P, NT, KVW]), M.sb("v_w", [P, NT, KVW])
                R["k_pe"] = M.sb("k_pe", [P, NT, ROPE])
                R["gates"] = M.sb("gates", [P, NT, 3 * H_NSA])
                R["kcT"] = M.sb("kcT", [96, G_NSA, 64])
                R["v_c"] = M.sb("v_c", [64, G_NSA, DH])
                with ExitStack() as blocks:
                    R["rawT"] = Mem(nc, blocks).sb("rawT", [P, 4, SEQ])
                    project(nc, C, R, a)
                    compress(nc, C, R, a)
                nc.clear_and_free_semaphores(C["sems"])
                nc.all_engine_barrier()
                C["sems"] = []
                mla(nc, C, R, a)
                nsa(nc, C, R)
            with ExitStack() as late:
                W = Weights(nc, Mem(nc, late, C["sems"]), a)
                route(nc, C, R, W, a)
                experts(nc, C, R, W)
        final(nc, C, R, a, out)


_INS = ["x", "positions", "attn_norm", "w_in", "mla_q_norm", "mla_w_q_up", "mla_kv_norm", "mla_w_kv_up",
        "nsa_cmp_pos", "nsa_cmp_w1", "nsa_cmp_w2", "w_out", "ffn_norm", "router_w", "router_b",
        "moe_w1", "moe_b1", "moe_w2", "moe_b2", "final_norm"]


def kernel(**inputs):
    import numpy as _np
    import concourse.bacc as _bacc
    from concourse import mybir as _mybir
    from concourse.bass_utils import run_bass_kernel_spmd as _run

    nc = _bacc.Bacc("TRN2", target_bir_lowering=False, num_devices=1)
    arrays, args = {}, {}
    for name in _INS:
        x = _np.ascontiguousarray(inputs[name])
        arrays[f"in_{name}"] = x
        args[name] = nc.dram_tensor(f"in_{name}", x.shape, _mybir.dt.from_np(x.dtype), kind="ExternalInput").ap()
    out = nc.dram_tensor("out_0", (1, SEQ, D), F32, kind="ExternalOutput").ap()
    layer(nc, args, out)
    r = _run(nc, [arrays], core_ids=[0])
    return r.results[0]["out_0"]
```

```python
from contextlib import ExitStack

import numpy as np

import concourse.bass as bass
from concourse import mybir
from concourse.alu_op_type import AluOpType as ALU

F32 = mybir.dt.float32
BF16 = mybir.dt.bfloat16
I32 = mybir.dt.int32
U32 = mybir.dt.uint32
ACT = mybir.ActivationFunctionType
AX_X = mybir.AxisListType.X
AX_XY = mybir.AxisListType.XY

P = 128
SEQ, D = 1024, 1024
NT, KT = SEQ // P, D // P
EPS = 1e-5
NEG = -1e30
THETA = 500000.0

H_MLA, NOPE, ROPE, V_DIM = 8, 64, 32, 64
QK_MLA = NOPE + ROPE
Q_RANK, KV_RANK = 256, 128
H_NSA, G_NSA, DH, ROPE_N = 8, 2, 64, 16
CMP_BLOCK, CMP_STRIDE, CMP_HID = 32, 16, 128
N_CMP = (SEQ - CMP_BLOCK) // CMP_STRIDE + 1
WINDOW = 512
WT = WINDOW // P
KVW = G_NSA * DH
IN_COLS = Q_RANK + KV_RANK + ROPE + H_NSA * DH + 6 * KVW + 3 * H_NSA
C_Q, C_KV = 0, Q_RANK
C_PE = C_KV + KV_RANK
C_QN = C_PE + ROPE
C_KC = C_QN + H_NSA * DH
C_KW = C_KC + 4 * KVW
NF = ROPE // 2 + ROPE_N // 2

NE, TOPK, DFF = 32, 4, 1024
LIMIT, ALPHA = 7.0, 1.702
CAP = 192
VARIANTS = tuple(range(P, CAP + 1, 8))
MORE = (SEQ - 1) // CAP
EXTRA = SEQ * TOPK // CAP + 1
MAX_ITEMS = NE + EXTRA
DUMP = 256
FC = 8
DC = 4

TWO_PI = 2.0 * np.pi
C1 = 6.28125
C2 = float(np.float32(np.round((TWO_PI - C1) * 2.0 ** 20) / 2.0 ** 20))
C3 = float(TWO_PI - C1 - C2)
ROUND = 12582912.0
PI_IN = 3.1415925


class Steps:

    def __init__(self, sem, base=0):
        self.sem, self.base, self.n = sem, base, 0

    def mark(self, ins):
        ins.then_inc(self.sem, 1)
        self.n += 1
        return ins

    def wait(self, eng):
        eng.wait_ge(self.sem, self.base + self.n)


def hold(eng, sem, value, passed):
    eng.wait_ge(sem, value)
    eng.sem_inc(passed, 1)


def frequencies():
    def inv(rot):
        return np.float32(THETA ** (-np.arange(0, rot, 2) / rot))
    return [float(f) for f in np.concatenate([inv(ROPE), inv(ROPE_N)])]


class Mem:

    def __init__(self, nc, ctx, sems=None):
        self.nc, self.ctx, self.sems = nc, ctx, sems

    def sb(self, name, shape, dt=F32):
        return self.ctx.enter_context(self.nc.sbuf_tensor(name, shape, dt))

    def ps(self, name, shape, dt=F32):
        return self.ctx.enter_context(self.nc.psum_tensor(name, shape, dt))

    def sem(self, name):
        self.sems.append(self.nc.alloc_semaphore(name=name))
        return self.sems[-1]


class Ahead:

    def __init__(self, nc, M, a):
        self.a = a
        self.w_in = M.sb("w_in", [P, KT, IN_COLS])
        self.x_t = M.sb("x_t", [P, D])
        self.w_loaded, self.x_loaded = [M.sem(f"p_w{i}") for i in range(4)], M.sem("p_x")
        self.x_rows = a["x"].rearrange("b (t p) d -> (b t) p d", p=P)
        LP = CMP_BLOCK // 2
        self.cmp_w1 = M.sb("cw1", [P, 2, LP, CMP_HID])
        self.cmp_w2 = M.sb("cw2", [P, 2, DH])
        self.cmp_pos = M.sb("cpos", [2 * LP, 2 * DH])
        self.cmp_loaded, self.pos_loaded = M.sem("cc_ld"), M.sem("cc_ldp")

    def load_products(self, sp):
        w_rows = self.a["w_in"].rearrange("l (k p) c -> (l p) k c", p=P)
        sp.dma_start(self.x_t[:], self.x_rows[0]).then_inc(self.x_loaded, 16)
        for i, (c0, c1) in enumerate(PROJ):
            sp.dma_start(self.w_in[:, :, c0:c1], w_rows[:, :, c0:c1]).then_inc(self.w_loaded[i], 16)

    def load_compress(self, sp):
        a = self.a
        sp.dma_start(self.cmp_pos[:], a["nsa_cmp_pos"].rearrange("l c (lp two) d -> (l c lp) (two d)", two=2)
                     ).then_inc(self.pos_loaded, 16)
        for c in range(2):
            sp.dma_start(self.cmp_w1[:, c], a["nsa_cmp_w1"][0, c].rearrange("(lp two) d h -> (two d) lp h", two=2)
                         ).then_inc(self.cmp_loaded, 16)
        sp.dma_start(self.cmp_w2[:], a["nsa_cmp_w2"].rearrange("l c h d -> (l h) c d")).then_inc(self.cmp_loaded, 16)


def constants(nc, C, F, a):
    with ExitStack() as ctx:
        M = Mem(nc, ctx, C["sems"])
        rows = M.sb("rows", [19, P])
        rows_b1 = M.sb("rows_b1", [P, 4, P])
        rows_b2 = M.sb("rows_b2", [P, 2, P])
        pos_i = M.sb("pos_i", [NT, P], I32)
        pos_r = M.sb("pos_r", [NT, P])
        posc_i = M.sb("posc_i", [N_CMP, 1], I32)
        posp = M.sb("posp", [P, NT + 1])
        freq = M.sb("freq", [P, NF])
        ang = M.sb("ang", [P, NT + 1, NF])
        turns = M.sb("turns", [P, 2, NT + 1, NF])
        red = M.sb("red", [P, 2, NT + 1, NF])
        ones_f = M.sb("ones_f", [P, P])
        it_i = M.sb("it_i", [P, CAP], I32)
        pS = [M.ps(f"pc{i}", [P, 4, P]) for i in range(4)]
        ld_rows, ld_b, ld_pos, ld_posc = M.sem("c_rows"), M.sem("c_b"), M.sem("c_pos"), M.sem("c_posc")
        masks, fr, tr, own = M.sem("c_masks"), M.sem("c_freq"), M.sem("c_tr"), M.sem("c_own")
        zeroed, table, ev = M.sem("c_zero"), M.sem("c_table"), M.sem("c_ev")
        block = ctx.enter_context(nc.Block())

        @block.sync
        def _(sp):
            for r0, name, n in ((0, "attn_norm", 8), (8, "mla_q_norm", 2), (10, "mla_kv_norm", 1),
                                (11, "ffn_norm", 8)):
                sp.dma_start(rows[r0:r0 + n, :], a[name].rearrange("l (k p) -> (l k) p", p=P)).then_inc(ld_rows, 16)
            sp.dma_start(pos_i[:], a["positions"].rearrange("b (t p) -> (b t) p", p=P)).then_inc(ld_pos, 16)
            ends = a["positions"].rearrange("b (n s) -> (b n) s", s=CMP_STRIDE)[1:1 + N_CMP, CMP_STRIDE - 1:CMP_STRIDE]
            sp.dma_start(posc_i[:], ends, allow_slow_non_contiguous=True).then_inc(ld_posc, 16)
            sp.dma_start(rows_b1[:], a["moe_b1"].rearrange("l (g e) (m p) -> (l e m) g p", g=4, p=P)
                         ).then_inc(ld_b, 16)
            sp.dma_start(rows_b2[:], a["moe_b2"].rearrange("l (g e) (m p) -> (l e m) g p", g=2, p=P)
                         ).then_inc(ld_b, 16)
            sp.dma_start(C["rb"][:], a["router_b"].rearrange("l e -> e l"),
                         allow_slow_non_contiguous=True).then_inc(ld_b, 16)
            F.load_products(sp)
            F.load_compress(sp)
            sp.wait_ge(ld_b, 48)

        @block.gpsimd
        def _(pool):
            pool.memset(C["ident"][:], 0.0).then_inc(zeroed, 1)
            pool.memset(C["ident_b"][:], 0.0).then_inc(zeroed, 1)
            pool.memset(C["causal"][:], 0.0).then_inc(zeroed, 1)
            pool.memset(C["far"][:], 0.0).then_inc(zeroed, 1)
            pool.memset(C["cmp_mask"][:], 0.0).then_inc(zeroed, 1)
            pool.memset(C["before"][:], 1.0).then_inc(zeroed, 1)
            pool.memset(C["ones_b"][:], 1.0).then_inc(zeroed, 1)
            pool.memset(C["late"][:], 1.0).then_inc(zeroed, 1)
            for j, f in enumerate(frequencies()):
                pool.memset(freq[:, j:j + 1], f).then_inc(fr, 1)
            pool.wait_ge(zeroed, 8)
            for t in ("ident", "ident_b"):
                pool.affine_select(out=C[t][:], in_=C[t][:], compare_op=ALU.not_equal, fill=1.0, base=0,
                                   pattern=[[-1, P]], channel_multiplier=1).then_inc(masks, 1)
            pool.affine_select(out=C["causal"][:], in_=C["causal"][:], compare_op=ALU.is_ge, fill=NEG, base=0,
                               pattern=[[-1, P]], channel_multiplier=1).then_inc(masks, 1)
            pool.affine_select(out=C["far"][:], in_=C["far"][:], compare_op=ALU.is_gt, fill=NEG, base=0,
                               pattern=[[1, P]], channel_multiplier=-1).then_inc(masks, 1)
            pool.affine_select(out=C["cmp_mask"][:], in_=C["cmp_mask"][:], compare_op=ALU.is_ge, fill=NEG,
                               base=-(CMP_BLOCK - 1), pattern=[[P, NT], [-CMP_STRIDE, 64]],
                               channel_multiplier=1).then_inc(masks, 1)
            pool.affine_select(out=C["before"][:], in_=C["before"][:], compare_op=ALU.is_gt, fill=0.0, base=0,
                               pattern=[[1, P]], channel_multiplier=-1).then_inc(masks, 1)
            pool.affine_select(out=C["late"][:], in_=C["late"][:], compare_op=ALU.is_ge, fill=0.0,
                               base=-(CMP_BLOCK - 1), pattern=[[0, 1]], channel_multiplier=1).then_inc(masks, 1)
            pool.iota(C["iota_i"][:], [[1, CAP]], base=0, channel_multiplier=0).then_inc(masks, 1)
            pool.iota(C["iota_p_i"][:], [[0, 1]], base=0, channel_multiplier=1).then_inc(masks, 1)
            pool.iota(C["iota_t_i"][:], [[1, NT]], base=0, channel_multiplier=0).then_inc(masks, 1)
            pool.wait_ge(masks, 10)

        @block.tensor
        def _(pe):
            pe.wait_ge(masks, 10)
            pe.wait_ge(ld_rows, 64)
            pe.wait_ge(own, 1)
            nc.tensor.transpose(pS[0][:, 0, 0:19], rows[:], C["ident"][0:19, 0:19])
            nc.tensor.transpose(pS[0][:, 1, 0:NT], pos_r[:], C["ident"][0:NT, 0:NT]).then_inc(tr, 1)
            pe.wait_ge(ld_b, 48)
            for g in range(4):
                nc.tensor.transpose(pS[1][:, g, :], rows_b1[:, g, :], C["ident"][:])
            for g in range(2):
                last = nc.tensor.transpose(pS[2][:, g, :], rows_b2[:, g, :], C["ident"][:])
            last.then_inc(tr, 1)

        @block.vector
        def _(dve):
            S = Steps(own)
            dve.wait_ge(ld_pos, 16)
            S.mark(nc.vector.tensor_copy(pos_r[:], pos_i[:]))
            S.mark(nc.vector.memset(posp[:], 0.0))
            dve.wait_ge(ld_posc, 16)
            S.wait(dve)
            S.mark(nc.vector.tensor_copy(posp[0:N_CMP, NT:NT + 1], posc_i[:]))
            dve.wait_ge(tr, 1)
            S.mark(nc.vector.tensor_copy(C["vec"][:], pS[0][:, 0, 0:19]))
            S.mark(nc.vector.tensor_copy(posp[:, 0:NT], pS[0][:, 1, 0:NT]))
            dve.wait_ge(masks, 10)
            S.mark(nc.vector.tensor_copy(C["iota"][:], C["iota_i"][:]))
            S.mark(nc.vector.tensor_copy(C["iota_p"][:], C["iota_p_i"][:]))
            S.mark(nc.vector.tensor_copy(C["iota_t"][:], C["iota_t_i"][:]))
            dve.wait_ge(tr, 2)
            S.mark(nc.vector.tensor_copy(C["b1"][:], pS[1][:]))
            S.mark(nc.vector.tensor_copy(C["b2"][:], pS[2][:, 0:2, :]))
            dve.wait_ge(fr, NF)
            S.wait(dve)
            S.mark(nc.vector.tensor_tensor(ang[:], posp[:].unsqueeze(2).to_broadcast([P, NT + 1, NF]),
                                           freq[:].unsqueeze(1).to_broadcast([P, NT + 1, NF]), ALU.mult))
            S.wait(dve)
            S.mark(nc.vector.tensor_scalar(turns[:, 0], ang[:], 1.0 / TWO_PI, None, ALU.mult))
            S.mark(nc.vector.tensor_scalar(turns[:, 1], ang[:], 1.0 / TWO_PI, 0.25, ALU.mult, ALU.add))
            for k in (ROUND, -ROUND):
                S.wait(dve)
                S.mark(nc.vector.tensor_scalar(turns[:], turns[:], k, None, ALU.add))
            S.wait(dve)
            for j in range(2):
                S.mark(nc.vector.scalar_tensor_tensor(red[:, j], turns[:, j], -C1, ang[:], ALU.mult, ALU.add))
            for k in (C2, C3):
                S.wait(dve)
                S.mark(nc.vector.scalar_tensor_tensor(red[:], turns[:], -k, red[:], ALU.mult, ALU.add))
            S.wait(dve)
            S.mark(nc.vector.tensor_scalar(red[:, 1], red[:, 1], float(np.pi / 2), None, ALU.add))
            S.wait(dve)
            S.mark(nc.vector.tensor_scalar(red[:], red[:], PI_IN, -PI_IN, ALU.min, ALU.max))
            S.wait(dve)
            dve.sem_inc(table, 1)

        @block.scalar
        def _(act):
            act.wait_ge(table, 1)
            nc.scalar.activation(C["trig"][:], red[:], ACT.Sin).then_inc(ev, 1)
            act.wait_ge(ev, 1)


def rope(nc, dve, S, x, heads, r0, half, sin, cos, t1, t2):
    p = x.shape[0]
    n = p, heads, 2, half
    xr = x[:, :, r0:r0 + 2 * half].rearrange("p h (two f) -> p h two f", two=2)
    c = cos.unsqueeze(1).unsqueeze(1).to_broadcast([*n])
    s = sin.unsqueeze(1).to_broadcast([p, heads, half])
    S.wait(dve)
    S.mark(nc.vector.tensor_tensor(t1, xr, c, ALU.mult))
    S.mark(nc.vector.tensor_tensor(t2[:, :, 0, :], xr[:, :, 1, :], s, ALU.mult))
    S.mark(nc.vector.tensor_tensor(t2[:, :, 1, :], xr[:, :, 0, :], s, ALU.mult))
    S.wait(dve)
    S.mark(nc.vector.tensor_tensor(xr[:, :, 0, :], t1[:, :, 0, :], t2[:, :, 0, :], ALU.subtract))
    S.mark(nc.vector.tensor_tensor(xr[:, :, 1, :], t1[:, :, 1, :], t2[:, :, 1, :], ALU.add))


PROJ = ((C_Q, C_QN), (C_KC, C_KW), (C_KW, IN_COLS), (C_QN, C_KC))
PROJ_ACT, PROJ_DVE = 12, 14


def project(nc, C, R, F, a):
    with ExitStack() as ctx:
        M = Mem(nc, ctx, C["sems"])
        w_in, x_t, w_loaded, x_loaded, x_rows = F.w_in, F.x_t, F.w_loaded, F.x_loaded, F.x_rows
        xs = M.sb("xs", [P, D])
        junk = M.sb("junk", [P, D], BF16)
        uT = M.sb("uT", [P, KT, P])
        lat = M.sb("lat", [P, Q_RANK + KV_RANK])
        stage = M.sb("stage", [P, 12, DH])
        raw = M.sb("raw", [P, 4, 2, DH])
        ss, rec, rstd = M.sb("ss", [P, 1]), M.sb("rec", [P, 1]), M.sb("rstd", [P, 1])
        ss2, rec2, rstd2 = M.sb("ss2", [P, 2]), M.sb("rec2", [P, 2]), M.sb("rstd2", [P, 2])
        t1, t2 = M.sb("t1", [P, 12, 2, 8]), M.sb("t2", [P, 12, 2, 8])
        t3, t4 = M.sb("t3", [P, 1, 2, 16]), M.sb("t4", [P, 1, 2, 16])
        pe_t = M.sb("pe_t", [P, 1, ROPE])
        sig = M.sb("sig", [P, 1])
        pX = [M.ps(f"pX{i}", [P, 4, P]) for i in range(2)]
        pJ = [M.ps(f"pJ{i}", [P, 512]) for i in range(4)]
        pY = [M.ps(f"pY{i}", [P, 4, P]) for i in range(2)]
        xs_ready, x_turned, u_ready = (M.sem("p_" + s) for s in ("xs", "xt", "u"))
        sq_ready, rec_ready = M.sem("p_sq"), M.sem("p_rec")
        lsq_ready, lrec_ready = M.sem("p_lsq"), M.sem("p_lrec")
        product, copied, lat_ready, roped = (M.sem("p_" + s) for s in ("prod", "copied", "lat", "roped"))
        y_turned, y_dve, y_act = M.sem("p_yt"), M.sem("p_yd"), M.sem("p_ya")
        own_act, own_dve, passed = M.sem("p_oa"), M.sem("p_od"), M.sem("p_passed")
        zero, gates_ready = M.sem("p_zero"), M.sem("p_gates")
        block = ctx.enter_context(nc.Block())

        @block.sync
        def _(sp):
            with sp.Fori(1, NT) as t:
                sp.wait_ge(xs_ready, t)
                sp.dma_start(x_t[:], x_rows[bass.ds(t, 1)].rearrange("a p d -> (a p) d")).then_inc(x_loaded, 16)

        @block.gpsimd
        def _(pool):
            pool.memset(R["nsaT"][64:96, :, :], 0.0).then_inc(zero, 1)
            pool.wait_ge(zero, 1)

        @block.tensor
        def _(pe):
            def turn_x(t, first=False):
                pe.wait_ge(xs_ready, t + 1)
                if not first:
                    pe.wait_ge(u_ready, 2 * t)
                for k in range(KT):
                    last = nc.tensor.transpose(pX[k // 4][:, k % 4, :], xs[:, k * P:(k + 1) * P], C["ident"][:])
                    if k % 4 == 3:
                        last.then_inc(x_turned, 1)

            def products(t, first=False, final=False):
                for i, (c0, c1) in enumerate(PROJ):
                    if i == 3 and not final:
                        turn_x(t + 1)
                    if first:
                        pe.wait_ge(w_loaded[i], 16)
                    else:
                        pe.wait_ge(copied, 4 * t - 3 + i)
                    for k in range(KT):
                        if i == 0 and k % 4 == 0:
                            pe.wait_ge(u_ready, 2 * t + 1 + k // 4)
                        last = nc.tensor.matmul(pJ[i][:, 0:c1 - c0], uT[:, k, :], w_in[:, k, c0:c1],
                                                start=(k == 0), stop=(k == KT - 1))
                    last.then_inc(product, 1)
                    if i < 3 and not first:
                        turn_y(t - 1, ((0, 1), (2, 3), (4,))[i])

            def turn_y(t, groups):
                for g in groups:
                    if g == 0:
                        pe.wait_ge(lat_ready, t + 1)
                    if g == 1:
                        hold(pe, roped, t + 1, passed)
                    if g % 2 == 0:
                        hold(pe, y_dve, 3 * t + 1 + g // 2, passed)
                    else:
                        hold(pe, y_act, 2 * t + 1 + g // 2, passed)
                    for j in range(3 if g == 0 else 4):
                        if g == 0:
                            turned, of = pY[0][:, j, :], lat[:, j * P:(j + 1) * P]
                        elif g == 4:
                            turned, of = pY[0][:, j, :], raw[:, j].rearrange("p r d -> p (r d)")
                        else:
                            turned, of = pY[g % 2][0:DH, j, :], stage[:, 4 * g - 4 + j, :]
                        last = nc.tensor.transpose(turned, of, C["ident"][:])
                    last.then_inc(y_turned, 1)

            pe.sem_inc(y_dve, 1)
            pe.sem_inc(y_act, 1)
            turn_x(0, True)
            products(0, True)
            with pe.Fori(1, NT - 1) as t:
                products(t)
            products(NT - 1, final=True)
            turn_y(NT - 1, range(5))

        @block.scalar
        def _(act):
            def before(t, S, first=False):
                act.wait_ge(x_loaded, 16 * t + 16)
                nc.scalar.activation(junk[:], x_t[:], ACT.Square, accum_out=ss[:]).then_inc(sq_ready, 1)
                act.wait_ge(rec_ready, t + 1)
                S.mark(nc.scalar.activation(rstd[:], rec[:], ACT.Sqrt))
                if not first:
                    act.wait_ge(x_turned, 2 * t)
                S.wait(act)
                nc.scalar.activation(xs[:], x_t[:], ACT.Copy, scale=rstd[:]).then_inc(xs_ready, 1)

            def after(t, S, first=False):
                act.wait_ge(product, 4 * t + 1)
                if not first:
                    act.wait_ge(y_turned, 5 * t)
                S.mark(nc.scalar.activation(junk[:, 0:Q_RANK], pJ[0][:, 0:Q_RANK], ACT.Square,
                                            accum_out=ss2[:, 0:1]))
                S.wait(act)
                nc.scalar.activation(junk[:, 0:KV_RANK], pJ[0][:, C_KV:C_PE], ACT.Square,
                                     accum_out=ss2[:, 1:2]).then_inc(lsq_ready, 1)
                if not first:
                    act.wait_ge(roped, t)
                S.mark(nc.scalar.activation(pe_t[:, 0, :], pJ[0][:, C_PE:C_QN], ACT.Copy))
                act.wait_ge(lrec_ready, t + 1)
                S.mark(nc.scalar.activation(rstd2[:], rec2[:], ACT.Sqrt))
                S.wait(act)
                S.mark(nc.scalar.activation(lat[:, 0:Q_RANK], pJ[0][:, 0:Q_RANK], ACT.Copy, scale=rstd2[:, 0:1]))
                S.mark(nc.scalar.activation(lat[:, Q_RANK:], pJ[0][:, C_KV:C_PE], ACT.Copy, scale=rstd2[:, 1:2]))
                S.wait(act)
                act.sem_inc(lat_ready, 1)
                act.sem_inc(copied, 1)
                act.wait_ge(product, 4 * t + 2)
                S.mark(nc.scalar.activation(
                    raw[:], pJ[1][:, 0:2 * KVW].rearrange("p (j d) -> p j d", d=DH).unsqueeze(2)
                    .to_broadcast([P, 4, 2, DH]), ACT.Copy))
                S.mark(nc.scalar.activation(stage[:, 8:10, :].rearrange("p j d -> p (j d)"),
                                            pJ[1][:, 2 * KVW:3 * KVW], ACT.Copy))
                S.mark(nc.scalar.activation(R["v_s"][:, bass.ds(t, 1), :].rearrange("p a c -> p (a c)"),
                                            pJ[1][:, 3 * KVW:4 * KVW], ACT.Copy))
                S.wait(act)
                act.sem_inc(copied, 1)
                act.wait_ge(product, 4 * t + 3)
                S.mark(nc.scalar.activation(stage[:, 10:12, :].rearrange("p j d -> p (j d)"),
                                            pJ[2][:, 0:KVW], ACT.Copy))
                S.mark(nc.scalar.activation(R["v_w"][:, bass.ds(t, 1), :].rearrange("p a c -> p (a c)"),
                                            pJ[2][:, KVW:2 * KVW], ACT.Copy))
                S.mark(nc.scalar.activation(R["gates"][:, bass.ds(t, 1), :].rearrange("p a c -> p (a c)"),
                                            pJ[2][:, 2 * KVW:2 * KVW + 3 * H_NSA], ACT.Copy))
                S.wait(act)
                act.sem_inc(copied, 1)
                act.wait_ge(product, 4 * t + 4)
                nc.scalar.activation(stage[:, 0:8, :].rearrange("p j d -> p (j d)"), pJ[3][:], ACT.Copy
                                     ).then_inc(copied, 1)

            def from_y(t):
                for n, g in enumerate((0, 2)):
                    act.wait_ge(y_turned, 5 * t + 2 + 2 * n)
                    nc.scalar.activation(R["nsaT"][0:DH, 4 * g:4 * g + 4, bass.ds(t * P, P)],
                                         pY[1][0:DH], ACT.Copy).then_inc(y_act, 1)

            S = Steps(own_act)
            before(0, S, True)
            before(1, S)
            after(0, S, True)
            from_y(0)
            n0 = S.n
            with act.Fori(1, NT - 1) as t:
                S = Steps(own_act, (t - 1) * PROJ_ACT + n0)
                before(t + 1, S)
                after(t, S)
                from_y(t)
            assert S.n == PROJ_ACT, S.n
            S = Steps(own_act, (NT - 2) * PROJ_ACT + n0)
            after(NT - 1, S)
            from_y(NT - 1)
            S.wait(act)
            S.mark(nc.scalar.activation(R["gates"][:], R["gates"][:], ACT.Sigmoid))
            S.wait(act)
            nc.scalar.activation(R["gates"][:, 0, 0:3 * H_NSA:3], R["gates"][:, 0, 0:3 * H_NSA:3], ACT.Copy,
                                 scale=C["late"][:]).then_inc(gates_ready, 1)
            act.wait_ge(gates_ready, 1)

        @block.vector
        def _(dve):
            def reciprocal(S, out, x, n):
                S.mark(nc.vector.tensor_scalar(out, x, 1.0 / n, EPS, ALU.mult, ALU.add))
                S.wait(dve)
                return nc.vector.reciprocal(out, out)

            def before(t, S):
                dve.wait_ge(sq_ready, t + 1)
                reciprocal(S, rec[:], ss[:], D).then_inc(rec_ready, 1)

            def turned(t, first=False):
                for i in range(2):
                    dve.wait_ge(x_turned, 2 * t + 1 + i)
                    if i == 0 and not first:
                        dve.wait_ge(product, 4 * t)
                    nc.vector.tensor_tensor(uT[:, 4 * i:4 * i + 4, :], pX[i][:],
                                            C["vec"][:, 4 * i:4 * i + 4].unsqueeze(2).to_broadcast([P, 4, P]),
                                            ALU.mult).then_inc(u_ready, 1)

            def latents(t, S):
                dve.wait_ge(lsq_ready, t + 1)
                for i, n in enumerate((Q_RANK, KV_RANK)):
                    S.mark(nc.vector.tensor_scalar(rec2[:, i:i + 1], ss2[:, i:i + 1], 1.0 / n, EPS,
                                                   ALU.mult, ALU.add))
                S.wait(dve)
                nc.vector.reciprocal(rec2[:], rec2[:]).then_inc(lrec_ready, 1)
                dve.wait_ge(lat_ready, t + 1)
                sin, cos = (C["trig"][:, j, bass.ds(t, 1), :].rearrange("p a f -> p (a f)") for j in (0, 1))
                rope(nc, dve, S, pe_t[:], 1, 0, ROPE // 2, sin[:, 0:16], cos[:, 0:16], t3[:], t4[:])
                S.wait(dve)
                S.mark(nc.vector.tensor_copy(R["k_pe"][:, bass.ds(t, 1), :], pe_t[:]))

            def heads(t, S):
                sin, cos = (C["trig"][:, j, bass.ds(t, 1), :].rearrange("p a f -> p (a f)") for j in (0, 1))
                dve.wait_ge(copied, 4 * t + 4)
                rope(nc, dve, S, stage[:], 12, 0, ROPE_N // 2, sin[:, 16:24], cos[:, 16:24], t1[:], t2[:])
                S.wait(dve)
                dve.sem_inc(roped, 1)

            def early_y(t):
                dve.wait_ge(y_turned, 5 * t + 1)
                nc.vector.tensor_tensor(R["latT"][:, :, bass.ds(t * P, P)], pY[0][:, 0:3, :],
                                        C["vec"][:, 8:11].unsqueeze(2).to_broadcast([P, 3, P]),
                                        ALU.mult).then_inc(y_dve, 1)
                dve.wait_ge(y_turned, 5 * t + 3)
                nc.vector.tensor_copy(R["nsaT"][0:DH, 4:8, bass.ds(t * P, P)], pY[0][0:DH]).then_inc(y_dve, 1)

            def late_y(t):
                dve.wait_ge(y_turned, 5 * t + 5)
                nc.vector.tensor_copy(R["rawT"][:, :, bass.ds(t * P, P)], pY[0][:]).then_inc(y_dve, 1)

            def tile(t, S, last=False):
                latents(t, S)
                turned(t + 1)
                heads(t, S)
                early_y(t)
                if not last:
                    before(t + 2, S)
                late_y(t)

            S = Steps(own_dve)
            before(0, S)
            turned(0, True)
            before(1, S)
            tile(0, S)
            n0 = S.n
            with dve.Fori(1, NT - 2) as t:
                S = Steps(own_dve, (t - 1) * PROJ_DVE + n0)
                tile(t, S)
            assert S.n == PROJ_DVE, S.n
            S = Steps(own_dve, (NT - 3) * PROJ_DVE + n0)
            tile(NT - 2, S, True)
            latents(NT - 1, S)
            heads(NT - 1, S)
            early_y(NT - 1)
            late_y(NT - 1)


def compress(nc, C, R, F):
    LP = CMP_BLOCK // 2
    with ExitStack() as ctx:
        M = Mem(nc, ctx, C["sems"])
        w1, w2, pos = F.cmp_w1, F.cmp_w2, F.cmp_pos
        posT = M.sb("cposT", [P, 2, LP])
        blocks = M.sb("cblocks", [P, 2, LP, G_NSA, N_CMP])
        sg, hid = M.sb("csg", [P, 2, G_NSA * N_CMP]), M.sb("chid", [P, 2, G_NSA * N_CMP])
        kc = M.sb("ckc", [64, G_NSA, DH])
        t1, t2 = M.sb("ct1", [64, G_NSA, 2, 8]), M.sb("ct2", [64, G_NSA, 2, 8])
        pH = [M.ps(f"cpH{i}", [P, 512]) for i in range(2)]
        pO, pT = M.ps("cpO", [64, 4, DH]), M.ps("cpT", [P, 4, P])
        ld, ldp, turned, posT_ready = F.cmp_loaded, F.pos_loaded, M.sem("cc_turned"), M.sem("cc_posT")
        built, hid_ready, sg_ready, silu = M.sem("cc_built"), M.sem("cc_hid"), M.sem("cc_sg"), M.sem("cc_silu")
        out_ready, own, kc_ready, kc_turned = M.sem("cc_out"), M.sem("cc_own"), M.sem("cc_kc"), M.sem("cc_kct")
        zero, zero2 = M.sem("cc_zero"), M.sem("cc_zero2")
        block = ctx.enter_context(nc.Block())

        def windows(c, g):
            half = []
            for two in range(2):
                src = R["rawT"][64 * two:64 * two + 64, 2 * c + g, :]
                v = bass.AP(tensor=src.tensor, offset=src.offset + two,
                            ap=[list(src.ap[0]), [2, LP], [CMP_STRIDE, N_CMP]])
                half.append(v)
            return half

        def build(eng, c):
            for g in range(G_NSA):
                for two, v in enumerate(windows(c, g)):
                    h = slice(64 * two, 64 * two + 64)
                    eng.tensor_tensor(blocks[h, c, :, g, :], v,
                                      posT[h, c, :].unsqueeze(2).to_broadcast([64, LP, N_CMP]),
                                      ALU.add).then_inc(built, 1)

        @block.gpsimd
        def _(pool):
            for t in (kc, R["kcT"], R["v_c"]):
                pool.memset(t[:], 0.0).then_inc(zero, 1)
            pool.wait_ge(zero, 3)
            pool.sem_inc(zero2, 1)

        @block.vector
        def _(dve):
            S = Steps(own)
            dve.wait_ge(turned, 1)
            nc.vector.tensor_copy(posT[:], pT[:, 0, 0:2 * LP].rearrange("p (c l) -> p c l", c=2)
                                  ).then_inc(posT_ready, 1)
            dve.wait_ge(posT_ready, 1)
            build(nc.vector, 0)
            build(nc.vector, 1)
            for c in range(2):
                dve.wait_ge(sg_ready, c + 1)
                nc.vector.tensor_tensor(hid[:, c, :], pH[c][:, 0:G_NSA * N_CMP], sg[:, c, :], ALU.mult
                                        ).then_inc(silu, 1)
            dve.wait_ge(zero2, 1)
            dve.wait_ge(out_ready, 1)
            S.mark(nc.vector.tensor_copy(kc[0:N_CMP], pO[0:N_CMP, 0:2, :]))
            rope(nc, dve, S, kc[0:N_CMP], G_NSA, 0, ROPE_N // 2, C["trig"][0:N_CMP, 0, NT, 16:24],
                 C["trig"][0:N_CMP, 1, NT, 16:24], t1[0:N_CMP], t2[0:N_CMP])
            S.wait(dve)
            nc.vector.tensor_copy(R["v_c"][0:N_CMP], pO[0:N_CMP, 2:4, :]).then_inc(kc_ready, 1)
            dve.wait_ge(kc_turned, 1)
            nc.vector.tensor_copy(R["kcT"][0:DH], pT[0:DH, 1:3, 0:64]).then_inc(kc_ready, 1)
            dve.wait_ge(kc_ready, 2)

        @block.scalar
        def _(act):
            for c in range(2):
                act.wait_ge(hid_ready, c + 1)
                nc.scalar.activation(sg[:, c, :], pH[c][:, 0:G_NSA * N_CMP], ACT.Sigmoid).then_inc(sg_ready, 1)

        @block.tensor
        def _(pe):
            pe.wait_ge(ldp, 16)
            nc.tensor.transpose(pT[:, 0, 0:2 * LP], pos[:], C["ident"][0:2 * LP, 0:2 * LP]).then_inc(turned, 1)
            pe.wait_ge(ld, 48)
            for c in range(2):
                pe.wait_ge(built, 4 * c + 4)
                for lp in range(LP):
                    last = nc.tensor.matmul(pH[c][:, 0:G_NSA * N_CMP], w1[:, c, lp, :],
                                            blocks[:, c, lp].rearrange("p g n -> p (g n)"),
                                            start=(lp == 0), stop=(lp == LP - 1))
                last.then_inc(hid_ready, 1)
            pe.wait_ge(silu, 2)
            for c in range(2):
                for g in range(G_NSA):
                    last = nc.tensor.matmul(pO[0:N_CMP, 2 * c + g, :], hid[:, c, g * N_CMP:(g + 1) * N_CMP],
                                            w2[:, c, :], start=True, stop=True)
            last.then_inc(out_ready, 1)
            pe.wait_ge(kc_ready, 1)
            for g in range(G_NSA):
                last = nc.tensor.transpose(pT[0:DH, 1 + g, 0:64], kc[:, g, :], C["ident"][0:64, 0:64])
            last.then_inc(kc_turned, 1)


QG = 4
LAG = 3


class Unit:

    def __init__(self, kind, pair, qg, head, i):
        self.kind, self.pair, self.qg, self.head, self.i = kind, pair, qg, head, i
        if kind == "win":
            self.k0 = max(0, i - WT)
            w = (i + 1 - self.k0) * P
            self.spans = [(0, w, 0), ((WT + 1) * P, (WT + 1) * P + 64, 1)]
            pieces = [(P * j, P, self.k0 + j) for j in range(i + 1 - self.k0)] + [((WT + 1) * P, 64, None)]
        else:
            self.k0 = 0
            w = (i + 1) * P
            self.spans = [(0, w, 0)]
            pieces = [(P * j, P, j) for j in range(i + 1)]
        self.width = w
        self.banks = [pieces[j:j + 4] for j in range(0, len(pieces), 4)]


def plan(kinds, pairs):
    units, first, groups = [], [], []
    for pair in range(pairs):
        for qg in range(NT // QG):
            for kind in kinds:
                for i in range(QG * qg, QG * qg + QG):
                    for head in range(2):
                        first.append(sum(len(u.banks) for u in units))
                        units.append(Unit(kind, pair, qg, head, i))
                groups.append((len(units) - 1, kind, pair, qg))
    return units, first, groups


def value_tiles(kind, qg):
    q0, q1 = QG * qg, QG * qg + QG
    if kind == "win":
        return [(k, max(k, q0), min(k + WT + 1, q1)) for k in range(max(0, q0 - WT), q1)]
    return [(k, max(k, q0), q1) for k in range(q1)]


class Attention:

    def __init__(self, nc, M, C, R, name, kinds, pairs, prep, gated):
        self.nc, self.C, self.R, self.kinds, self.gated = nc, C, R, kinds, gated
        self.units, self.first, self.groups = plan(kinds, pairs)
        self.OUTS = 2 * pairs
        self.U, self.NG = len(self.units), len(self.groups)
        self.prep = prep
        banks = prep + sum(len(u.banks) for u in self.units)
        assert banks % 2 == 0 and self.U % 4 == 0 and prep % 2 == 0
        self.half = banks // 2
        self.probs = M.sb(name + "probs", [P, 4, SEQ])
        self.probsT = M.sb(name + "probsT", [P, 2, NT, QG * P])
        self.negmax = M.sb(name + "negmax", [P, 4, 2])
        self.sums = M.sb(name + "sums", [P, 4, 2])
        self.weight = M.sb(name + "weight", [P, 4, 2])
        self.pS = [M.ps(f"{name}pS{i}", [P, SEQ]) for i in range(2)]
        self.pT = [M.ps(f"{name}pT{i}", [P, 4, P]) for i in range(2)]
        self.pO = [M.ps(f"{name}pO{i}", [P, QG * P]) for i in range(2)]
        s = lambda x: M.sem(name + x)
        self.staged = s("staged")
        self.scored, self.maxed, self.exped, self.inverted = s("scored"), s("maxed"), s("exped"), s("inv")
        self.scaled = s("scaled")
        self.bank_turned = [s("bt0"), s("bt1")]
        self.bank_read = [s("br0"), s("br1")]
        self.valued, self.out_read = s("valued"), s("outd")
        self.passed = s("passed")

    FREE_BANK, FREE_SCORES, FREE_OUT, FREE_VALUED, NO_BANK = 1, 2, 2, 1, 1

    def start(self, pe):
        for b in range(2):
            pe.sem_inc(self.bank_read[b], self.FREE_BANK)
            pe.sem_inc(self.bank_turned[b], self.NO_BANK)
        pe.sem_inc(self.exped, self.FREE_SCORES)
        pe.sem_inc(self.out_read, self.FREE_OUT)
        pe.sem_inc(self.valued, self.FREE_VALUED)

    def wait_bank(self, pe, it, seq):
        pe.wait_ge(self.bank_read[seq % 2], it * self.half + seq // 2 + self.FREE_BANK)

    def wait_turned(self, eng, it, seq):
        eng.wait_ge(self.bank_turned[seq % 2], it * self.half + seq // 2 + 1 + self.NO_BANK)

    def scores(self, pe, it, n):
        nc, C, u, pS = self.nc, self.C, self.units[n], self.pS[n % 2]
        pe.wait_ge(self.exped, it * self.U + n + 1)
        q = self.queries(u)
        for c0 in range(0, u.width, 512):
            c1 = min(c0 + 512, u.width)
            diag = u.width - P >= c0 and u.width - P < c1
            far = u.kind == "win" and u.i >= WT and c0 == 0
            nc.tensor.matmul(pS[:, c0:c1], q, self.keys(u, u.k0 * P + c0, u.k0 * P + c1), start=True,
                             stop=not (diag or far))
            if far:
                nc.tensor.matmul(pS[:, 0:P], C["ident_b"][:], C["far"][:], start=False, stop=not diag)
            if diag:
                last = nc.tensor.matmul(pS[:, u.width - P:u.width], C["ident_b"][:], C["causal"][:],
                                        start=False, stop=True)
        if u.kind == "win":
            c0 = (WT + 1) * P
            nc.tensor.matmul(pS[:, c0:c0 + 64], q, self.keys(u, None, None), start=True, stop=False)
            last = nc.tensor.matmul(pS[:, c0:c0 + 64], C["ident_b"][:], C["cmp_mask"][:, u.i, :],
                                    start=False, stop=True)
        last.then_inc(self.scored, 1)

    def turn(self, pe, it, n):
        nc, u = self.nc, self.units[n]
        pe.wait_ge(self.scaled, it * self.U + n + 1)
        for j, pieces in enumerate(u.banks):
            seq = self.prep + self.first[n] + j
            self.wait_bank(pe, it, seq)
            if pieces[0][1] != P:
                pe.sem_inc(self.passed, 1)
            for k, (col, rows, _) in enumerate(pieces):
                last = nc.tensor.transpose(self.pT[seq % 2][0:rows, k, :], self.probs[:, n % 4, col:col + rows],
                                           self.C["ident"][:])
            last.then_inc(self.bank_turned[seq % 2], 1)

    def values(self, pe, it, g):
        nc, (n, kind, pair, qg) = self.nc, self.groups[g]
        opening, closing = kind == self.kinds[0], kind == self.kinds[-1]
        seqs = self.prep + self.first[n] + len(self.units[n].banks)
        for b in range(2):
            pe.wait_ge(self.bank_read[b], it * self.half + (seqs + 1 - b) // 2 + self.FREE_BANK)
        if opening:
            pe.wait_ge(self.out_read, self.OUTS * it + 2 * pair + qg - 1 + self.FREE_OUT)
        tiles = value_tiles(kind, qg)
        for j, (k, i0, i1) in enumerate(tiles):
            c0, c1 = (i0 - QG * qg) * P, (i1 - QG * qg) * P
            end = closing and kind != "win" and j == len(tiles) - 1
            for h in range(2):
                last = nc.tensor.matmul(self.pO[qg][64 * h:64 * h + 64, c0:c1], self.value(kind, k, h),
                                        self.probsT[:, h, k, c0:c1], start=opening and j == 0, stop=end)
        if kind == "win":
            for h in range(2):
                last = nc.tensor.matmul(self.pO[qg][64 * h:64 * h + 64, :], self.value("cmp", 0, h),
                                        self.cmpT[:, h, :], start=False, stop=True)
        last.then_inc(self.valued, 1)

    def tensor(self, pe, it):
        for s in range(self.U + LAG + 1):
            if LAG <= s < self.U + LAG:
                self.turn(pe, it, s - LAG)
            if s < self.U:
                self.scores(pe, it, s)
            for g, (n, *_) in enumerate(self.groups):
                if n == s - LAG - 1:
                    self.values(pe, it, g)

    def read_banks(self, eng, copy, it, n, parity):
        u = self.units[n]
        group = next(g for g, (m, *_) in enumerate(self.groups) if n <= m)
        for j, pieces in enumerate(u.banks):
            seq = self.prep + self.first[n] + j
            if seq % 2 != parity:
                continue
            eng.wait_ge(self.valued, it * self.NG + group + self.FREE_VALUED)
            self.wait_turned(eng, it, seq)
            c = (u.i % QG) * P
            full = [x for x in pieces if x[1] == P]
            k0 = full[0][2] if full else 0
            if full:
                last = copy(self.probsT[:, u.head, k0:k0 + len(full), c:c + P], self.pT[seq % 2][:, 0:len(full), :])
            if len(full) < len(pieces):
                last = copy(self.cmpT[0:64, u.head, c:c + P], self.pT[seq % 2][0:64, len(full), :])
            last.then_inc(self.bank_read[seq % 2], 1)

    def scalar(self, act, it, out_tile):
        nc = self.nc
        for s in range(self.U + LAG + 2):
            if LAG <= s < self.U + LAG:
                self.read_banks(act, nc.scalar.copy, it, s - LAG, 0)
            for g, (n, kind, pair, qg) in enumerate(self.groups):
                if n == s - LAG - 2 and kind == self.kinds[-1]:
                    act.wait_ge(self.valued, it * self.NG + g + 1 + self.FREE_VALUED)
                    nc.scalar.copy(out_tile(pair)[:, :, qg * QG * P:(qg + 1) * QG * P].rearrange("p a q -> p (a q)"),
                                   self.pO[qg][:]).then_inc(self.out_read, 1)
            if s < self.U:
                act.wait_ge(self.maxed, it * self.U + s + 1)
                if s >= 4:
                    self.wait_turned(act, it, self.prep + self.first[s - 4] + len(self.units[s - 4].banks) - 1)
                else:
                    for b in range(2):
                        act.wait_ge(self.bank_turned[b], it * self.half + self.NO_BANK)
                for c0, c1, k in self.units[s].spans:
                    last = nc.scalar.activation(self.probs[:, s % 4, c0:c1], self.pS[s % 2][:, c0:c1], ACT.Exp,
                                                bias=self.negmax[:, s % 4, k:k + 1],
                                                accum_out=self.sums[:, s % 4, k:k + 1])
                last.then_inc(self.exped, 1)

    def vector(self, dve, it):
        nc = self.nc
        for s in range(self.U + LAG):
            if s >= LAG:
                self.read_banks(dve, nc.vector.tensor_copy, it, s - LAG, 1)
            if s < self.U:
                dve.wait_ge(self.scored, it * self.U + s + 1)
                for c0, c1, k in self.units[s].spans:
                    last = nc.vector.tensor_reduce(self.negmax[:, s % 4, k:k + 1], self.pS[s % 2][:, c0:c1],
                                                   AX_X, ALU.max, negate=True)
                last.then_inc(self.maxed, 1)
            if 1 <= s <= self.U:
                n = s - 1
                u, w = self.units[n], self.weight[:, n % 4, 0:len(self.units[n].spans)]
                dve.wait_ge(self.exped, it * self.U + n + 1 + self.FREE_SCORES)
                nc.vector.reciprocal(w, self.sums[:, n % 4, 0:len(u.spans)]).then_inc(self.inverted, 1)
                if self.gated:
                    dve.wait_ge(self.inverted, 2 * (it * self.U + n) + 1)
                    gate = [1] if u.kind == "sel" else [2, 0]
                    for k, br in enumerate(gate):
                        last = nc.vector.tensor_tensor(w[:, k:k + 1], w[:, k:k + 1],
                                                       self.gate(u, br), ALU.mult)
                    last.then_inc(self.inverted, 1)
                    dve.wait_ge(self.inverted, 2 * (it * self.U + n) + 2)
                else:
                    dve.wait_ge(self.inverted, it * self.U + n + 1)
                for c0, c1, k in u.spans:
                    last = nc.vector.tensor_scalar(self.probs[:, n % 4, c0:c1], self.probs[:, n % 4, c0:c1],
                                                   w[:, k:k + 1], None, ALU.mult)
                last.then_inc(self.scaled, 1)


def mla(nc, C, R, a):
    scale = QK_MLA ** -0.5
    ROPES = 5
    with ExitStack() as ctx:
        M = Mem(nc, ctx, C["sems"])
        A = Attention(nc, M, C, R, "m_", ("mla",), 1, NT, False)
        wq = M.sb("m_wq", [P, Q_RANK // P, 2 * QK_MLA])
        wkv = M.sb("m_wkv", [P, 2 * (NOPE + V_DIM)])
        stage = M.sb("m_stage", [P, 2, 4, QK_MLA])
        qkT = M.sb("m_qkT", [QK_MLA, 4, SEQ])
        v = M.sb("m_v", [P, NT, 2, V_DIM])
        t1, t2 = M.sb("m_t1", [P, 2, 2, 16]), M.sb("m_t2", [P, 2, 2, 16])
        loaded, product, copied, roped, own = (M.sem("m_" + s) for s in ("ld", "prod", "copied", "roped", "own"))
        A.queries = lambda u: qkT[:, u.head, u.i * P:(u.i + 1) * P]
        A.keys = lambda u, c0, c1: qkT[:, 2 + u.head, c0:c1]
        A.value = lambda kind, k, h: v[:, k, h, :]
        PAIRS = H_MLA // 2
        block = ctx.enter_context(nc.Block())

        @block.sync
        def _(sp):
            def load(it):
                sp.dma_start(wq[:], a["mla_w_q_up"].rearrange("l (k p) (a c) -> (l p) k a c", p=P, a=PAIRS)
                             [:, :, bass.ds(it, 1), :].rearrange("p k a c -> p k (a c)")).then_inc(loaded, 16)
                sp.dma_start(wkv[:], a["mla_w_kv_up"].rearrange("l p (a c) -> (l p) a c", a=PAIRS)
                             [:, bass.ds(it, 1), :].rearrange("p a c -> p (a c)")).then_inc(loaded, 16)
            load(0)
            with sp.Fori(1, PAIRS) as it:
                sp.wait_ge(product, NT * it)
                load(it)

        @block.tensor
        def _(pe):
            A.start(pe)
            pe.sem_inc(copied, 1)
            with pe.Fori(0, PAIRS) as it:
                pe.wait_ge(loaded, 32 * it + 32)
                pe.wait_ge(A.exped, it * A.U + A.FREE_SCORES)
                for j in range(NT + 1):
                    if j < NT:
                        b = A.pS[j % 2]
                        pe.wait_ge(copied, NT * it + max(j - 1, 0) + 1)
                        for k in range(Q_RANK // P):
                            nc.tensor.matmul(b[:, 0:2 * QK_MLA], R["latT"][:, k, j * P:(j + 1) * P], wq[:, k, :],
                                             start=(k == 0), stop=(k == Q_RANK // P - 1))
                        nc.tensor.matmul(b[:, 512:768], R["latT"][:, 2, j * P:(j + 1) * P], wkv[:],
                                         start=True, stop=True).then_inc(product, 1)
                    if j >= 1:
                        pe.wait_ge(roped, NT * it + j)
                        A.wait_bank(pe, it, j - 1)
                        for k in range(4):
                            last = nc.tensor.transpose(A.pT[(j - 1) % 2][0:QK_MLA, k, :], stage[:, (j - 1) % 2, k, :],
                                                       C["ident"][:])
                        last.then_inc(A.bank_turned[(j - 1) % 2], 1)
                for b in range(2):
                    pe.wait_ge(A.bank_read[b], it * A.half + NT // 2 + A.FREE_BANK)
                A.tensor(pe, it)

        @block.scalar
        def _(act):
            with act.Fori(0, PAIRS) as it:
                for j in range(NT):
                    b = A.pS[j % 2]
                    act.wait_ge(product, NT * it + j + 1)
                    if j >= 2:
                        A.wait_turned(act, it, j - 2)
                    nc.scalar.activation(stage[:, j % 2, 0:2, :].rearrange("p h c -> p (h c)"), b[:, 0:2 * QK_MLA],
                                         ACT.Copy, scale=scale).then_inc(copied, 1)
                    if j % 2 == 0 and j >= 2:
                        A.wait_turned(act, it, j - 2)
                        nc.scalar.copy(qkT[:, :, (j - 2) * P:(j - 1) * P], A.pT[0][0:QK_MLA]).then_inc(A.bank_read[0], 1)
                A.wait_turned(act, it, NT - 2)
                nc.scalar.copy(qkT[:, :, (NT - 2) * P:(NT - 1) * P], A.pT[0][0:QK_MLA]).then_inc(A.bank_read[0], 1)
                A.scalar(act, it, lambda pair: R["mixT"][:, bass.ds(it, 1), :])

        @block.vector
        def _(dve):
            with dve.Fori(0, PAIRS) as it:
                S = Steps(own, it * ROPES * NT)
                for j in range(NT):
                    b = A.pS[j % 2]
                    dve.wait_ge(product, NT * it + j + 1)
                    if j >= 2:
                        A.wait_turned(dve, it, j - 2)
                    nc.vector.tensor_copy(stage[:, j % 2, 2:4, 0:NOPE],
                                          b[:, 512:768].rearrange("p (h c) -> p h c", h=2)[:, :, 0:NOPE])
                    nc.vector.tensor_copy(v[:, j], b[:, 512:768].rearrange("p (h c) -> p h c", h=2)[:, :, NOPE:])
                    nc.vector.tensor_copy(stage[:, j % 2, 2:4, NOPE:],
                                          R["k_pe"][:, j:j + 1, :].to_broadcast([P, 2, ROPE]))
                    dve.wait_ge(copied, NT * it + j + 2)
                    rope(nc, dve, S, stage[:, j % 2, 0:2, :], 2, NOPE, ROPE // 2, C["trig"][:, 0, j, 0:16],
                         C["trig"][:, 1, j, 0:16], t1[:], t2[:])
                    S.wait(dve)
                    dve.sem_inc(roped, 1)
                    if j % 2 == 1 and j >= 3:
                        A.wait_turned(dve, it, j - 2)
                        nc.vector.tensor_copy(qkT[:, :, (j - 2) * P:(j - 1) * P], A.pT[1][0:QK_MLA]
                                              ).then_inc(A.bank_read[1], 1)
                assert S.n == ROPES * NT
                A.wait_turned(dve, it, NT - 1)
                nc.vector.tensor_copy(qkT[:, :, (NT - 1) * P:], A.pT[1][0:QK_MLA]).then_inc(A.bank_read[1], 1)
                A.vector(dve, it)


def nsa(nc, C, R):
    PER_G = H_NSA // G_NSA // 2
    with ExitStack() as ctx:
        M = Mem(nc, ctx, C["sems"])
        A = Attention(nc, M, C, R, "n_", ("sel", "win"), PER_G, 0, True)
        A.cmpT = M.sb("n_cmpT", [P, 2, QG * P])
        q = M.sb("n_q", [96, 2 * PER_G, SEQ])
        k = M.sb("n_k", [96, 2, SEQ])
        kc = M.sb("n_kc", [96, 64])
        v = M.sb("n_v", [P, 2, NT, DH])
        vc = M.sb("n_vc", [P, DH])
        gp = M.sb("n_g", [P, NT, 6 * PER_G])
        q_staged, k_staged, v_staged, g_staged, zero, copied, passed = (
            M.sem("n_" + s) for s in ("q", "k", "v", "g", "z", "copied", "n_passed"))
        A.queries = lambda u: q[:, 2 * u.pair + u.head, u.i * P:(u.i + 1) * P]
        A.keys = lambda u, c0, c1: kc[:] if c0 is None else k[:, 0 if u.kind == "sel" else 1, c0:c1]
        A.value = lambda kind, t, h: vc[:] if kind == "cmp" else v[:, 0 if kind == "sel" else 1, t, :]
        A.gate = lambda u, br: gp[:, u.i, 6 * u.pair + 3 * u.head + br:6 * u.pair + 3 * u.head + br + 1]
        block = ctx.enter_context(nc.Block())

        @block.gpsimd
        def _(pool):
            pool.memset(A.cmpT[64:128], 0.0).then_inc(zero, 1)
            pool.wait_ge(zero, 1)
            pool.memset(vc[64:128], 0.0).then_inc(zero, 1)
            pool.wait_ge(zero, 2)
            with pool.Fori(0, G_NSA) as g:
                pool.wait_ge(A.valued, g * A.NG + A.FREE_VALUED)
                pool.tensor_copy(v[:, 0], R["v_s"][:, :, bass.ds(g * DH, DH)]).then_inc(copied, 1)
                pool.wait_ge(copied, 2 * g + 1)
                pool.tensor_copy(v[:, 1], R["v_w"][:, :, bass.ds(g * DH, DH)]).then_inc(copied, 1)
                pool.wait_ge(copied, 2 * g + 2)
                pool.tensor_copy(vc[0:64].rearrange("p (a d) -> p a d", a=1), R["v_c"][:, bass.ds(g, 1), :]
                                 ).then_inc(v_staged, 1)

        @block.tensor
        def _(pe):
            A.start(pe)
            pe.wait_ge(zero, 2)
            with pe.Fori(0, G_NSA) as g:
                pe.wait_ge(k_staged, g + 1)
                pe.wait_ge(v_staged, g + 1)
                hold(pe, q_staged, g + 1, passed)
                A.tensor(pe, g)

        @block.scalar
        def _(act):
            with act.Fori(0, G_NSA) as g:
                act.wait_ge(A.valued, g * A.NG + A.FREE_VALUED)
                for h in range(2 * PER_G):
                    last = nc.scalar.activation(q[:, h:h + 1, :], R["nsaT"][:, bass.ds(2 * PER_G * g + h, 1), :],
                                                ACT.Copy, scale=DH ** -0.5)
                last.then_inc(q_staged, 1)
                A.scalar(act, g, lambda pair: R["mixT"][:, bass.ds(PER_G * g + pair + H_MLA // 2, 1), :])

        @block.vector
        def _(dve):
            with dve.Fori(0, G_NSA) as g:
                dve.wait_ge(A.valued, g * A.NG + A.FREE_VALUED)
                nc.vector.tensor_copy(k[:, 0:1, :], R["nsaT"][:, bass.ds(g + 8, 1), :])
                nc.vector.tensor_copy(k[:, 1:2, :], R["nsaT"][:, bass.ds(g + 10, 1), :])
                nc.vector.tensor_copy(kc[:].rearrange("p (a n) -> p a n", a=1), R["kcT"][:, bass.ds(g, 1), :]
                                      ).then_inc(k_staged, 1)
                nc.vector.tensor_copy(gp[:], R["gates"][:, :, bass.ds(g * (6 * PER_G), 6 * PER_G)]).then_inc(g_staged, 1)
                dve.wait_ge(g_staged, g + 1)
                A.vector(dve, g)


def route(nc, C, R, W, a):
    with ExitStack() as ctx:
        M = Mem(nc, ctx, C["sems"])
        w_out = M.sb("r_wout", [P, KT, D])
        rw = M.sb("r_rw", [P, KT, NE])
        g_ffn = M.sb("r_gffn", [P, D])
        mix = M.sb("r_mix", [P, KT, P])
        x_t, h_t, hn_t = M.sb("r_x", [P, D]), M.sb("r_h", [P, D]), M.sb("r_hn", [P, D])
        junk = M.sb("r_junk", [P, D], BF16)
        hnT = M.sb("r_hnT", [P, KT, P])
        lgT = M.sb("r_lgT", [NE, P])
        lg_t, top_t, top_i = M.sb("r_lgt", [P, NE]), M.sb("r_top", [P, 8]), M.sb("r_topi", [P, 8], U32)
        top_f, hot = M.sb("r_topf", [P, TOPK]), M.sb("r_hot", [P, TOPK, NE])
        lg = M.sb("r_lg", [P, NT, NE])
        took, took_b = M.sb("r_took", [P, NT, NE]), M.sb("r_tookb", [P, NT, NE], BF16)
        ss, rec, rstd = M.sb("r_ss", [P, 1]), M.sb("r_rec", [P, 1]), M.sb("r_rstd", [P, 1])
        se = M.sb("r_se", [P, NT])
        more, cum2 = M.sb("r_more", [P, NE]), M.sb("r_cum2", [P, NE])
        cnt, cum = W.cnt, W.cum
        zeros = w_out[:, 1, :]
        rest = w_out[:, 2, 0:NT * NE].rearrange("p (t e) -> p t e", t=NT)
        pM = M.ps("r_pM", [P, D])
        pX = [M.ps(f"r_pX{i}", [P, 4, P]) for i in range(2)]
        pR, pL = M.ps("r_pR", [NE, P]), M.ps("r_pL", [P, NE])
        pP, pC = M.ps("r_pP", [P, NT, NE]), M.ps("r_pC", [P, NE])
        s = lambda x: M.sem("r_" + x)
        wld = [s(f"wld{i}") for i in range(KT // 2)]
        rld, x_in, mixed, product = s("rld"), s("xin"), s("mixed"), s("prod")
        summed, sq, rec_r, rstd_r, normed = s("sum"), s("sq"), s("rec"), s("rstd"), s("norm")
        h_out, hn_out, turned, x0_read, x1_read = s("hout"), s("hnout"), s("turned"), s("x0"), s("x1")
        lt, lt_ready, l_turned, l_read = s("lt"), s("ltr"), s("lturn"), s("lread")
        zero, z_out, own, e_in, e_out, took_r, posd = s("z"), s("zout"), s("own"), s("ein"), s("eout"), s("took"), s("pos")
        passed, known = s("passed"), s("known")
        block = ctx.enter_context(nc.Block())
        x_rows = a["x"].rearrange("b (t p) d -> (b t) p d", p=P)
        tiles = lambda dram: dram[0:SEQ].rearrange("(t p) d -> t p d", p=P)
        one_of = lambda v, t: v[bass.ds(t, 1)].rearrange("a p d -> (a p) d")

        @block.sync
        def _(sp):
            w_rows = a["w_out"].rearrange("l (k p) d -> (l p) k d", p=P)
            for i in range(KT // 2):
                sp.dma_start(w_out[:, 2 * i:2 * i + 2], w_rows[:, 2 * i:2 * i + 2]).then_inc(wld[i], 16)
                if i == 0:
                    sp.dma_start(x_t[:], x_rows[0]).then_inc(x_in, 16)
            sp.dma_start(rw[:], a["router_w"].rearrange("l (k p) e -> (l p) k e", p=P)).then_inc(rld, 16)
            sp.dma_start(g_ffn[:], a["ffn_norm"].to_broadcast([P, D])).then_inc(rld, 16)
            for t in range(1, NT):
                sp.wait_ge(summed, 2 * t)
                sp.dma_start(x_t[:], x_rows[t]).then_inc(x_in, 16)
                W.load(sp, 0, first=True, chunks=range(2 * t - 2, min(2 * t, FC + DC)))

        @block.gpsimd
        def _(pool):
            def stage(t, h):
                pool.tensor_copy(mix[:, 4 * h:4 * h + 4], R["mixT"][:, 4 * h:4 * h + 4, bass.ds(t * P, P)]
                                 ).then_inc(mixed, 1)
                pool.wait_ge(mixed, 2 * t + h + 1)
            stage(0, 0)
            stage(0, 1)
            for c, src in ((0, C["iota_p"][:].unsqueeze(2)), (1, C["iota_t"][:].unsqueeze(2)), (2, C["ones_b"][:, 0:1].unsqueeze(2))):
                pool.tensor_copy(W.facts[:, :, :, c], src.to_broadcast([P, NT, NE])).then_inc(known, 1)
                pool.wait_ge(known, c + 1)
            with pool.Fori(1, NT) as t:
                for h in range(2):
                    pool.wait_ge(product, 3 * t - 2 + 2 * h)
                    stage(t, h)

        @block.tensor
        def _(pe):
            def products(t, ks, first=False):
                if ks[0] == 0:
                    pe.wait_ge(mixed, 2 * t + 1)
                    if not first:
                        pe.wait_ge(summed, 2 * t)
                if ks[0] == 4:
                    pe.wait_ge(mixed, 2 * t + 2)
                steps = [(k, i) for k in ks for i in range(2)]
                if ks[0] == 6:
                    steps.sort(key=lambda s: s[1])
                for k, i in steps:
                    if first and i == 0 and k % 2 == 0:
                        pe.wait_ge(wld[k // 2], 16)
                    last = nc.tensor.matmul(pM[:, i * 512:(i + 1) * 512], mix[:, k, :],
                                            w_out[:, k, i * 512:(i + 1) * 512], start=(k == 0), stop=(k == KT - 1))
                    if k == KT - 1 or (k, i) == (3, 1):
                        last.then_inc(product, 1)

            def turn(t):
                pe.wait_ge(normed, t + 1)
                for k in range(KT):
                    if k == 0:
                        pe.wait_ge(x0_read, t + 1)
                    if k == 4:
                        pe.wait_ge(x1_read, t + 1)
                    last = nc.tensor.transpose(pX[k // 4][:, k % 4, :], hn_t[:, k * P:(k + 1) * P], C["ident"][:])
                    if k % 4 == 3:
                        last.then_inc(turned, 1)

            def router(t):
                pe.wait_ge(x0_read, t + 2)
                pe.wait_ge(x1_read, t + 2)
                for k in range(KT):
                    last = nc.tensor.matmul(pR[:], rw[:, k, :], hnT[:, k, :], start=(k == 0), stop=(k == KT - 1))
                last.then_inc(lt, 1)

            def turn_logits(t):
                pe.wait_ge(lt_ready, t + 1)
                hold(pe, l_read, t + 1, passed)
                nc.tensor.transpose(pL[:], lgT[:], C["ident"][0:NE, 0:NE]).then_inc(l_turned, 1)

            for q in (x0_read, x1_read, l_read):
                pe.sem_inc(q, 1)
            products(0, (0, 1, 2, 3), True)
            products(0, (4, 5), True)
            products(0, (6, 7), True)
            pe.wait_ge(rld, 32)
            with pe.Fori(1, NT) as t:
                products(t, (0, 1, 2, 3))
                turn(t - 1)
                products(t, (4, 5))
                router(t - 1)
                products(t, (6, 7))
                turn_logits(t - 1)
            turn(NT - 1)
            router(NT - 1)
            turn_logits(NT - 1)
            pe.wait_ge(took_r, 1)
            for j in range(NT):
                nc.tensor.matmul(pC[:], C["ones_b"][:], took_b[:, j, :], start=(j == 0), stop=(j == NT - 1))
            for t in range(NT):
                for j in range(t):
                    nc.tensor.matmul(pP[:, t, :], C["ones_b"][:], took_b[:, j, :], start=(j == 0), stop=False)
                last = nc.tensor.matmul(pP[:, t, :], C["before"][:], took_b[:, t, :], start=(t == 0), stop=True)
            last.then_inc(posd, 1)

        @block.scalar
        def _(act):
            def squares(t):
                act.wait_ge(summed, 2 * t + 2)
                act.dma_start(one_of(tiles(R["acc"]), t), h_t[:]).then_inc(h_out, 16)
                nc.scalar.activation(junk[:], h_t[:], ACT.Square, accum_out=ss[:]).then_inc(sq, 1)
                act.wait_ge(rec_r, t + 1)
                nc.scalar.activation(rstd[:], rec[:], ACT.Sqrt).then_inc(rstd_r, 1)
                act.wait_ge(normed, t + 1)
                act.dma_start(one_of(tiles(R["hn"]), t), hn_t[:]).then_inc(hn_out, 16)

            def logits(t):
                act.wait_ge(turned, 2 * t + 1)
                nc.scalar.copy(hnT[:, 0:4, :], pX[0][:]).then_inc(x0_read, 1)
                act.wait_ge(lt, t + 1)
                nc.scalar.activation(lgT[:], pR[:], ACT.Identity, bias=C["rb"][:]).then_inc(lt_ready, 1)

            squares(0)
            with act.Fori(1, NT) as t:
                logits(t - 1)
                squares(t)
            logits(NT - 1)
            act.wait_ge(zero, 1)
            for d in (R["acc"], R["hn"]):
                for i in range(DUMP // P):
                    act.dma_start(d[SEQ + i * P:SEQ + (i + 1) * P, :], zeros).then_inc(z_out, 16)
            act.wait_ge(e_in, NT)
            nc.scalar.activation(lg[:], lg[:], ACT.Exp).then_inc(e_out, 1)
            act.wait_ge(h_out, 16 * NT)
            act.wait_ge(hn_out, 16 * NT)
            act.wait_ge(z_out, 16 * 2 * DUMP // P)

        @block.vector
        def _(dve):
            V = nc.vector
            B = lambda x, n: x.to_broadcast(n)

            def residual(t, first=False):
                dve.wait_ge(x_in, 16 * t + 16)
                if not first:
                    dve.wait_ge(h_out, 16 * t)
                for i in range(2):
                    dve.wait_ge(product, 3 * t + 2 + i)
                    c = slice(i * 512, (i + 1) * 512)
                    V.tensor_tensor(h_t[:, c], pM[:, c], x_t[:, c], ALU.add).then_inc(summed, 1)

            def norm(t, S, first=False):
                dve.wait_ge(sq, t + 1)
                S.mark(V.tensor_scalar(rec[:], ss[:], 1.0 / D, EPS, ALU.mult, ALU.add))
                S.wait(dve)
                V.reciprocal(rec[:], rec[:]).then_inc(rec_r, 1)
                dve.wait_ge(rstd_r, t + 1)
                if not first:
                    dve.wait_ge(hn_out, 16 * t)
                    dve.wait_ge(turned, 2 * t)
                V.scalar_tensor_tensor(hn_t[:], h_t[:], rstd[:], g_ffn[:], ALU.mult, ALU.mult).then_inc(normed, 1)

            def turned_half(t):
                dve.wait_ge(turned, 2 * t + 2)
                V.tensor_copy(hnT[:, 4:8, :], pX[1][:]).then_inc(x1_read, 1)

            def top(t, S):
                dve.wait_ge(l_turned, t + 1)
                V.tensor_copy(lg_t[:], pL[:]).then_inc(l_read, 1)
                hold(dve, l_read, t + 2, passed)
                S.mark(V.max(top_t[:], lg_t[:]))
                S.wait(dve)
                V.tensor_tensor(lg[:, bass.ds(t, 1), :], lg_t[:].unsqueeze(1),
                                B(top_t[:, 0:1].unsqueeze(1), [P, 1, NE]), ALU.subtract).then_inc(e_in, 1)
                S.mark(V.max_index(top_i[:], top_t[:], lg_t[:]))
                S.wait(dve)
                S.mark(V.tensor_copy(top_f[:], top_i[:, 0:TOPK]))
                S.wait(dve)
                S.mark(V.tensor_tensor(hot[:], B(top_f[:].unsqueeze(2), [P, TOPK, NE]),
                                       B(C["iota"][:, 0:NE].unsqueeze(1), [P, TOPK, NE]), ALU.is_equal))
                S.wait(dve)
                S.mark(V.tensor_reduce(took[:, bass.ds(t, 1), :], hot[:].rearrange("p k (a e) -> p a e k", a=1),
                                       AX_X, ALU.add))

            TURN = 6
            S = Steps(own)
            residual(0, True)
            dve.wait_ge(rld, 32)
            norm(0, S, True)
            n0 = S.n
            with dve.Fori(1, NT) as t:
                S = Steps(own, (t - 1) * TURN + n0)
                turned_half(t - 1)
                residual(t)
                top(t - 1, S)
                norm(t, S)
            assert S.n == TURN, S.n
            S = Steps(own, (NT - 1) * TURN + n0)
            turned_half(NT - 1)
            V.memset(zeros, 0.0).then_inc(zero, 1)
            top(NT - 1, S)
            S.wait(dve)
            V.tensor_copy(took_b[:], took[:]).then_inc(took_r, 1)
            dve.wait_ge(posd, 1)
            S.mark(V.tensor_copy(cnt[:], pC[:]))
            S.mark(V.scalar_tensor_tensor(W.place[:], pP[:], 1.0, took[:], ALU.add, ALU.mult))
            S.wait(dve)
            S.mark(V.tensor_scalar(W.place[:], W.place[:], -1.0, None, ALU.add))
            S.mark(V.tensor_scalar(more[:], cnt[:], float(CAP), None, ALU.is_gt))
            for j in range(2, MORE + 1):
                S.wait(dve)
                S.mark(V.scalar_tensor_tensor(more[:], cnt[:], float(CAP * j), more[:], ALU.is_gt, ALU.add))
            src, dst, other = more, cum, cum2
            for d in (1, 2, 4, 8, 16):
                S.wait(dve)
                S.mark(V.tensor_copy(dst[:, 0:d], src[:, 0:d]))
                S.mark(V.tensor_tensor(dst[:, d:], src[:, d:], src[:, 0:NE - d], ALU.add))
                src, dst, other = dst, other, dst
            assert src is cum
            S.wait(dve)
            S.mark(V.tensor_copy(W.items[:, 0:NE, 0], C["iota"][:, 0:NE]))
            S.mark(V.tensor_copy(W.items[:, 0:NE, 1], cnt[:]))
            S.mark(V.memset(W.items[:, 0:NE, 3], 0.0))
            S.mark(V.tensor_scalar(W.items[:, 0:NE, 2], B(cum[:, NE - 1:NE], [P, NE]), float(NE), None, ALU.add))
            S.wait(dve)
            S.mark(V.tensor_copy(W.tab_f[:, 0:NE], W.items[:, 0:NE, 3]))
            S.mark(V.tensor_copy(W.tab[:, 0:NE], W.items[:, 0:NE]))
            dve.wait_ge(e_out, 1)
            S.mark(V.tensor_tensor(lg[:], lg[:], took[:], ALU.mult))
            S.wait(dve)
            S.mark(V.tensor_reduce(se[:], lg[:], AX_X, ALU.add))
            S.wait(dve)
            S.mark(V.reciprocal(se[:], se[:]))
            S.wait(dve)
            S.mark(V.tensor_tensor(lg[:], lg[:], B(se[:].unsqueeze(2), [P, NT, NE]), ALU.mult))
            S.wait(dve)
            S.mark(V.tensor_copy(W.facts[:, :, :, 3], lg[:]))
            S.wait(dve)
            S.mark(V.tensor_tensor(rest, lg[:], W.facts[:, :, :, 3], ALU.subtract))
            S.wait(dve)
            S.mark(V.tensor_copy(W.facts[:, :, :, 4], rest))
            S.wait(dve)
            S.mark(V.tensor_tensor(rest, rest, W.facts[:, :, :, 4], ALU.subtract))
            S.wait(dve)
            S.mark(V.tensor_copy(W.facts[:, :, :, 5], rest))
            S.wait(dve)


class Weights:

    def __init__(self, nc, M, a):
        self.a = a
        self.w1 = [M.sb(f"w1_{c}", [P, KT, 2, P]) for c in range(FC)]
        self.w2 = [M.sb(f"w2_{c}", [P, DFF // P, D // DC]) for c in range(DC)]
        self.tab = M.sb("tab", [P, MAX_ITEMS, 4], I32)
        self.tab_f = M.sb("tab_f", [P, MAX_ITEMS])
        self.facts = M.sb("facts", [P, NT, NE, 6], BF16)
        self.place = M.sb("place", [P, NT, NE])
        self.items = M.sb("items", [P, MAX_ITEMS, 4])
        self.cnt, self.cum = M.sb("cnt", [P, NE]), M.sb("cum", [P, NE])
        self.w1_in = [M.sem(f"w1in{c}") for c in range(FC)]
        self.w2_in = [M.sem(f"w2in{c}") for c in range(DC)]
        self.up_done, self.down_done = M.sem("up_done"), M.sem("down_done")

    def load(self, sp, n, e=0, first=False, chunks=range(FC + DC)):
        w1 = self.a["moe_w1"].rearrange("l e (k p) (two c f) -> c (l e) two p k f", p=P, two=2, f=P)
        w2 = self.a["moe_w2"].rearrange("l e (k p) (c d) -> c (l e) p k d", p=P, c=DC)
        for c in (c for c in chunks if c < FC):
            if not first:
                sp.wait_ge(self.up_done, FC * (n - 1) + c + 1)
            for two in range(2):
                sp.dma_start(self.w1[c][:, :, two, :], w1[c, bass.ds(e, 1), two].rearrange("a p k f -> (a p) k f")
                             ).then_inc(self.w1_in[c], 16)
        for c in (c - FC for c in chunks if c >= FC):
            if not first:
                sp.wait_ge(self.down_done, DC * (n - 1) + c + 1)
            sp.dma_start(self.w2[c][:], w2[c, bass.ds(e, 1)].rearrange("a p k d -> (a p) k d")
                         ).then_inc(self.w2_in[c], 16)


def experts(nc, C, R, W):
    with ExitStack() as ctx:
        M = Mem(nc, ctx, C["sems"])
        place_e, facts_e = M.sb("e_place", [P, NT]), M.sb("e_facts", [P, NT, 6], BF16)
        onehot = M.sb("e_onehot", [P, NT, CAP], BF16)
        iota8 = C["iota"]
        told = M.sb("e_told", [P, 2, 6])
        tmp = M.sb("e_tmp", [P, 4, 2])
        dump = M.sb("e_dump", [P, 2])
        extra = M.sb("e_extra", [P, 3, EXTRA])
        is_e, sums = M.sb("e_ise", [P, EXTRA, NE]), M.sb("e_sums", [P, EXTRA, NE])
        idx_next, idx = M.sb("e_idxn", [P, 2], I32), M.sb("e_idx", [P, 2], I32)
        gate_next, gate = M.sb("e_gaten", [P, 2]), M.sb("e_gate", [P, 2])
        x0, x1 = M.sb("e_x0", [P, D]), M.sb("e_x1", [64, D])
        xT = M.sb("e_xT", [P, KT, CAP])
        b1, b2 = M.sb("e_b1", [P, 2 * FC]), M.sb("e_b2", [P, KT])
        g1, g2, up = M.sb("e_g1", [P, 2, CAP]), M.sb("e_g2", [P, 2, CAP]), M.sb("e_up", [P, 2, CAP])
        sg = M.sb("e_sg", [P, 2, CAP])
        hT = M.sb("e_hT", [P, FC, CAP])
        yT = M.sb("e_yT", [P, KT, CAP])
        y0, y1 = M.sb("e_y0", [P, D]), M.sb("e_y1", [64, D])
        pH = [M.ps(f"e_pH{i}", [P, 2, 256]) for i in range(2)]
        pY = [M.ps(f"e_pY{i}", [P, 2, 256]) for i in range(2)]
        pX = [M.ps(f"e_pX{i}", [P, 4, P]) for i in range(2)]
        pD = M.ps("e_pD", [P, 2, 8])
        s = lambda x: M.sem("e_" + x)
        cleared, cleared_y, picked, told_ready, idx_ready = s("clr"), s("clry"), s("picked"), s("told"), s("idx")
        gathered, cur_ready = [s("ga0"), s("ga1")], s("cur")
        bank_turned, bank_read = [s("bt0"), s("bt1")], [s("br0"), s("br1")]
        h_read, lin_ready, sg_ready, h_ready = s("hread"), s("lin"), s("sg"), s("h")
        yT_ready, scat, scattered = s("yT"), [s("sc0"), s("sc1")], s("scattered")
        own_d, own_a, b_staged, passed = s("od"), s("oa"), s("bst"), s("passed")
        table_ready = s("table")
        block = ctx.enter_context(nc.Block())
        PER, FREE = 4, 1

        def seq_late(n):
            return 2 + PER * n

        def seq_x(n):
            return 3 + PER * n

        def seq_early(n):
            return 5 + PER * n

        def n_items(eng):
            return eng.value_load(W.tab[0:1, 0, 2:3], min_val=NE, max_val=NE + SEQ * TOPK // CAP)

        def expert(eng, n):
            return eng.value_load(W.tab[0:1, bass.ds(n, 1), 0:1].rearrange("p a c -> p (a c)"),
                                  min_val=0, max_val=NE - 1)

        @block.sync
        def _(sp):
            hold(sp, table_ready, 1, passed)
            last = n_items(sp)
            with sp.Fori(1, last) as n:
                W.load(sp, n, expert(sp, n))

        @block.gpsimd
        def _(pool):
            def gather(i):
                hold(pool, idx_ready, i + 1, passed)
                pool.indirect_dma_start(x0[:], None, R["hn"], bass.IndirectOffsetOnAxis(idx_next[:, 0:1], 0)
                                        ).then_inc(gathered[0], 16)
                pool.indirect_dma_start(x1[:], None, R["hn"], bass.IndirectOffsetOnAxis(idx_next[0:64, 1:2], 0)
                                        ).then_inc(gathered[1], 16)
            last = n_items(pool)
            gather(0)
            for c, t in enumerate((yT[:, 4:8], y0[:], y1[:])):
                pool.memset(t, 0.0).then_inc(cleared_y, 1)
                pool.wait_ge(cleared_y, c + 1)
            def scatter(n):
                for b in range(2):
                    hold(pool, bank_read[b], seq_late(n) + 1 + FREE, passed)
                pool.indirect_dma_start(R["acc"], bass.IndirectOffsetOnAxis(idx[:, 0:1], 0), y0[:], None,
                                        compute_op=ALU.add).then_inc(scat[0], 16)
                pool.indirect_dma_start(R["acc"], bass.IndirectOffsetOnAxis(idx[0:64, 1:2], 0), y1[:], None,
                                        compute_op=ALU.add).then_inc(scat[1], 16)
                for b in range(2):
                    pool.wait_ge(scat[b], 16 * n + 16)
                pool.sem_inc(scattered, 1)

            with pool.Fori(0, last) as n:
                scatter(n)
                gather(n + 1)
            scatter(last)
            for b in range(2):
                pool.wait_ge(gathered[b], 16)

        @block.tensor
        def _(pe):
            def pick(i):
                pe.wait_ge(picked, i + 1)
                for j, rows in enumerate((P, 64)):
                    for t in range(NT):
                        last = nc.tensor.matmul(pD[0:rows, j, 0:6], onehot[:, t, j * P:j * P + rows],
                                                facts_e[:, t, :], start=(t == 0), stop=(t == NT - 1))
                last.then_inc(told_ready, 1)

            def turn_x(i, seq, steps):
                for j in steps:
                    if j == 0:
                        for b in range(2):
                            pe.wait_ge(gathered[b], 16 * i + 16)
                    pe.wait_ge(bank_read[j % 2], seq + j // 2 + FREE)
                    for m in range(2):
                        k = 2 * j + m
                        room = pX[j % 2][:, 2 * m:2 * m + 2, :].rearrange("p a q -> p (a q)")
                        nc.tensor.transpose(room[:, 0:P], x0[:, k * P:(k + 1) * P], C["ident"][:])
                        last = nc.tensor.transpose(room[:, P:CAP], x1[:, k * P:(k + 1) * P], C["ident"][0:64, 0:64])
                    last.then_inc(bank_turned[j % 2], 1)

            def turn_y(n, c):
                if c < 2:
                    pe.wait_ge(yT_ready, DC * n + c + 1 + 2)
                    pe.wait_ge(bank_read[c % 2], seq_early(n) + FREE)
                else:
                    pe.wait_ge(yT_ready, DC * n + c + 1 + 2 - DC)
                    pe.wait_ge(bank_read[c % 2], seq_late(n) + FREE)
                for m in range(2):
                    nc.tensor.transpose(pX[c % 2][:, m, :], yT[:, 2 * c + m, 0:P], C["ident"][:])
                    last = nc.tensor.transpose(pX[c % 2][0:64, 2 + m, :], yT[:, 2 * c + m, P:CAP], C["ident"][:])
                last.then_inc(bank_turned[c % 2], 1)

            def item(n, N):
                for b in range(2):
                    pe.wait_ge(bank_read[b], PER * n + 1 + FREE)
                for c in range(FC):
                    pe.wait_ge(W.w1_in[c], 32 * n + 32)
                    pe.wait_ge(h_read, FC * n + c + 1)
                    for two in range(2):
                        for k in range(KT):
                            last = nc.tensor.matmul(pH[c % 2][:, two, 0:N], W.w1[c][:, k, two, :], xT[:, k, 0:N],
                                                    start=(k == 0), stop=(k == KT - 1))
                    last.then_inc(W.up_done, 1)
                    if c == 0:
                        turn_y(n, 2)
                        turn_y(n, 3)
                    if c == 4:
                        pick(n + 1)
                for c in range(DC):
                    pe.wait_ge(W.w2_in[c], 16 * n + 16)
                    pe.wait_ge(yT_ready, DC * n + c + 1)
                    steps = [(k, m) for m in range(2) for k in range(DFF // P)]
                    if c == 0:
                        steps.sort(key=lambda s: s[0] == DFF // P - 1)
                    for k, m in steps:
                        if c == 0 and m == 0:
                            pe.wait_ge(h_ready, FC * n + k + 1)
                        last = nc.tensor.matmul(pY[c % 2][:, m, 0:N], W.w2[c][:, k, m * P:(m + 1) * P],
                                                hT[:, k, 0:N], start=(k, m) == steps[0], stop=(k, m) == steps[-1])
                    last.then_inc(W.down_done, 1)
                    if c < 2:
                        turn_x(n + 1, seq_x(n), (2 * c, 2 * c + 1))
                    if c == 2:
                        turn_y(n, 0)
                        turn_y(n, 1)

            def choose(n, left, variants):
                if len(variants) == 1:
                    item(n, variants[0])
                    return
                with pe.If(left <= variants[0]):
                    item(n, variants[0])
                with pe.Else():
                    choose(n, left, variants[1:])

            for b in range(2):
                pe.sem_inc(bank_read[b], FREE)
            pe.sem_inc(h_read, 2)
            pe.sem_inc(yT_ready, 2)
            last = n_items(pe)
            pick(0)
            turn_x(0, 0, range(4))
            for b in range(2):
                pe.wait_ge(bank_read[b], 2 + FREE)
            hold(pe, table_ready, 1, passed)
            pe.wait_ge(cleared, 4)
            pe.wait_ge(cleared_y, 3)
            with pe.Fori(0, last) as n:
                left = pe.value_load(W.tab[0:1, bass.ds(n, 1), 1:2].rearrange("p a c -> p (a c)"),
                                     min_val=-SEQ * 64, max_val=SEQ)
                choose(n, left, VARIANTS)
            turn_y(last, 2)
            turn_y(last, 3)

        @block.scalar
        def _(act):
            def stage_b2(i):
                e = expert(act, i)
                nc.scalar.copy(b2[:], C["b2"][:, bass.ds(e * KT, KT)]).then_inc(own_a, 1)

            def read_x(seq, steps=(0, 2)):
                for j in steps:
                    act.wait_ge(bank_turned[0], seq + j // 2 + 1)
                    nc.scalar.copy(xT[:, 2 * j:2 * j + 2, :],
                                   pX[0][:].rearrange("p (m a) q -> p m (a q)", m=2)[:, :, 0:CAP]
                                   ).then_inc(bank_read[0], 1)

            stage_b2(0)
            last = n_items(act)
            read_x(0)
            def results(n, c):
                seq = seq_early(n) if c < 2 else seq_late(n)
                act.wait_ge(bank_turned[0], seq + 1)
                nc.scalar.activation(y0[:, 2 * c * P:(2 * c + 2) * P], pX[0][:, 0:2, :].rearrange("p a q -> p (a q)"),
                                     ACT.Copy, scale=gate[:, 0:1])
                nc.scalar.activation(y1[:, 2 * c * P:(2 * c + 2) * P],
                                     pX[0][0:64, 2:4, :].rearrange("p a q -> p (a q)"),
                                     ACT.Copy, scale=gate[0:64, 1:2]).then_inc(bank_read[0], 1)

            hold(act, table_ready, 1, passed)
            with act.Fori(0, last) as n:
                for c in range(FC):
                    act.wait_ge(lin_ready, FC * n + c + 1)
                    nc.scalar.activation(sg[:, c % 2], g1[:, c % 2], ACT.Sigmoid, scale=ALPHA).then_inc(sg_ready, 1)
                    if c == 0:
                        results(n, 2)
                act.wait_ge(own_a, n + 1)
                for c in range(DC):
                    act.wait_ge(W.down_done, DC * n + c + 1)
                    for m in range(2):
                        k = 2 * c + m
                        ins = nc.scalar.activation(yT[:, k, :], pY[c % 2][:, m, 0:CAP], ACT.Identity,
                                                   bias=b2[:, k:k + 1])
                    ins.then_inc(yT_ready, 1)
                    if c < 2:
                        read_x(seq_x(n), (2 * c,))
                    if c == 2:
                        act.wait_ge(cur_ready, n + 1)
                        results(n, 0)
                act.wait_ge(yT_ready, DC * (n + 1) + 2)
                stage_b2(n + 1)
            results(last, 2)

        @block.vector
        def _(dve):
            V = nc.vector
            B = lambda x, n: x.to_broadcast(n)
            OWN = 3 * FC + 2 + 6

            def prepare(i):
                e = expert(dve, i)
                V.tensor_scalar(place_e[:].unsqueeze(2), W.place[:, :, bass.ds(e, 1)],
                                W.tab_f[:, bass.ds(i, 1)], None, ALU.subtract).then_inc(b_staged, 1)
                V.tensor_copy(facts_e[:].unsqueeze(2), W.facts[:, :, bass.ds(e, 1), :])
                dve.wait_ge(b_staged, 2 * i + 1)
                for t in range(NT):
                    ins = V.tensor_scalar(onehot[:, t, :], C["iota"][:], place_e[:, t:t + 1], None, ALU.is_equal)
                ins.then_inc(picked, 1)

            def stage_b1(i):
                e = expert(dve, i)
                V.tensor_copy(b1[:], C["b1"][:, bass.ds(e * (2 * FC), 2 * FC)]).then_inc(b_staged, 1)

            def addresses(i, S):
                dve.wait_ge(told_ready, i + 1)
                S.mark(V.tensor_copy(told[:, 0, :], pD[:, 0, 0:6]))
                S.mark(V.tensor_copy(told[0:64, 1, :], pD[0:64, 1, 0:6]))
                S.wait(dve)
                S.mark(V.tensor_scalar(tmp[:, 0], told[:, :, 2], -1.0, 1.0, ALU.mult, ALU.add))
                S.mark(V.scalar_tensor_tensor(tmp[:, 1], told[:, :, 1], float(P), told[:, :, 0], ALU.mult, ALU.add))
                S.mark(V.tensor_tensor(tmp[:, 2], told[:, :, 3], told[:, :, 4], ALU.add))
                S.wait(dve)
                S.mark(V.tensor_tensor(tmp[:, 0], tmp[:, 0], dump[:], ALU.mult))
                V.tensor_tensor(gate_next[:], tmp[:, 2], told[:, :, 5], ALU.add)
                S.wait(dve)
                V.tensor_tensor(idx_next[:], tmp[:, 0], tmp[:, 1], ALU.add).then_inc(idx_ready, 1)

            def read_x(seq):
                for j in (1, 3):
                    dve.wait_ge(bank_turned[1], seq + j // 2 + 1)
                    V.tensor_copy(xT[:, 2 * j:2 * j + 2, :],
                                  pX[1][:].rearrange("p (m a) q -> p m (a q)", m=2)[:, :, 0:CAP]
                                  ).then_inc(bank_read[1], 1)

            S = Steps(own_d)
            S.mark(V.memset(told[:], 0.0))
            S.mark(V.memset(gate[:], 0.0))
            S.mark(V.tensor_scalar(dump[:, 0:1], C["iota_p"][:], float(SEQ), None, ALU.add))
            S.mark(V.tensor_scalar(dump[:, 1:2], C["iota_p"][:], float(SEQ + P), None, ALU.add))
            S.wait(dve)
            prepare(0)
            stage_b1(0)
            addresses(0, S)
            full = [P, EXTRA, NE]
            x_no, experts_no, items = C["iota"][:, 0:EXTRA], C["iota"][:, 0:NE], W.items
            S.mark(V.tensor_tensor(is_e[:], B(W.cum[:].unsqueeze(1), full), B(x_no.unsqueeze(2), full), ALU.is_le))
            S.mark(V.tensor_copy(items[:, NE:, 2], B(items[:, 0:1, 2], [P, EXTRA])))
            S.wait(dve)
            S.mark(V.tensor_tensor(sums[:], is_e[:], B(W.cum[:].unsqueeze(1), full), ALU.mult))
            S.mark(V.tensor_reduce(items[:, NE:, 0], is_e[:], AX_X, ALU.add))
            S.wait(dve)
            S.mark(V.tensor_reduce(extra[:, 0, :], sums[:], AX_X, ALU.max))
            S.mark(V.tensor_scalar(items[:, NE:, 0], items[:, NE:, 0], float(NE - 1), None, ALU.min))
            S.wait(dve)
            S.mark(V.tensor_tensor(is_e[:], B(experts_no.unsqueeze(1), full), B(items[:, NE:, 0:1], full), ALU.is_equal))
            S.mark(V.tensor_tensor(extra[:, 2, :], x_no, extra[:, 0, :], ALU.subtract))
            S.wait(dve)
            S.mark(V.tensor_tensor(is_e[:], is_e[:], B(W.cnt[:].unsqueeze(1), full), ALU.mult))
            S.mark(V.tensor_scalar(items[:, NE:, 3], extra[:, 2, :], float(CAP), float(CAP), ALU.mult, ALU.add))
            S.wait(dve)
            S.mark(V.tensor_reduce(extra[:, 1, :], is_e[:], AX_X, ALU.add))
            S.wait(dve)
            S.mark(V.tensor_tensor(items[:, NE:, 1], extra[:, 1, :], items[:, NE:, 3], ALU.subtract))
            S.mark(V.tensor_copy(W.tab_f[:, NE:], items[:, NE:, 3]))
            S.wait(dve)
            V.tensor_copy(W.tab[:, NE:], items[:, NE:]).then_inc(table_ready, 1)
            dve.wait_ge(table_ready, 1)
            for ps in (*pH, *pY):
                V.memset(ps[:], 0.0).then_inc(cleared, 1)
            S.mark(V.tensor_copy(idx[:], dump[:]))
            S.wait(dve)

            def results(n, c):
                seq = seq_early(n) if c < 2 else seq_late(n)
                dve.wait_ge(bank_turned[1], seq + 1)
                V.tensor_scalar(y0[:, 2 * c * P:(2 * c + 2) * P], pX[1][:, 0:2, :].rearrange("p a q -> p (a q)"),
                                gate[:, 0:1], None, ALU.mult)
                V.tensor_scalar(y1[:, 2 * c * P:(2 * c + 2) * P], pX[1][0:64, 2:4, :].rearrange("p a q -> p (a q)"),
                                gate[0:64, 1:2], None, ALU.mult).then_inc(bank_read[1], 1)

            last = n_items(dve)
            read_x(0)
            n0 = S.n
            with dve.Fori(0, last) as n:
                S = Steps(own_d, n * OWN + n0)
                dve.wait_ge(b_staged, 2 * n + 2)
                for c in range(FC):
                    dve.wait_ge(W.up_done, FC * n + c + 1)
                    S.mark(V.tensor_scalar(g1[:, c % 2], pH[c % 2][:, 0, 0:CAP], b1[:, c:c + 1], LIMIT, ALU.add, ALU.min))
                    V.tensor_scalar(up[:, c % 2], pH[c % 2][:, 1, 0:CAP], b1[:, FC + c:FC + c + 1], LIMIT,
                                    ALU.add, ALU.min).then_inc(h_read, 1)
                    V.drain().then_inc(lin_ready, 1)
                    dve.wait_ge(lin_ready, FC * n + c + 1)
                    S.mark(V.tensor_scalar(up[:, c % 2], up[:, c % 2], -LIMIT, 1.0, ALU.max, ALU.add))
                    dve.wait_ge(sg_ready, FC * n + c + 1)
                    S.mark(V.tensor_tensor(g2[:, c % 2], g1[:, c % 2], sg[:, c % 2], ALU.mult))
                    S.wait(dve)
                    V.tensor_tensor(hT[:, c, :], g2[:, c % 2], up[:, c % 2], ALU.mult).then_inc(h_ready, 1)
                    if c == 0:
                        results(n, 3)
                    if c == 1:
                        prepare(n + 1)
                    if c == 5:
                        dve.wait_ge(scattered, n + 1)
                        dve.wait_ge(bank_read[0], seq_late(n) + 1 + FREE)
                        dve.wait_ge(idx_ready, n + 1)
                        for b in range(2):
                            dve.wait_ge(gathered[b], 16 * n + 16)
                        S.mark(V.tensor_copy(idx[:], idx_next[:]))
                        S.mark(V.tensor_copy(gate[:], gate_next[:]))
                        S.wait(dve)
                        dve.sem_inc(cur_ready, 1)
                        addresses(n + 1, S)
                stage_b1(n + 1)
                read_x(seq_x(n))
                dve.wait_ge(cur_ready, n + 1)
                results(n, 1)
            results(last, 3)
            assert S.n == OWN, S.n


def final(nc, C, R, a, out):
    HALVES = NT // 2
    with ExitStack() as ctx:
        M = Mem(nc, ctx, C["sems"])
        h = M.sb("f_h", [P, NT, D])
        g = M.sb("f_g", [P, D])
        junk = M.sb("f_junk", [P, NT, D], BF16)
        ss, rec, rstd = M.sb("f_ss", [P, NT]), M.sb("f_rec", [P, NT]), M.sb("f_rstd", [P, NT])
        h_in = [M.sem(f"f_in{t}") for t in range(NT)]
        g_in, sq, own, rec_r, rstd_r, done, stored = (M.sem("f_" + s) for s in ("g", "sq", "own", "rec", "rstd", "done", "st"))
        block = ctx.enter_context(nc.Block())
        acc = R["acc"][0:SEQ].rearrange("(t p) d -> t p d", p=P)
        res = out.rearrange("b (t p) d -> (b t) p d", p=P)

        @block.sync
        def _(sp):
            sp.dma_start(g[:], a["final_norm"].rearrange("(l d) -> l d", l=1).to_broadcast([P, D])).then_inc(g_in, 16)
            for t in range(NT):
                sp.dma_start(h[:, t, :], acc[t]).then_inc(h_in[t], 16)
            for t in range(NT):
                sp.wait_ge(done, t + 1)
                sp.dma_start(res[t], h[:, t, :]).then_inc(stored, 16)
            sp.wait_ge(stored, 16 * NT)

        @block.scalar
        def _(act):
            for t in range(NT):
                act.wait_ge(h_in[t], 16)
                nc.scalar.activation(junk[:, t], h[:, t, :], ACT.Square, accum_out=ss[:, t:t + 1]).then_inc(sq, 1)
                if t >= 1:
                    act.wait_ge(rec_r, t)
                    nc.scalar.activation(rstd[:, t - 1:t], rec[:, t - 1:t], ACT.Sqrt).then_inc(rstd_r, 1)
            act.wait_ge(rec_r, NT)
            nc.scalar.activation(rstd[:, NT - 1:], rec[:, NT - 1:], ACT.Sqrt).then_inc(rstd_r, 1)

        @block.vector
        def _(dve):
            dve.wait_ge(g_in, 16)
            for t in range(NT + 1):
                if t < NT:
                    dve.wait_ge(sq, t + 1)
                    nc.vector.tensor_scalar(rec[:, t:t + 1], ss[:, t:t + 1], 1.0 / D, EPS, ALU.mult, ALU.add
                                            ).then_inc(own, 1)
                    dve.wait_ge(own, t + 1)
                    nc.vector.reciprocal(rec[:, t:t + 1], rec[:, t:t + 1]).then_inc(rec_r, 1)
                if t >= 1:
                    dve.wait_ge(rstd_r, t)
                    nc.vector.scalar_tensor_tensor(h[:, t - 1, :], h[:, t - 1, :], rstd[:, t - 1:t], g[:],
                                                   ALU.mult, ALU.mult).then_inc(done, 1)


def layer(nc, a, out, upto=None, debug=None):
    R = {k: nc.dram_tensor(k, (SEQ + DUMP, D), F32, kind="Internal").ap() for k in ("acc", "hn")}
    with ExitStack() as whole:
        M = Mem(nc, whole)
        C = {
            "sems": [],
            "ident": M.sb("ident", [P, P]), "ident_b": M.sb("ident_b", [P, P], BF16),
            "causal": M.sb("causal", [P, P], BF16), "far": M.sb("far", [P, P], BF16),
            "cmp_mask": M.sb("cmp_mask", [P, NT, 64], BF16), "before": M.sb("before", [P, P], BF16),
            "ones_b": M.sb("ones_b", [P, P], BF16), "late": M.sb("late", [P, 1]),
            "iota_i": M.sb("iota_i", [P, CAP], I32), "iota": M.sb("iota", [P, CAP]),
            "iota_p_i": M.sb("iota_p_i", [P, 1], I32), "iota_p": M.sb("iota_p", [P, 1]),
            "iota_t_i": M.sb("iota_t_i", [P, NT], I32), "iota_t": M.sb("iota_t", [P, NT]),
            "vec": M.sb("vec", [P, 19]), "b1": M.sb("b1", [P, NE * 2 * FC]), "b2": M.sb("b2", [P, NE * KT]),
            "rb": M.sb("rb", [NE, 1]), "trig": M.sb("trig", [P, 2, NT + 1, NF]),
        }
        with ExitStack() as early:
            with ExitStack() as heads:
                M = Mem(nc, heads)
                R["latT"] = M.sb("latT", [P, 3, SEQ])
                R["nsaT"] = M.sb("nsaT", [96, 12, SEQ])
                R["v_s"], R["v_w"] = M.sb("v_s", [P, NT, KVW]), M.sb("v_w", [P, NT, KVW])
                R["k_pe"] = M.sb("k_pe", [P, NT, ROPE])
                R["gates"] = M.sb("gates", [P, NT, 3 * H_NSA])
                R["kcT"] = M.sb("kcT", [96, G_NSA, 64])
                R["v_c"] = M.sb("v_c", [64, G_NSA, DH])
                with ExitStack() as blocks:
                    M = Mem(nc, blocks, C["sems"])
                    R["rawT"] = M.sb("rawT", [P, 4, SEQ])
                    F = Ahead(nc, M, a)
                    constants(nc, C, F, a)
                    project(nc, C, R, F, a)
                    compress(nc, C, R, F)
                nc.clear_and_free_semaphores(C["sems"])
                nc.all_engine_barrier()
                C["sems"] = []
                R["mixT"] = early.enter_context(nc.sbuf_tensor("mixT", [P, KT, SEQ], F32, side="right"))
                mla(nc, C, R, a)
                nsa(nc, C, R)
            with ExitStack() as late:
                W = Weights(nc, Mem(nc, late, C["sems"]), a)
                route(nc, C, R, W, a)
                experts(nc, C, R, W)
        final(nc, C, R, a, out)


_INS = ["x", "positions", "attn_norm", "w_in", "mla_q_norm", "mla_w_q_up", "mla_kv_norm", "mla_w_kv_up",
        "nsa_cmp_pos", "nsa_cmp_w1", "nsa_cmp_w2", "w_out", "ffn_norm", "router_w", "router_b",
        "moe_w1", "moe_b1", "moe_w2", "moe_b2", "final_norm"]


def kernel(**inputs):
    import numpy as _np
    import concourse.bacc as _bacc
    from concourse import mybir as _mybir
    from concourse.bass_utils import run_bass_kernel_spmd as _run

    nc = _bacc.Bacc("TRN2", target_bir_lowering=False, num_devices=1)
    arrays, args = {}, {}
    for name in _INS:
        x = _np.ascontiguousarray(inputs[name])
        arrays[f"in_{name}"] = x
        args[name] = nc.dram_tensor(f"in_{name}", x.shape, _mybir.dt.from_np(x.dtype), kind="ExternalInput").ap()
    out = nc.dram_tensor("out_0", (1, SEQ, D), F32, kind="ExternalOutput").ap()
    layer(nc, args, out)
    r = _run(nc, [arrays], core_ids=[0])
    return r.results[0]["out_0"]
```

```python
from contextlib import ExitStack

import numpy as np

import concourse.bass as bass
from concourse import mybir
from concourse.alu_op_type import AluOpType as ALU

F32 = mybir.dt.float32
F32R = mybir.dt.float32r
BF16 = mybir.dt.bfloat16
I32 = mybir.dt.int32
U32 = mybir.dt.uint32
ACT = mybir.ActivationFunctionType
AX_X = mybir.AxisListType.X
AX_XY = mybir.AxisListType.XY

P = 128
SEQ, D = 1024, 1024
NT, KT = SEQ // P, D // P
EPS = 1e-5
NEG = -1e30
THETA = 500000.0

H_MLA, NOPE, ROPE, V_DIM = 8, 64, 32, 64
QK_MLA = NOPE + ROPE
Q_RANK, KV_RANK = 256, 128
H_NSA, G_NSA, DH, ROPE_N = 8, 2, 64, 16
CMP_BLOCK, CMP_STRIDE, CMP_HID = 32, 16, 128
N_CMP = (SEQ - CMP_BLOCK) // CMP_STRIDE + 1
WINDOW = 512
WT = WINDOW // P
KVW = G_NSA * DH
IN_COLS = Q_RANK + KV_RANK + ROPE + H_NSA * DH + 6 * KVW + 3 * H_NSA
C_Q, C_KV = 0, Q_RANK
C_PE = C_KV + KV_RANK
C_QN = C_PE + ROPE
C_KC = C_QN + H_NSA * DH
C_KW = C_KC + 4 * KVW
NF = ROPE // 2 + ROPE_N // 2

NE, TOPK, DFF = 32, 4, 1024
LIMIT, ALPHA = 7.0, 1.702
CAP = 192
VARIANTS = tuple(range(P, CAP + 1, 8))
MORE = (SEQ - 1) // CAP
EXTRA = SEQ * TOPK // CAP + 1
MAX_ITEMS = NE + EXTRA
DUMP = 256
REST = CAP - P
FC = 8
FIRST = 2
DC = 4

TWO_PI = 2.0 * np.pi
C1 = 6.28125
C2 = float(np.float32(np.round((TWO_PI - C1) * 2.0 ** 20) / 2.0 ** 20))
C3 = float(TWO_PI - C1 - C2)
ROUND = 12582912.0
PI_IN = 3.1415925


def stored(x):
    return x.rearrange("p (h j f) -> p h j f", h=2, f=P)


def natural(x):
    return x.rearrange("p (j h f) -> p h j f", h=2, f=P)


def place_of(k):
    return (k % 2) * (D // 2) + (k // 2) * P


class Steps:

    def __init__(self, sem, base=0):
        self.sem, self.base, self.n = sem, base, 0

    def mark(self, ins):
        ins.then_inc(self.sem, 1)
        self.n += 1
        return ins

    def wait(self, eng):
        eng.wait_ge(self.sem, self.base + self.n)


def hold(eng, sem, value, passed):
    eng.wait_ge(sem, value)
    eng.sem_inc(passed, 1)


def frequencies():
    def inv(rot):
        return np.float32(THETA ** (-np.arange(0, rot, 2) / rot))
    return [float(f) for f in np.concatenate([inv(ROPE), inv(ROPE_N)])]


class Mem:

    def __init__(self, nc, ctx, sems=None):
        self.nc, self.ctx, self.sems = nc, ctx, sems

    def sb(self, name, shape, dt=F32):
        return self.ctx.enter_context(self.nc.sbuf_tensor(name, shape, dt))

    def ps(self, name, shape, dt=F32):
        return self.ctx.enter_context(self.nc.psum_tensor(name, shape, dt))

    def sem(self, name):
        self.sems.append(self.nc.alloc_semaphore(name=name))
        return self.sems[-1]


class Ahead:

    def __init__(self, nc, M, a, later):
        self.a = a
        self.w_in = [M.sb(f"w_in{i}", [P, KT, c1 - c0])[:] for i, (c0, c1) in enumerate(PROJ[:WHOLE])]
        for (c0, c1), room in zip(PROJ[WHOLE:], later):
            flat = room[:].rearrange("p j s -> p (j s)")[:, 0:KT * (c1 - c0)]
            self.w_in.append(flat.rearrange("p (k c) -> p k c", k=KT))
        self.x_t = M.sb("x_t", [P, D])
        self.w_loaded, self.x_loaded = [M.sem(f"p_w{i}") for i in range(4)], M.sem("p_x")
        self.x_rows = a["x"].rearrange("b (t p) d -> (b t) p d", p=P)
        LP = CMP_BLOCK // 2
        self.cmp_w1 = self.w_in[1].rearrange("p k c -> p (k c)").rearrange("p (c lp h) -> p c lp h", c=2, lp=LP)
        self.cmp_w2 = self.w_in[0].rearrange("p k c -> p (k c)")[:, 0:2 * DH].rearrange("p (c d) -> p c d", c=2)
        self.cmp_pos = M.sb("cpos", [2 * LP, 2 * DH])
        self.cmp_loaded, self.pos_loaded = M.sem("cc_ld"), M.sem("cc_ldp")

    def load_products(self, sp):
        w_rows = self.a["w_in"].rearrange("l (k p) c -> (l p) k c", p=P)
        sp.dma_start(self.x_t[:], self.x_rows[0]).then_inc(self.x_loaded, 16)
        for i, (c0, c1) in enumerate(PROJ):
            sp.dma_start(self.w_in[i], w_rows[:, :, c0:c1]).then_inc(self.w_loaded[i], 16)

    def load_compress(self, sp):
        w1, w2 = self.a["nsa_cmp_w1"], self.a["nsa_cmp_w2"]
        for c in range(2):
            sp.dma_start(self.cmp_w1[:, c], w1[0, c].rearrange("(lp two) d h -> (two d) lp h", two=2)
                         ).then_inc(self.cmp_loaded, 16)
        sp.dma_start(self.cmp_w2, w2.rearrange("l c h d -> (l h) c d")).then_inc(self.cmp_loaded, 16)

    def load_positions(self, sp):
        sp.dma_start(self.cmp_pos[:], self.a["nsa_cmp_pos"].rearrange("l c (lp two) d -> (l c lp) (two d)", two=2)
                     ).then_inc(self.pos_loaded, 16)


def constants(nc, C, F, a):
    with ExitStack() as ctx:
        M = Mem(nc, ctx, C["sems"])
        rows = M.sb("rows", [19, P])
        rows_b1 = M.sb("rows_b1", [P, 4, P])
        rows_b2 = M.sb("rows_b2", [P, 2, P])
        pos_i = M.sb("pos_i", [NT, P], I32)
        pos_r = M.sb("pos_r", [NT, P])
        posc_i = M.sb("posc_i", [N_CMP, 1], I32)
        posp = M.sb("posp", [P, NT + 1])
        freq = M.sb("freq", [P, NF])
        ang = M.sb("ang", [P, NT + 1, NF])
        turns = M.sb("turns", [P, 2, NT + 1, NF])
        red = M.sb("red", [P, 2, NT + 1, NF])
        ones_f = M.sb("ones_f", [P, P])
        it_i = M.sb("it_i", [P, CAP], I32)
        pS = [M.ps(f"pc{i}", [P, 4, P]) for i in range(4)]
        ld_rows, ld_b, ld_pos, ld_posc = M.sem("c_rows"), M.sem("c_b"), M.sem("c_pos"), M.sem("c_posc")
        masks, fr, tr, own = M.sem("c_masks"), M.sem("c_freq"), M.sem("c_tr"), M.sem("c_own")
        zeroed, table, ev = M.sem("c_zero"), M.sem("c_table"), M.sem("c_ev")
        block = ctx.enter_context(nc.Block())

        @block.sync
        def _(sp):
            for r0, name, n in ((0, "attn_norm", 8), (8, "mla_q_norm", 2), (10, "mla_kv_norm", 1),
                                (11, "ffn_norm", 8)):
                sp.dma_start(rows[r0:r0 + n, :], a[name].rearrange("l (k p) -> (l k) p", p=P)).then_inc(ld_rows, 16)
            sp.dma_start(pos_i[:], a["positions"].rearrange("b (t p) -> (b t) p", p=P)).then_inc(ld_pos, 16)
            ends = a["positions"].rearrange("b (n s) -> (b n) s", s=CMP_STRIDE)[1:1 + N_CMP, CMP_STRIDE - 1:CMP_STRIDE]
            sp.dma_start(posc_i[:], ends, allow_slow_non_contiguous=True).then_inc(ld_posc, 16)
            sp.dma_start(rows_b1[:], a["moe_b1"].rearrange("l (g e) (m p) -> (l e m) g p", g=4, p=P)
                         ).then_inc(ld_b, 16)
            sp.dma_start(rows_b2[:], a["moe_b2"].rearrange("l (g e) (m p) -> (l e m) g p", g=2, p=P)
                         ).then_inc(ld_b, 16)
            F.load_products(sp)
            F.load_positions(sp)
            sp.wait_ge(ld_b, 32)

        @block.gpsimd
        def _(pool):
            pool.memset(C["ident"][:], 0.0).then_inc(zeroed, 1)
            pool.memset(C["ident_b"][:], 0.0).then_inc(zeroed, 1)
            pool.memset(C["causal"][:], 0.0).then_inc(zeroed, 1)
            pool.memset(C["far"][:], 0.0).then_inc(zeroed, 1)
            pool.memset(C["cmp_mask"][:], 0.0).then_inc(zeroed, 1)
            pool.memset(C["before"][:], 1.0).then_inc(zeroed, 1)
            pool.memset(C["ones_b"][:], 1.0).then_inc(zeroed, 1)
            pool.memset(C["late"][:], 1.0).then_inc(zeroed, 1)
            for j, f in enumerate(frequencies()):
                pool.memset(freq[:, j:j + 1], f).then_inc(fr, 1)
            pool.wait_ge(zeroed, 8)
            for t in ("ident", "ident_b"):
                pool.affine_select(out=C[t][:], in_=C[t][:], compare_op=ALU.not_equal, fill=1.0, base=0,
                                   pattern=[[-1, P]], channel_multiplier=1).then_inc(masks, 1)
            pool.affine_select(out=C["causal"][:], in_=C["causal"][:], compare_op=ALU.is_ge, fill=NEG, base=0,
                               pattern=[[-1, P]], channel_multiplier=1).then_inc(masks, 1)
            pool.affine_select(out=C["far"][:], in_=C["far"][:], compare_op=ALU.is_gt, fill=NEG, base=0,
                               pattern=[[1, P]], channel_multiplier=-1).then_inc(masks, 1)
            pool.affine_select(out=C["cmp_mask"][:], in_=C["cmp_mask"][:], compare_op=ALU.is_ge, fill=NEG,
                               base=-(CMP_BLOCK - 1), pattern=[[P, NT], [-CMP_STRIDE, 64]],
                               channel_multiplier=1).then_inc(masks, 1)
            pool.affine_select(out=C["before"][:], in_=C["before"][:], compare_op=ALU.is_gt, fill=0.0, base=0,
                               pattern=[[1, P]], channel_multiplier=-1).then_inc(masks, 1)
            pool.affine_select(out=C["late"][:], in_=C["late"][:], compare_op=ALU.is_ge, fill=0.0,
                               base=-(CMP_BLOCK - 1), pattern=[[0, 1]], channel_multiplier=1).then_inc(masks, 1)
            pool.iota(C["iota_i"][:], [[1, CAP]], base=0, channel_multiplier=0).then_inc(masks, 1)
            pool.iota(C["iota_p_i"][:], [[0, 1]], base=0, channel_multiplier=1).then_inc(masks, 1)
            pool.iota(C["iota_t_i"][:], [[1, NT]], base=0, channel_multiplier=0).then_inc(masks, 1)
            pool.wait_ge(masks, 10)

        @block.tensor
        def _(pe):
            pe.wait_ge(masks, 10)
            pe.wait_ge(ld_rows, 64)
            pe.wait_ge(own, 1)
            nc.tensor.transpose(pS[0][:, 0, 0:19], rows[:], C["ident"][0:19, 0:19])
            nc.tensor.transpose(pS[0][:, 1, 0:NT], pos_r[:], C["ident"][0:NT, 0:NT]).then_inc(tr, 1)
            pe.wait_ge(ld_b, 32)
            for g in range(4):
                nc.tensor.transpose(pS[1][:, g, :], rows_b1[:, g, :], C["ident"][:])
            for g in range(2):
                last = nc.tensor.transpose(pS[2][:, g, :], rows_b2[:, g, :], C["ident"][:])
            last.then_inc(tr, 1)

        @block.vector
        def _(dve):
            S = Steps(own)
            dve.wait_ge(ld_pos, 16)
            S.mark(nc.vector.tensor_copy(pos_r[:], pos_i[:]))
            S.mark(nc.vector.memset(posp[:], 0.0))
            dve.wait_ge(ld_posc, 16)
            S.wait(dve)
            S.mark(nc.vector.tensor_copy(posp[0:N_CMP, NT:NT + 1], posc_i[:]))
            dve.wait_ge(tr, 1)
            S.mark(nc.vector.tensor_copy(C["vec"][:], pS[0][:, 0, 0:19]))
            S.mark(nc.vector.tensor_copy(posp[:, 0:NT], pS[0][:, 1, 0:NT]))
            dve.wait_ge(masks, 10)
            S.mark(nc.vector.tensor_copy(C["iota"][:], C["iota_i"][:]))
            S.mark(nc.vector.tensor_copy(C["iota_p"][:], C["iota_p_i"][:]))
            S.mark(nc.vector.tensor_copy(C["iota_t"][:], C["iota_t_i"][:]))
            dve.wait_ge(tr, 2)
            S.mark(nc.vector.tensor_copy(C["b1"][:], pS[1][:]))
            S.mark(nc.vector.tensor_copy(C["b2"][:], pS[2][:, 0:2, :]))
            dve.wait_ge(fr, NF)
            S.wait(dve)
            S.mark(nc.vector.tensor_tensor(ang[:], posp[:].unsqueeze(2).to_broadcast([P, NT + 1, NF]),
                                           freq[:].unsqueeze(1).to_broadcast([P, NT + 1, NF]), ALU.mult))
            S.wait(dve)
            S.mark(nc.vector.tensor_scalar(turns[:, 0], ang[:], 1.0 / TWO_PI, None, ALU.mult))
            S.mark(nc.vector.tensor_scalar(turns[:, 1], ang[:], 1.0 / TWO_PI, 0.25, ALU.mult, ALU.add))
            for k in (ROUND, -ROUND):
                S.wait(dve)
                S.mark(nc.vector.tensor_scalar(turns[:], turns[:], k, None, ALU.add))
            S.wait(dve)
            for j in range(2):
                S.mark(nc.vector.scalar_tensor_tensor(red[:, j], turns[:, j], -C1, ang[:], ALU.mult, ALU.add))
            for k in (C2, C3):
                S.wait(dve)
                S.mark(nc.vector.scalar_tensor_tensor(red[:], turns[:], -k, red[:], ALU.mult, ALU.add))
            S.wait(dve)
            S.mark(nc.vector.tensor_scalar(red[:, 1], red[:, 1], float(np.pi / 2), None, ALU.add))
            S.wait(dve)
            S.mark(nc.vector.tensor_scalar(red[:], red[:], PI_IN, -PI_IN, ALU.min, ALU.max))
            S.wait(dve)
            dve.sem_inc(table, 1)

        @block.scalar
        def _(act):
            act.wait_ge(table, 1)
            nc.scalar.activation(C["trig"][:], red[:], ACT.Sin).then_inc(ev, 1)
            act.wait_ge(ev, 1)


def rope(nc, dve, S, x, heads, r0, half, sin, cos, t1, t2):
    p = x.shape[0]
    n = p, heads, 2, half
    xr = x[:, :, r0:r0 + 2 * half].rearrange("p h (two f) -> p h two f", two=2)
    c = cos.unsqueeze(1).unsqueeze(1).to_broadcast([*n])
    s = sin.unsqueeze(1).to_broadcast([p, heads, half])
    S.wait(dve)
    S.mark(nc.vector.tensor_tensor(t1, xr, c, ALU.mult))
    S.mark(nc.vector.tensor_tensor(t2[:, :, 0, :], xr[:, :, 1, :], s, ALU.mult))
    S.mark(nc.vector.tensor_tensor(t2[:, :, 1, :], xr[:, :, 0, :], s, ALU.mult))
    S.wait(dve)
    S.mark(nc.vector.tensor_tensor(xr[:, :, 0, :], t1[:, :, 0, :], t2[:, :, 0, :], ALU.subtract))
    S.mark(nc.vector.tensor_tensor(xr[:, :, 1, :], t1[:, :, 1, :], t2[:, :, 1, :], ALU.add))


PROJ = ((C_Q, C_QN), (C_KC, C_KW), (C_KW, IN_COLS), (C_QN, C_KC))
WHOLE = 2
PROJ_ACT, PROJ_DVE = 12, 14


def project(nc, C, R, F, a):
    with ExitStack() as ctx:
        M = Mem(nc, ctx, C["sems"])
        w_in, x_t, w_loaded, x_loaded, x_rows = F.w_in, F.x_t, F.w_loaded, F.x_loaded, F.x_rows
        xs = M.sb("xs", [P, D])
        junk = M.sb("junk", [P, D], BF16)
        uT = M.sb("uT", [P, KT, P])
        HALVES = (slice(0, 4), slice(4, 8))
        u_hi, u_lo = M.sb("u_hi", [P, KT, P], F32R), M.sb("u_lo", [P, KT, P], F32R)
        w_hi, w_lo = ({i: M.sb(f"w_{n}{i}", [P, KT, PROJ[i][1] - PROJ[i][0]], F32R) for i in range(WHOLE, 4)}
                      for n in ("hi", "lo"))
        halves_of_w = [(i, ks) for i in range(WHOLE, 4) for ks in HALVES]
        lat = M.sb("lat", [P, Q_RANK + KV_RANK])
        stage = M.sb("stage", [P, 12, DH])
        raw = M.sb("raw", [P, 4, 2, DH])
        ss, rec, rstd = M.sb("ss", [P, 1]), M.sb("rec", [P, 1]), M.sb("rstd", [P, 1])
        ss2, rec2, rstd2 = M.sb("ss2", [P, 2]), M.sb("rec2", [P, 2]), M.sb("rstd2", [P, 2])
        t1, t2 = M.sb("t1", [P, 12, 2, 8]), M.sb("t2", [P, 12, 2, 8])
        t3, t4 = M.sb("t3", [P, 1, 2, 16]), M.sb("t4", [P, 1, 2, 16])
        pe_t = M.sb("pe_t", [P, 1, ROPE])
        sig = M.sb("sig", [P, 1])
        pX = [M.ps(f"pX{i}", [P, 4, P]) for i in range(2)]
        pJ = [M.ps(f"pJ{i}", [P, 512]) for i in range(4)]
        pY = [M.ps(f"pY{i}", [P, 4, P]) for i in range(2)]
        xs_ready, x_turned, u_ready = (M.sem("p_" + s) for s in ("xs", "xt", "u"))
        sq_ready, rec_ready = M.sem("p_sq"), M.sem("p_rec")
        lsq_ready, lrec_ready = M.sem("p_lsq"), M.sem("p_lrec")
        product, copied, lat_ready, roped = (M.sem("p_" + s) for s in ("prod", "copied", "lat", "roped"))
        y_turned, y_dve, y_act = M.sem("p_yt"), M.sem("p_yd"), M.sem("p_ya")
        own_act, own_dve, passed = M.sem("p_oa"), M.sem("p_od"), M.sem("p_passed")
        zero, gates_ready = M.sem("p_zero"), M.sem("p_gates")
        u_parts, w_rounded, w_split = M.sem("p_up"), M.sem("p_whi"), M.sem("p_wlo")
        block = ctx.enter_context(nc.Block())

        @block.sync
        def _(sp):
            with sp.Fori(1, NT) as t:
                sp.wait_ge(xs_ready, t)
                sp.dma_start(x_t[:], x_rows[bass.ds(t, 1)].rearrange("a p d -> (a p) d")).then_inc(x_loaded, 16)
            sp.wait_ge(product, 4 * (NT - 1) + WHOLE)
            F.load_compress(sp)

        @block.gpsimd
        def _(pool):
            def parts(t, first=False):
                if not first:
                    hold(pool, product, 4 * t, passed)
                for h, ks in enumerate(HALVES):
                    hold(pool, u_ready, 2 * t + 1 + h, passed)
                    pool.tensor_copy(u_hi[:, ks], uT[:, ks]).then_inc(u_parts, 1)
                    hold(pool, u_parts, 4 * t + 2 * h + 1, passed)
                    pool.tensor_tensor(u_lo[:, ks], uT[:, ks], u_hi[:, ks].bitcast(F32), ALU.subtract
                                       ).then_inc(u_parts, 1)
                    hold(pool, u_parts, 4 * t + 2 * h + 2, passed)
            parts(0, True)
            pool.memset(R["nsaT"][64:96, :, :], 0.0).then_inc(zero, 1)
            pool.wait_ge(zero, 1)
            with pool.Fori(1, NT) as t:
                parts(t)

        @block.tensor
        def _(pe):
            def turn_x(t, first=False):
                pe.wait_ge(xs_ready, t + 1)
                if not first:
                    pe.wait_ge(u_ready, 2 * t)
                for k in range(KT):
                    last = nc.tensor.transpose(pX[k // 4][:, k % 4, :], xs[:, k * P:(k + 1) * P], C["ident"][:])
                    if k % 4 == 3:
                        last.then_inc(x_turned, 1)

            def products(t, first=False, final=False):
                for i, (c0, c1) in enumerate(PROJ):
                    if i == 3 and not final:
                        turn_x(t + 1)
                    if not first:
                        pe.wait_ge(copied, 4 * t - 3 + i)
                    elif i < WHOLE:
                        pe.wait_ge(w_loaded[i], 16)
                    for k in range(KT):
                        if i == 0 and k % 4 == 0:
                            pe.wait_ge(u_ready, 2 * t + 1 + k // 4)
                        if i < WHOLE:
                            last = nc.tensor.matmul(pJ[i][:, 0:c1 - c0], uT[:, k, :], w_in[i][:, k, :],
                                                    start=(k == 0), stop=(k == KT - 1))
                            continue
                        if k % 4 == 0:
                            if i == WHOLE:
                                pe.wait_ge(u_parts, 4 * t + 2 + k // 2)
                            if first:
                                pe.wait_ge(w_rounded, 2 * (i - WHOLE) + 1 + k // 4)
                                pe.wait_ge(w_split, 2 * (i - WHOLE) + 1 + k // 4)
                        for j, (u, w) in enumerate(((u_hi, w_hi[i]), (u_hi, w_lo[i]), (u_lo, w_hi[i]))):
                            last = nc.tensor.matmul(pJ[i][:, 0:c1 - c0], u[:, k, :], w[:, k, :],
                                                    start=(k == 0 and j == 0),
                                                    stop=(k == KT - 1 and j == 2))
                    last.then_inc(product, 1)
                    if i < 3 and not first:
                        turn_y(t - 1, ((0, 1), (2, 3), (4,))[i])

            def turn_y(t, groups):
                for g in groups:
                    if g == 0:
                        pe.wait_ge(lat_ready, t + 1)
                    if g == 1:
                        hold(pe, roped, t + 1, passed)
                    if g % 2 == 0:
                        hold(pe, y_dve, 3 * t + 1 + g // 2, passed)
                    else:
                        hold(pe, y_act, 2 * t + 1 + g // 2, passed)
                    for j in range(3 if g == 0 else 4):
                        if g == 0:
                            turned, of = pY[0][:, j, :], lat[:, j * P:(j + 1) * P]
                        elif g == 4:
                            turned, of = pY[0][:, j, :], raw[:, j].rearrange("p r d -> p (r d)")
                        else:
                            turned, of = pY[g % 2][0:DH, j, :], stage[:, 4 * g - 4 + j, :]
                        last = nc.tensor.transpose(turned, of, C["ident"][:])
                    last.then_inc(y_turned, 1)

            pe.sem_inc(y_dve, 1)
            pe.sem_inc(y_act, 1)
            turn_x(0, True)
            products(0, True)
            with pe.Fori(1, NT - 1) as t:
                products(t)
            products(NT - 1, final=True)
            turn_y(NT - 1, range(5))

        @block.scalar
        def _(act):
            def before(t, S, first=False):
                act.wait_ge(x_loaded, 16 * t + 16)
                nc.scalar.activation(junk[:], x_t[:], ACT.Square, accum_out=ss[:]).then_inc(sq_ready, 1)
                act.wait_ge(rec_ready, t + 1)
                S.mark(nc.scalar.activation(rstd[:], rec[:], ACT.Sqrt))
                if not first:
                    act.wait_ge(x_turned, 2 * t)
                S.wait(act)
                nc.scalar.activation(xs[:], x_t[:], ACT.Copy, scale=rstd[:]).then_inc(xs_ready, 1)

            def after(t, S, first=False):
                act.wait_ge(product, 4 * t + 1)
                if not first:
                    act.wait_ge(y_turned, 5 * t)
                S.mark(nc.scalar.activation(junk[:, 0:Q_RANK], pJ[0][:, 0:Q_RANK], ACT.Square,
                                            accum_out=ss2[:, 0:1]))
                S.wait(act)
                nc.scalar.activation(junk[:, 0:KV_RANK], pJ[0][:, C_KV:C_PE], ACT.Square,
                                     accum_out=ss2[:, 1:2]).then_inc(lsq_ready, 1)
                if not first:
                    act.wait_ge(roped, t)
                S.mark(nc.scalar.activation(pe_t[:, 0, :], pJ[0][:, C_PE:C_QN], ACT.Copy))
                act.wait_ge(lrec_ready, t + 1)
                S.mark(nc.scalar.activation(rstd2[:], rec2[:], ACT.Sqrt))
                S.wait(act)
                S.mark(nc.scalar.activation(lat[:, 0:Q_RANK], pJ[0][:, 0:Q_RANK], ACT.Copy, scale=rstd2[:, 0:1]))
                S.mark(nc.scalar.activation(lat[:, Q_RANK:], pJ[0][:, C_KV:C_PE], ACT.Copy, scale=rstd2[:, 1:2]))
                S.wait(act)
                act.sem_inc(lat_ready, 1)
                act.sem_inc(copied, 1)
                act.wait_ge(product, 4 * t + 2)
                S.mark(nc.scalar.activation(
                    raw[:], pJ[1][:, 0:2 * KVW].rearrange("p (j d) -> p j d", d=DH).unsqueeze(2)
                    .to_broadcast([P, 4, 2, DH]), ACT.Copy))
                S.mark(nc.scalar.activation(stage[:, 8:10, :].rearrange("p j d -> p (j d)"),
                                            pJ[1][:, 2 * KVW:3 * KVW], ACT.Copy))
                S.mark(nc.scalar.activation(R["v_s"][:, bass.ds(t, 1), :].rearrange("p a c -> p (a c)"),
                                            pJ[1][:, 3 * KVW:4 * KVW], ACT.Copy))
                S.wait(act)
                act.sem_inc(copied, 1)
                act.wait_ge(product, 4 * t + 3)
                S.mark(nc.scalar.activation(stage[:, 10:12, :].rearrange("p j d -> p (j d)"),
                                            pJ[2][:, 0:KVW], ACT.Copy))
                S.mark(nc.scalar.activation(R["v_w"][:, bass.ds(t, 1), :].rearrange("p a c -> p (a c)"),
                                            pJ[2][:, KVW:2 * KVW], ACT.Copy))
                S.mark(nc.scalar.activation(R["gates"][:, bass.ds(t, 1), :].rearrange("p a c -> p (a c)"),
                                            pJ[2][:, 2 * KVW:2 * KVW + 3 * H_NSA], ACT.Copy))
                S.wait(act)
                act.sem_inc(copied, 1)
                act.wait_ge(product, 4 * t + 4)
                nc.scalar.activation(stage[:, 0:8, :].rearrange("p j d -> p (j d)"), pJ[3][:], ACT.Copy
                                     ).then_inc(copied, 1)

            def from_y(t):
                for n, g in enumerate((0, 2)):
                    act.wait_ge(y_turned, 5 * t + 2 + 2 * n)
                    nc.scalar.activation(R["nsaT"][0:DH, 4 * g:4 * g + 4, bass.ds(t * P, P)],
                                         pY[1][0:DH], ACT.Copy).then_inc(y_act, 1)

            S = Steps(own_act)
            before(0, S, True)
            before(1, S)
            for i, ks in halves_of_w:
                act.wait_ge(w_loaded[i], 16)
                nc.scalar.copy(w_hi[i][:, ks], w_in[i][:, ks]).then_inc(w_rounded, 1)
            after(0, S, True)
            from_y(0)
            n0 = S.n
            with act.Fori(1, NT - 1) as t:
                S = Steps(own_act, (t - 1) * PROJ_ACT + n0)
                before(t + 1, S)
                after(t, S)
                from_y(t)
            assert S.n == PROJ_ACT, S.n
            S = Steps(own_act, (NT - 2) * PROJ_ACT + n0)
            after(NT - 1, S)
            from_y(NT - 1)
            S.wait(act)
            S.mark(nc.scalar.activation(R["gates"][:], R["gates"][:], ACT.Sigmoid))
            S.wait(act)
            nc.scalar.activation(R["gates"][:, 0, 0:3 * H_NSA:3], R["gates"][:, 0, 0:3 * H_NSA:3], ACT.Copy,
                                 scale=C["late"][:]).then_inc(gates_ready, 1)
            act.wait_ge(gates_ready, 1)

        @block.vector
        def _(dve):
            def reciprocal(S, out, x, n):
                S.mark(nc.vector.tensor_scalar(out, x, 1.0 / n, EPS, ALU.mult, ALU.add))
                S.wait(dve)
                return nc.vector.reciprocal(out, out)

            def before(t, S):
                dve.wait_ge(sq_ready, t + 1)
                reciprocal(S, rec[:], ss[:], D).then_inc(rec_ready, 1)

            def turned(t, first=False):
                for i in range(2):
                    dve.wait_ge(x_turned, 2 * t + 1 + i)
                    if i == 0 and not first:
                        dve.wait_ge(product, 4 * t - 4 + WHOLE)
                        dve.wait_ge(u_parts, 4 * t)
                    nc.vector.tensor_tensor(uT[:, 4 * i:4 * i + 4, :], pX[i][:],
                                            C["vec"][:, 4 * i:4 * i + 4].unsqueeze(2).to_broadcast([P, 4, P]),
                                            ALU.mult).then_inc(u_ready, 1)

            def latents(t, S):
                dve.wait_ge(lsq_ready, t + 1)
                for i, n in enumerate((Q_RANK, KV_RANK)):
                    S.mark(nc.vector.tensor_scalar(rec2[:, i:i + 1], ss2[:, i:i + 1], 1.0 / n, EPS,
                                                   ALU.mult, ALU.add))
                S.wait(dve)
                nc.vector.reciprocal(rec2[:], rec2[:]).then_inc(lrec_ready, 1)
                dve.wait_ge(lat_ready, t + 1)
                sin, cos = (C["trig"][:, j, bass.ds(t, 1), :].rearrange("p a f -> p (a f)") for j in (0, 1))
                rope(nc, dve, S, pe_t[:], 1, 0, ROPE // 2, sin[:, 0:16], cos[:, 0:16], t3[:], t4[:])
                S.wait(dve)
                S.mark(nc.vector.tensor_copy(R["k_pe"][:, bass.ds(t, 1), :], pe_t[:]))

            def heads(t, S):
                sin, cos = (C["trig"][:, j, bass.ds(t, 1), :].rearrange("p a f -> p (a f)") for j in (0, 1))
                dve.wait_ge(copied, 4 * t + 4)
                rope(nc, dve, S, stage[:], 12, 0, ROPE_N // 2, sin[:, 16:24], cos[:, 16:24], t1[:], t2[:])
                S.wait(dve)
                dve.sem_inc(roped, 1)

            def early_y(t):
                dve.wait_ge(y_turned, 5 * t + 1)
                nc.vector.tensor_tensor(R["latT"][:, :, bass.ds(t * P, P)], pY[0][:, 0:3, :],
                                        C["vec"][:, 8:11].unsqueeze(2).to_broadcast([P, 3, P]),
                                        ALU.mult).then_inc(y_dve, 1)
                dve.wait_ge(y_turned, 5 * t + 3)
                nc.vector.tensor_copy(R["nsaT"][0:DH, 4:8, bass.ds(t * P, P)], pY[0][0:DH]).then_inc(y_dve, 1)

            def late_y(t):
                dve.wait_ge(y_turned, 5 * t + 5)
                nc.vector.tensor_copy(R["rawT"][:, :, bass.ds(t * P, P)], pY[0][:]).then_inc(y_dve, 1)

            def tile(t, S, last=False):
                latents(t, S)
                turned(t + 1)
                heads(t, S)
                early_y(t)
                if not last:
                    before(t + 2, S)
                late_y(t)

            S = Steps(own_dve)
            before(0, S)
            turned(0, True)
            before(1, S)
            for n, (i, ks) in enumerate(halves_of_w):
                dve.wait_ge(w_rounded, n + 1)
                nc.vector.tensor_tensor(w_lo[i][:, ks], w_in[i][:, ks], w_hi[i][:, ks].bitcast(F32), ALU.subtract
                                        ).then_inc(w_split, 1)
            tile(0, S)
            n0 = S.n
            with dve.Fori(1, NT - 2) as t:
                S = Steps(own_dve, (t - 1) * PROJ_DVE + n0)
                tile(t, S)
            assert S.n == PROJ_DVE, S.n
            S = Steps(own_dve, (NT - 3) * PROJ_DVE + n0)
            tile(NT - 2, S, True)
            latents(NT - 1, S)
            heads(NT - 1, S)
            early_y(NT - 1)
            late_y(NT - 1)


def compress(nc, C, R, F):
    LP = CMP_BLOCK // 2
    with ExitStack() as ctx:
        M = Mem(nc, ctx, C["sems"])
        w1, w2, pos = F.cmp_w1, F.cmp_w2, F.cmp_pos
        posT = M.sb("cposT", [P, 2, LP])
        blocks = M.sb("cblocks", [P, 2, LP, G_NSA, N_CMP])
        sg, hid = M.sb("csg", [P, 2, G_NSA * N_CMP]), M.sb("chid", [P, 2, G_NSA * N_CMP])
        kc = M.sb("ckc", [64, G_NSA, DH])
        t1, t2 = M.sb("ct1", [64, G_NSA, 2, 8]), M.sb("ct2", [64, G_NSA, 2, 8])
        pH = [M.ps(f"cpH{i}", [P, 512]) for i in range(2)]
        pO, pT = M.ps("cpO", [64, 4, DH]), M.ps("cpT", [P, 4, P])
        ld, ldp, turned, posT_ready = F.cmp_loaded, F.pos_loaded, M.sem("cc_turned"), M.sem("cc_posT")
        built, hid_ready, sg_ready, silu = M.sem("cc_built"), M.sem("cc_hid"), M.sem("cc_sg"), M.sem("cc_silu")
        out_ready, own, kc_ready, kc_turned = M.sem("cc_out"), M.sem("cc_own"), M.sem("cc_kc"), M.sem("cc_kct")
        zero, zero2 = M.sem("cc_zero"), M.sem("cc_zero2")
        block = ctx.enter_context(nc.Block())

        def windows(c, g):
            half = []
            for two in range(2):
                src = R["rawT"][64 * two:64 * two + 64, 2 * c + g, :]
                v = bass.AP(tensor=src.tensor, offset=src.offset + two,
                            ap=[list(src.ap[0]), [2, LP], [CMP_STRIDE, N_CMP]])
                half.append(v)
            return half

        def build(eng, c):
            for g in range(G_NSA):
                for two, v in enumerate(windows(c, g)):
                    h = slice(64 * two, 64 * two + 64)
                    eng.tensor_tensor(blocks[h, c, :, g, :], v,
                                      posT[h, c, :].unsqueeze(2).to_broadcast([64, LP, N_CMP]),
                                      ALU.add).then_inc(built, 1)

        @block.gpsimd
        def _(pool):
            for t in (kc, R["kcT"], R["v_c"]):
                pool.memset(t[:], 0.0).then_inc(zero, 1)
            pool.wait_ge(zero, 3)
            pool.sem_inc(zero2, 1)

        @block.vector
        def _(dve):
            S = Steps(own)
            dve.wait_ge(turned, 1)
            nc.vector.tensor_copy(posT[:], pT[:, 0, 0:2 * LP].rearrange("p (c l) -> p c l", c=2)
                                  ).then_inc(posT_ready, 1)
            dve.wait_ge(posT_ready, 1)
            build(nc.vector, 0)
            build(nc.vector, 1)
            for c in range(2):
                dve.wait_ge(sg_ready, c + 1)
                nc.vector.tensor_tensor(hid[:, c, :], pH[c][:, 0:G_NSA * N_CMP], sg[:, c, :], ALU.mult
                                        ).then_inc(silu, 1)
            dve.wait_ge(zero2, 1)
            dve.wait_ge(out_ready, 1)
            S.mark(nc.vector.tensor_copy(kc[0:N_CMP], pO[0:N_CMP, 0:2, :]))
            rope(nc, dve, S, kc[0:N_CMP], G_NSA, 0, ROPE_N // 2, C["trig"][0:N_CMP, 0, NT, 16:24],
                 C["trig"][0:N_CMP, 1, NT, 16:24], t1[0:N_CMP], t2[0:N_CMP])
            S.wait(dve)
            nc.vector.tensor_copy(R["v_c"][0:N_CMP], pO[0:N_CMP, 2:4, :]).then_inc(kc_ready, 1)
            dve.wait_ge(kc_turned, 1)
            nc.vector.tensor_copy(R["kcT"][0:DH], pT[0:DH, 1:3, 0:64]).then_inc(kc_ready, 1)
            dve.wait_ge(kc_ready, 2)

        @block.scalar
        def _(act):
            for c in range(2):
                act.wait_ge(hid_ready, c + 1)
                nc.scalar.activation(sg[:, c, :], pH[c][:, 0:G_NSA * N_CMP], ACT.Sigmoid).then_inc(sg_ready, 1)

        @block.tensor
        def _(pe):
            pe.wait_ge(ldp, 16)
            nc.tensor.transpose(pT[:, 0, 0:2 * LP], pos[:], C["ident"][0:2 * LP, 0:2 * LP]).then_inc(turned, 1)
            pe.wait_ge(ld, 48)
            for c in range(2):
                pe.wait_ge(built, 4 * c + 4)
                for lp in range(LP):
                    last = nc.tensor.matmul(pH[c][:, 0:G_NSA * N_CMP], w1[:, c, lp, :],
                                            blocks[:, c, lp].rearrange("p g n -> p (g n)"),
                                            start=(lp == 0), stop=(lp == LP - 1))
                last.then_inc(hid_ready, 1)
            pe.wait_ge(silu, 2)
            for c in range(2):
                for g in range(G_NSA):
                    last = nc.tensor.matmul(pO[0:N_CMP, 2 * c + g, :], hid[:, c, g * N_CMP:(g + 1) * N_CMP],
                                            w2[:, c, :], start=True, stop=True)
            last.then_inc(out_ready, 1)
            pe.wait_ge(kc_ready, 1)
            for g in range(G_NSA):
                last = nc.tensor.transpose(pT[0:DH, 1 + g, 0:64], kc[:, g, :], C["ident"][0:64, 0:64])
            last.then_inc(kc_turned, 1)


QG = 4
RING = 5
LAG = 4


class Unit:

    def __init__(self, kind, pair, qg, head, i):
        self.kind, self.pair, self.qg, self.head, self.i = kind, pair, qg, head, i
        if kind == "win":
            self.k0 = max(0, i - WT)
            w = (i + 1 - self.k0) * P
            self.spans = [(0, w, 0), ((WT + 1) * P, (WT + 1) * P + 64, 1)]
            pieces = [(P * j, P, self.k0 + j) for j in range(i + 1 - self.k0)] + [((WT + 1) * P, 64, None)]
        else:
            self.k0 = 0
            w = (i + 1) * P
            self.spans = [(0, w, 0)]
            pieces = [(P * j, P, j) for j in range(i + 1)]
        self.width = w
        self.banks = [pieces[j:j + 4] for j in range(0, len(pieces), 4)]


def plan(kinds, pairs):
    units, first, groups = [], [], []
    for pair in range(pairs):
        for qg in range(NT // QG):
            for kind in kinds:
                for i in range(QG * qg, QG * qg + QG):
                    for head in range(2):
                        first.append(sum(len(u.banks) for u in units))
                        units.append(Unit(kind, pair, qg, head, i))
                groups.append((len(units) - 1, kind, pair, qg))
    return units, first, groups


def value_tiles(kind, qg):
    q0, q1 = QG * qg, QG * qg + QG
    if kind == "win":
        return [(k, max(k, q0), min(k + WT + 1, q1)) for k in range(max(0, q0 - WT), q1)]
    return [(k, max(k, q0), q1) for k in range(q1)]


class Attention:

    def __init__(self, nc, M, C, R, name, kinds, pairs, prep, gated):
        self.nc, self.C, self.R, self.kinds, self.gated = nc, C, R, kinds, gated
        self.units, self.first, self.groups = plan(kinds, pairs)
        self.OUTS = 2 * pairs
        self.U, self.NG = len(self.units), len(self.groups)
        self.prep = prep
        banks = prep + sum(len(u.banks) for u in self.units)
        assert banks % 2 == 0 and prep % 2 == 0
        self.half = banks // 2
        self.probs = M.sb(name + "probs", [P, RING, SEQ])
        self.probsT = M.sb(name + "probsT", [P, 2, NT, QG * P])
        self.negmax = M.sb(name + "negmax", [P, RING, 2])
        self.sums = M.sb(name + "sums", [P, RING, 2])
        self.weight = M.sb(name + "weight", [P, RING, 2])
        self.pS = [M.ps(f"{name}pS{i}", [P, SEQ]) for i in range(2)]
        self.pT = [M.ps(f"{name}pT{i}", [P, 4, P]) for i in range(2)]
        self.pO = [M.ps(f"{name}pO{i}", [P, QG * P]) for i in range(2)]
        s = lambda x: M.sem(name + x)
        self.staged = s("staged")
        self.scored, self.maxed, self.exped, self.inverted = s("scored"), s("maxed"), s("exped"), s("inv")
        self.scaled = s("scaled")
        self.bank_turned = [s("bt0"), s("bt1")]
        self.bank_read = [s("br0"), s("br1")]
        self.valued, self.out_read = s("valued"), s("outd")
        self.passed = s("passed")

    FREE_BANK, FREE_SCORES, FREE_OUT, FREE_VALUED, NO_BANK = 1, 2, 2, 1, 1

    def start(self, pe):
        for b in range(2):
            pe.sem_inc(self.bank_read[b], self.FREE_BANK)
            pe.sem_inc(self.bank_turned[b], self.NO_BANK)
        pe.sem_inc(self.exped, self.FREE_SCORES)
        pe.sem_inc(self.out_read, self.FREE_OUT)
        pe.sem_inc(self.valued, self.FREE_VALUED)

    def wait_bank(self, pe, it, seq):
        pe.wait_ge(self.bank_read[seq % 2], it * self.half + seq // 2 + self.FREE_BANK)

    def wait_turned(self, eng, it, seq):
        eng.wait_ge(self.bank_turned[seq % 2], it * self.half + seq // 2 + 1 + self.NO_BANK)

    def scores(self, pe, it, n):
        nc, C, u, pS = self.nc, self.C, self.units[n], self.pS[n % 2]
        pe.wait_ge(self.exped, it * self.U + n + 1)
        q = self.queries(u)
        for c0 in range(0, u.width, 512):
            c1 = min(c0 + 512, u.width)
            diag = u.width - P >= c0 and u.width - P < c1
            far = u.kind == "win" and u.i >= WT and c0 == 0
            nc.tensor.matmul(pS[:, c0:c1], q, self.keys(u, u.k0 * P + c0, u.k0 * P + c1), start=True,
                             stop=not (diag or far))
            if far:
                nc.tensor.matmul(pS[:, 0:P], C["ident_b"][:], C["far"][:], start=False, stop=not diag)
            if diag:
                last = nc.tensor.matmul(pS[:, u.width - P:u.width], C["ident_b"][:], C["causal"][:],
                                        start=False, stop=True)
        if u.kind == "win":
            c0 = (WT + 1) * P
            nc.tensor.matmul(pS[:, c0:c0 + 64], q, self.keys(u, None, None), start=True, stop=False)
            last = nc.tensor.matmul(pS[:, c0:c0 + 64], C["ident_b"][:], C["cmp_mask"][:, u.i, :],
                                    start=False, stop=True)
        last.then_inc(self.scored, 1)

    def turn(self, pe, it, n):
        nc, u = self.nc, self.units[n]
        pe.wait_ge(self.scaled, it * self.U + n + 1)
        for j, pieces in enumerate(u.banks):
            seq = self.prep + self.first[n] + j
            self.wait_bank(pe, it, seq)
            if pieces[0][1] != P:
                pe.sem_inc(self.passed, 1)
            for k, (col, rows, _) in enumerate(pieces):
                last = nc.tensor.transpose(self.pT[seq % 2][0:rows, k, :], self.probs[:, n % RING, col:col + rows],
                                           self.C["ident"][:])
            last.then_inc(self.bank_turned[seq % 2], 1)

    def values(self, pe, it, g):
        nc, (n, kind, pair, qg) = self.nc, self.groups[g]
        opening, closing = kind == self.kinds[0], kind == self.kinds[-1]
        seqs = self.prep + self.first[n] + len(self.units[n].banks)
        for b in range(2):
            pe.wait_ge(self.bank_read[b], it * self.half + (seqs + 1 - b) // 2 + self.FREE_BANK)
        if opening:
            pe.wait_ge(self.out_read, self.OUTS * it + 2 * pair + qg - 1 + self.FREE_OUT)
        tiles = value_tiles(kind, qg)
        for j, (k, i0, i1) in enumerate(tiles):
            c0, c1 = (i0 - QG * qg) * P, (i1 - QG * qg) * P
            end = closing and kind != "win" and j == len(tiles) - 1
            for h in range(2):
                last = nc.tensor.matmul(self.pO[qg][64 * h:64 * h + 64, c0:c1], self.value(kind, k, h),
                                        self.probsT[:, h, k, c0:c1], start=opening and j == 0, stop=end)
        if kind == "win":
            for h in range(2):
                last = nc.tensor.matmul(self.pO[qg][64 * h:64 * h + 64, :], self.value("cmp", 0, h),
                                        self.cmpT[:, h, :], start=False, stop=True)
        last.then_inc(self.valued, 1)

    def tensor(self, pe, it):
        for s in range(self.U + LAG + 1):
            if LAG <= s < self.U + LAG:
                self.turn(pe, it, s - LAG)
            if s < self.U:
                self.scores(pe, it, s)
            for g, (n, *_) in enumerate(self.groups):
                if n == s - LAG - 1:
                    self.values(pe, it, g)

    def read_banks(self, eng, copy, it, n, parity):
        u = self.units[n]
        group = next(g for g, (m, *_) in enumerate(self.groups) if n <= m)
        for j, pieces in enumerate(u.banks):
            seq = self.prep + self.first[n] + j
            if seq % 2 != parity:
                continue
            eng.wait_ge(self.valued, it * self.NG + group + self.FREE_VALUED)
            self.wait_turned(eng, it, seq)
            c = (u.i % QG) * P
            full = [x for x in pieces if x[1] == P]
            k0 = full[0][2] if full else 0
            if full:
                last = copy(self.probsT[:, u.head, k0:k0 + len(full), c:c + P], self.pT[seq % 2][:, 0:len(full), :])
            if len(full) < len(pieces):
                last = copy(self.cmpT[0:64, u.head, c:c + P], self.pT[seq % 2][0:64, len(full), :])
            last.then_inc(self.bank_read[seq % 2], 1)

    def scalar(self, act, it, out_tile):
        nc = self.nc
        for s in range(self.U + LAG + 2):
            if LAG <= s < self.U + LAG:
                self.read_banks(act, nc.scalar.copy, it, s - LAG, 0)
            for g, (n, kind, pair, qg) in enumerate(self.groups):
                if n == s - LAG - 2 and kind == self.kinds[-1]:
                    act.wait_ge(self.valued, it * self.NG + g + 1 + self.FREE_VALUED)
                    nc.scalar.copy(out_tile(pair)[:, :, qg * QG * P:(qg + 1) * QG * P].rearrange("p a q -> p (a q)"),
                                   self.pO[qg][:]).then_inc(self.out_read, 1)
            if 1 <= s <= self.U:
                n = s - 1
                act.wait_ge(self.maxed, it * self.U + n + 1)
                if n >= RING:
                    self.wait_turned(act, it, self.prep + self.first[n - RING] + len(self.units[n - RING].banks) - 1)
                else:
                    for b in range(2):
                        act.wait_ge(self.bank_turned[b], it * self.half + self.NO_BANK)
                for c0, c1, k in self.units[n].spans:
                    last = nc.scalar.activation(self.probs[:, n % RING, c0:c1], self.pS[n % 2][:, c0:c1], ACT.Exp,
                                                bias=self.negmax[:, n % RING, k:k + 1],
                                                accum_out=self.sums[:, n % RING, k:k + 1])
                last.then_inc(self.exped, 1)

    def vector(self, dve, it):
        nc, per = self.nc, 2 if self.gated else 1
        for s in range(self.U + LAG):
            scaling = 2 <= s < self.U + 2
            if scaling and self.gated:
                n = s - 2
                w = self.weight[:, n % RING, 0:len(self.units[n].spans)]
                dve.wait_ge(self.inverted, 2 * (it * self.U + n) + 1)
                nc.vector.tensor_tensor(w, w, self.gate(self.units[n]), ALU.mult).then_inc(self.inverted, 1)
            if s >= LAG:
                self.read_banks(dve, nc.vector.tensor_copy, it, s - LAG, 1)
            if scaling:
                n = s - 2
                dve.wait_ge(self.inverted, per * (it * self.U + n + 1))
                for c0, c1, k in self.units[n].spans:
                    last = nc.vector.tensor_scalar(self.probs[:, n % RING, c0:c1], self.probs[:, n % RING, c0:c1],
                                                   self.weight[:, n % RING, k:k + 1], None, ALU.mult)
                last.then_inc(self.scaled, 1)
            if s < self.U:
                dve.wait_ge(self.scored, it * self.U + s + 1)
                for c0, c1, k in self.units[s].spans:
                    last = nc.vector.tensor_reduce(self.negmax[:, s % RING, k:k + 1], self.pS[s % 2][:, c0:c1],
                                                   AX_X, ALU.max, negate=True)
                last.then_inc(self.maxed, 1)
            if 1 <= s <= self.U:
                n = s - 1
                spans = len(self.units[n].spans)
                dve.wait_ge(self.exped, it * self.U + n + 1 + self.FREE_SCORES)
                nc.vector.reciprocal(self.weight[:, n % RING, 0:spans], self.sums[:, n % RING, 0:spans]
                                     ).then_inc(self.inverted, 1)


def mla(nc, C, R, a):
    scale = QK_MLA ** -0.5
    ROPES = 5
    with ExitStack() as ctx:
        M = Mem(nc, ctx, C["sems"])
        A = Attention(nc, M, C, R, "m_", ("mla",), 1, NT, False)
        wq = M.sb("m_wq", [P, Q_RANK // P, 2 * QK_MLA])
        wkv = M.sb("m_wkv", [P, 2 * (NOPE + V_DIM)])
        stage = M.sb("m_stage", [P, 2, 4, QK_MLA])
        qkT = M.sb("m_qkT", [QK_MLA, 4, SEQ])
        v = M.sb("m_v", [P, NT, 2, V_DIM])
        t1, t2 = M.sb("m_t1", [P, 2, 2, 16]), M.sb("m_t2", [P, 2, 2, 16])
        loaded, product, copied, roped, own = (M.sem("m_" + s) for s in ("ld", "prod", "copied", "roped", "own"))
        A.queries = lambda u: qkT[:, u.head, u.i * P:(u.i + 1) * P]
        A.keys = lambda u, c0, c1: qkT[:, 2 + u.head, c0:c1]
        A.value = lambda kind, k, h: v[:, k, h, :]
        PAIRS = H_MLA // 2
        block = ctx.enter_context(nc.Block())

        @block.sync
        def _(sp):
            def load(it):
                sp.dma_start(wq[:], a["mla_w_q_up"].rearrange("l (k p) (a c) -> (l p) k a c", p=P, a=PAIRS)
                             [:, :, bass.ds(it, 1), :].rearrange("p k a c -> p k (a c)")).then_inc(loaded, 16)
                sp.dma_start(wkv[:], a["mla_w_kv_up"].rearrange("l p (a c) -> (l p) a c", a=PAIRS)
                             [:, bass.ds(it, 1), :].rearrange("p a c -> p (a c)")).then_inc(loaded, 16)
            load(0)
            with sp.Fori(1, PAIRS) as it:
                sp.wait_ge(product, NT * it)
                load(it)

        @block.tensor
        def _(pe):
            A.start(pe)
            pe.sem_inc(copied, 1)
            with pe.Fori(0, PAIRS) as it:
                pe.wait_ge(loaded, 32 * it + 32)
                pe.wait_ge(A.exped, it * A.U + A.FREE_SCORES)
                for j in range(NT + 1):
                    if j < NT:
                        b = A.pS[j % 2]
                        pe.wait_ge(copied, NT * it + max(j - 1, 0) + 1)
                        for k in range(Q_RANK // P):
                            nc.tensor.matmul(b[:, 0:2 * QK_MLA], R["latT"][:, k, j * P:(j + 1) * P], wq[:, k, :],
                                             start=(k == 0), stop=(k == Q_RANK // P - 1))
                        nc.tensor.matmul(b[:, 512:768], R["latT"][:, 2, j * P:(j + 1) * P], wkv[:],
                                         start=True, stop=True).then_inc(product, 1)
                    if j >= 1:
                        pe.wait_ge(roped, NT * it + j)
                        A.wait_bank(pe, it, j - 1)
                        for k in range(4):
                            last = nc.tensor.transpose(A.pT[(j - 1) % 2][0:QK_MLA, k, :], stage[:, (j - 1) % 2, k, :],
                                                       C["ident"][:])
                        last.then_inc(A.bank_turned[(j - 1) % 2], 1)
                for b in range(2):
                    pe.wait_ge(A.bank_read[b], it * A.half + NT // 2 + A.FREE_BANK)
                A.tensor(pe, it)

        @block.scalar
        def _(act):
            with act.Fori(0, PAIRS) as it:
                for j in range(NT):
                    b = A.pS[j % 2]
                    act.wait_ge(product, NT * it + j + 1)
                    if j >= 2:
                        A.wait_turned(act, it, j - 2)
                    nc.scalar.activation(stage[:, j % 2, 0:2, :].rearrange("p h c -> p (h c)"), b[:, 0:2 * QK_MLA],
                                         ACT.Copy, scale=scale).then_inc(copied, 1)
                    if j % 2 == 0 and j >= 2:
                        A.wait_turned(act, it, j - 2)
                        nc.scalar.copy(qkT[:, :, (j - 2) * P:(j - 1) * P], A.pT[0][0:QK_MLA]).then_inc(A.bank_read[0], 1)
                A.wait_turned(act, it, NT - 2)
                nc.scalar.copy(qkT[:, :, (NT - 2) * P:(NT - 1) * P], A.pT[0][0:QK_MLA]).then_inc(A.bank_read[0], 1)
                A.scalar(act, it, lambda pair: R["mixT"][:, bass.ds(it, 1), :])

        @block.vector
        def _(dve):
            with dve.Fori(0, PAIRS) as it:
                S = Steps(own, it * ROPES * NT)
                for j in range(NT):
                    b = A.pS[j % 2]
                    dve.wait_ge(product, NT * it + j + 1)
                    if j >= 2:
                        A.wait_turned(dve, it, j - 2)
                    nc.vector.tensor_copy(stage[:, j % 2, 2:4, 0:NOPE],
                                          b[:, 512:768].rearrange("p (h c) -> p h c", h=2)[:, :, 0:NOPE])
                    nc.vector.tensor_copy(v[:, j], b[:, 512:768].rearrange("p (h c) -> p h c", h=2)[:, :, NOPE:])
                    nc.vector.tensor_copy(stage[:, j % 2, 2:4, NOPE:],
                                          R["k_pe"][:, j:j + 1, :].to_broadcast([P, 2, ROPE]))
                    dve.wait_ge(copied, NT * it + j + 2)
                    rope(nc, dve, S, stage[:, j % 2, 0:2, :], 2, NOPE, ROPE // 2, C["trig"][:, 0, j, 0:16],
                         C["trig"][:, 1, j, 0:16], t1[:], t2[:])
                    S.wait(dve)
                    dve.sem_inc(roped, 1)
                    if j % 2 == 1 and j >= 3:
                        A.wait_turned(dve, it, j - 2)
                        nc.vector.tensor_copy(qkT[:, :, (j - 2) * P:(j - 1) * P], A.pT[1][0:QK_MLA]
                                              ).then_inc(A.bank_read[1], 1)
                assert S.n == ROPES * NT
                A.wait_turned(dve, it, NT - 1)
                nc.vector.tensor_copy(qkT[:, :, (NT - 1) * P:], A.pT[1][0:QK_MLA]).then_inc(A.bank_read[1], 1)
                A.vector(dve, it)


def nsa(nc, C, R, w_out):
    PER_G = H_NSA // G_NSA // 2
    with ExitStack() as ctx:
        M = Mem(nc, ctx, C["sems"])
        A = Attention(nc, M, C, R, "n_", ("sel", "win"), PER_G, 0, True)
        A.cmpT = M.sb("n_cmpT", [P, 2, QG * P])
        q = M.sb("n_q", [96, 2 * PER_G, SEQ])
        k = M.sb("n_k", [96, 2, SEQ])
        kc = M.sb("n_kc", [96, 64])
        v = M.sb("n_v", [P, 2, NT, DH])
        vc = M.sb("n_vc", [P, DH])
        gp = M.sb("n_g", [P, NT, 2 * PER_G, 3])
        q_staged, k_staged, v_staged, g_staged, zero, copied, passed = (
            M.sem("n_" + s) for s in ("q", "k", "v", "g", "z", "copied", "n_passed"))
        A.queries = lambda u: q[:, 2 * u.pair + u.head, u.i * P:(u.i + 1) * P]
        A.keys = lambda u, c0, c1: kc[:] if c0 is None else k[:, 0 if u.kind == "sel" else 1, c0:c1]
        A.value = lambda kind, t, h: vc[:] if kind == "cmp" else v[:, 0 if kind == "sel" else 1, t, :]
        A.gate = lambda u: gp[:, u.i, 2 * u.pair + u.head, 2 if u.kind == "sel" else 0:][:, 0:len(u.spans)]
        block = ctx.enter_context(nc.Block())

        @block.sync
        def _(sp):
            w_out.load(sp, range(2))

        @block.gpsimd
        def _(pool):
            pool.memset(A.cmpT[64:128], 0.0).then_inc(zero, 1)
            pool.wait_ge(zero, 1)
            pool.memset(vc[64:128], 0.0).then_inc(zero, 1)
            pool.wait_ge(zero, 2)
            with pool.Fori(0, G_NSA) as g:
                pool.wait_ge(A.valued, g * A.NG + A.FREE_VALUED)
                pool.tensor_copy(v[:, 0], R["v_s"][:, :, bass.ds(g * DH, DH)]).then_inc(copied, 1)
                pool.wait_ge(copied, 2 * g + 1)
                pool.tensor_copy(v[:, 1], R["v_w"][:, :, bass.ds(g * DH, DH)]).then_inc(copied, 1)
                pool.wait_ge(copied, 2 * g + 2)
                pool.tensor_copy(vc[0:64].rearrange("p (a d) -> p a d", a=1), R["v_c"][:, bass.ds(g, 1), :]
                                 ).then_inc(v_staged, 1)

        @block.tensor
        def _(pe):
            A.start(pe)
            pe.wait_ge(zero, 2)
            with pe.Fori(0, G_NSA) as g:
                pe.wait_ge(k_staged, g + 1)
                pe.wait_ge(v_staged, g + 1)
                hold(pe, q_staged, g + 1, passed)
                A.tensor(pe, g)

        @block.scalar
        def _(act):
            with act.Fori(0, G_NSA) as g:
                act.wait_ge(A.valued, g * A.NG + A.FREE_VALUED)
                for h in range(2 * PER_G):
                    last = nc.scalar.activation(q[:, h:h + 1, :], R["nsaT"][:, bass.ds(2 * PER_G * g + h, 1), :],
                                                ACT.Copy, scale=DH ** -0.5)
                last.then_inc(q_staged, 1)
                A.scalar(act, g, lambda pair: R["mixT"][:, bass.ds(PER_G * g + pair + H_MLA // 2, 1), :])

        @block.vector
        def _(dve):
            with dve.Fori(0, G_NSA) as g:
                dve.wait_ge(A.valued, g * A.NG + A.FREE_VALUED)
                nc.vector.tensor_copy(k[:, 0:1, :], R["nsaT"][:, bass.ds(g + 8, 1), :])
                nc.vector.tensor_copy(k[:, 1:2, :], R["nsaT"][:, bass.ds(g + 10, 1), :])
                nc.vector.tensor_copy(kc[:].rearrange("p (a n) -> p a n", a=1), R["kcT"][:, bass.ds(g, 1), :]
                                      ).then_inc(k_staged, 1)
                for branch, place in ((0, 1), (1, 2), (2, 0)):
                    of = R["gates"][:, :, bass.ds(g * (6 * PER_G), 6 * PER_G)].rearrange("p t (h b) -> p t h b", b=3)
                    last = nc.vector.tensor_copy(gp[:, :, :, place:place + 1], of[:, :, :, branch:branch + 1])
                last.then_inc(g_staged, 1)
                dve.wait_ge(g_staged, g + 1)
                A.vector(dve, g)


class OutWeights:

    def __init__(self, nc, M, a):
        self.dram = a["w_out"].rearrange("l (k p) d -> (l p) k d", p=P)
        self.rows = []
        self.loaded = [M.sem(f"w_out{k}") for k in range(KT)]

    def rooms(self, rooms):
        for w in rooms:
            pair = w[:].rearrange("p k f -> p (k f)").rearrange("p (two d) -> p two d", two=2)
            self.rows += [pair[:, 0, :], pair[:, 1, :]]

    def load(self, sp, ks):
        for k in ks:
            sp.dma_start(self.rows[k], self.dram[:, k]).then_inc(self.loaded[k], 16)


def route(nc, C, R, W, w_out, a):
    with ExitStack() as ctx:
        M = Mem(nc, ctx, C["sems"])
        rw, rb = M.sb("r_rw", [P, KT, NE]), M.sb("r_rb", [P, NE])
        g_ffn = M.sb("r_gffn", [P, D])
        mix_hi, mix_lo = M.sb("r_mixh", [P, KT, P], F32R), M.sb("r_mixl", [P, KT, P], F32R)
        parts = [M.sb(f"r_parts{k}", [P, 2 * D], F32R) for k in range(KT)]
        w_hi, w_lo = [w[:, 0:D] for w in parts], [w[:, D:2 * D] for w in parts]
        x_t, h_t, hn_t = M.sb("r_x", [P, D]), M.sb("r_h", [P, D]), M.sb("r_hn", [P, D])
        junk = M.sb("r_junk", [P, D], BF16)
        hnT = M.sb("r_hnT", [P, KT, P])
        lg_t, top_t, top_i = M.sb("r_lgt", [P, NE]), M.sb("r_top", [P, 8]), M.sb("r_topi", [P, 8], U32)
        top_f, hot = M.sb("r_topf", [P, TOPK]), M.sb("r_hot", [P, TOPK, NE])
        lg = M.sb("r_lg", [P, NT, NE])
        took, took_b = M.sb("r_took", [P, NT, NE]), M.sb("r_tookb", [P, NT, NE], BF16)
        ss, rec, rstd = M.sb("r_ss", [P, 1]), M.sb("r_rec", [P, 1]), M.sb("r_rstd", [P, 1])
        se = M.sb("r_se", [P, NT])
        more, cum2 = M.sb("r_more", [P, NE]), M.sb("r_cum2", [P, NE])
        cnt, cum = W.cnt, W.cum
        zeros = M.sb("r_zeros", [P, D])[:]
        rest = M.sb("r_rest", [P, NT, NE])[:]
        pM = M.ps("r_pM", [P, D])
        pX = [M.ps(f"r_pX{i}", [P, 4, P]) for i in range(2)]
        pL = M.ps("r_pL", [P, NE])
        pP, pC = M.ps("r_pP", [P, NT, NE]), M.ps("r_pC", [P, NE])
        s = lambda x: M.sem("r_" + x)
        rld, x_in, mixed, product = s("rld"), s("xin"), s("mixed"), s("prod")
        summed, sq, rec_r, rstd_r, normed = s("sum"), s("sq"), s("rec"), s("rstd"), s("norm")
        h_out, hn_out, turned, x0_read, x1_read = s("hout"), s("hnout"), s("turned"), s("x0"), s("x1")
        logits_done, l_read = s("logits"), s("lread")
        zero, z_out, own, e_in, e_out, took_r, posd = s("z"), s("zout"), s("own"), s("ein"), s("eout"), s("took"), s("pos")
        passed, known, w_rounded, w_split = s("passed"), s("known"), s("whi"), s("wlo")
        block = ctx.enter_context(nc.Block())
        x_rows = a["x"].rearrange("b (t p) d -> (b t) p d", p=P)
        tiles = lambda dram: dram[0:SEQ].rearrange("(t p) d -> t p d", p=P)
        one_of = lambda v, t: v[bass.ds(t, 1)].rearrange("a p d -> (a p) d")

        @block.sync
        def _(sp):
            w_out.load(sp, range(2, 4))
            sp.dma_start(x_t[:], x_rows[0]).then_inc(x_in, 16)
            w_out.load(sp, range(4, KT))
            sp.dma_start(rw[:], a["router_w"].rearrange("l (k p) e -> (l p) k e", p=P)).then_inc(rld, 16)
            sp.dma_start(g_ffn[:], a["ffn_norm"].to_broadcast([P, D])).then_inc(rld, 16)
            sp.dma_start(rb[:], a["router_b"].to_broadcast([P, NE])).then_inc(rld, 16)
            early = [[FC, FC + 1], [FC + 2, FC + 3]] + [[c] for c in range(FIRST)]
            for t in range(1, NT):
                if t == 1:
                    sp.wait_ge(w_split, KT)
                sp.wait_ge(summed, 2 * t)
                sp.dma_start(x_t[:], x_rows[t]).then_inc(x_in, 16)
                W.load(sp, 0, first=True, chunks=early[t - 1] if t <= len(early) else [])

        @block.gpsimd
        def _(pool):
            def stage(t, h):
                ks = slice(4 * h, 4 * h + 4)
                of = R["mixT"][:, ks, bass.ds(t * P, P)]
                pool.tensor_copy(mix_hi[:, ks], of).then_inc(mixed, 1)
                hold(pool, mixed, 4 * t + 2 * h + 1, passed)
                pool.tensor_tensor(mix_lo[:, ks], of, mix_hi[:, ks].bitcast(F32), ALU.subtract).then_inc(mixed, 1)
                pool.wait_ge(mixed, 4 * t + 2 * h + 2)
            stage(0, 0)
            stage(0, 1)
            for c, src in ((0, C["iota_p"][:].unsqueeze(2)), (1, C["iota_t"][:].unsqueeze(2)), (2, C["ones_b"][:, 0:1].unsqueeze(2))):
                pool.tensor_copy(W.facts[:, :, :, c], src.to_broadcast([P, NT, NE])).then_inc(known, 1)
                pool.wait_ge(known, c + 1)
            with pool.Fori(1, NT) as t:
                for h in range(2):
                    pool.wait_ge(product, 3 * t - 2 + 2 * h)
                    stage(t, h)

        @block.tensor
        def _(pe):
            def products(t, ks, first=False):
                if ks[0] == 0:
                    pe.wait_ge(mixed, 4 * t + 2)
                if ks[0] == 4:
                    pe.wait_ge(mixed, 4 * t + 4)
                steps = [(k, i) for k in ks for i in range(2)]
                if ks[0] == 6 or ks[0] == 0 and not first:
                    steps.sort(key=lambda s: s[1])
                for k, i in steps:
                    if k == 0 and not first:
                        pe.wait_ge(summed, 2 * t - 1 + i)
                    if first and i == 0:
                        pe.wait_ge(w_rounded, k + 1)
                        pe.wait_ge(w_split, k + 1)
                    c = slice(i * 512, (i + 1) * 512)
                    for j, (x, w) in enumerate(((mix_hi, w_hi), (mix_hi, w_lo), (mix_lo, w_hi))):
                        last = nc.tensor.matmul(pM[:, c], x[:, k, :], w[k][:, c], start=(k == 0 and j == 0),
                                                stop=(k == KT - 1 and j == 2))
                    if k == KT - 1 or (k, i) == (3, 1):
                        last.then_inc(product, 1)

            def turn(t):
                pe.wait_ge(normed, t + 1)
                for k in range(KT):
                    if k == 0:
                        pe.wait_ge(x0_read, t + 1)
                    if k == 4:
                        pe.wait_ge(x1_read, t + 1)
                    last = nc.tensor.transpose(pX[k // 4][:, k % 4, :], hn_t[:, place_of(k):place_of(k) + P],
                                               C["ident"][:])
                    if k % 4 == 3:
                        last.then_inc(turned, 1)

            def router(t):
                pe.wait_ge(x0_read, t + 2)
                pe.wait_ge(x1_read, t + 2)
                hold(pe, l_read, t + 1, passed)
                for k in range(KT):
                    last = nc.tensor.matmul(pL[:], hnT[:, k, :], rw[:, k, :], start=(k == 0), stop=(k == KT - 1))
                last.then_inc(logits_done, 1)

            for q in (x0_read, x1_read, l_read):
                pe.sem_inc(q, 1)
            products(0, (0, 1, 2, 3), True)
            products(0, (4, 5), True)
            products(0, (6, 7), True)
            pe.wait_ge(rld, 48)
            with pe.Fori(1, NT) as t:
                products(t, (0, 1, 2, 3))
                turn(t - 1)
                products(t, (4, 5))
                router(t - 1)
                products(t, (6, 7))
            turn(NT - 1)
            router(NT - 1)
            pe.wait_ge(took_r, 1)
            for j in range(NT):
                nc.tensor.matmul(pC[:], C["ones_b"][:], took_b[:, j, :], start=(j == 0), stop=(j == NT - 1))
            for t in range(NT):
                for j in range(t):
                    nc.tensor.matmul(pP[:, t, :], C["ones_b"][:], took_b[:, j, :], start=(j == 0), stop=False)
                last = nc.tensor.matmul(pP[:, t, :], C["before"][:], took_b[:, t, :], start=(t == 0), stop=True)
            last.then_inc(posd, 1)

        @block.scalar
        def _(act):
            def squares(t):
                act.wait_ge(summed, 2 * t + 2)
                act.dma_start(one_of(tiles(R["acc"]), t), h_t[:]).then_inc(h_out, 16)
                nc.scalar.activation(junk[:], h_t[:], ACT.Square, accum_out=ss[:]).then_inc(sq, 1)
                act.wait_ge(rec_r, t + 1)
                nc.scalar.activation(rstd[:], rec[:], ACT.Sqrt).then_inc(rstd_r, 1)
                act.wait_ge(normed, t + 1)
                act.dma_start(one_of(tiles(R["hn"]), t), hn_t[:]).then_inc(hn_out, 16)

            def turned_half(t):
                act.wait_ge(turned, 2 * t + 1)
                nc.scalar.copy(hnT[:, 0:4, :], pX[0][:]).then_inc(x0_read, 1)

            for k in range(KT):
                act.wait_ge(w_out.loaded[k], 16)
                nc.scalar.copy(w_hi[k], w_out.rows[k]).then_inc(w_rounded, 1)
            squares(0)
            with act.Fori(1, NT) as t:
                turned_half(t - 1)
                squares(t)
                hold(act, logits_done, t, passed)
            turned_half(NT - 1)
            act.wait_ge(zero, 1)
            for d in (R["acc"], R["hn"]):
                for i in range(DUMP // P):
                    act.dma_start(d[SEQ + i * P:SEQ + (i + 1) * P, :], zeros).then_inc(z_out, 16)
            act.wait_ge(e_in, NT)
            nc.scalar.activation(lg[:], lg[:], ACT.Exp).then_inc(e_out, 1)
            act.wait_ge(h_out, 16 * NT)
            act.wait_ge(hn_out, 16 * NT)
            act.wait_ge(z_out, 16 * 2 * DUMP // P)

        @block.vector
        def _(dve):
            V = nc.vector
            B = lambda x, n: x.to_broadcast(n)

            def residual(t, first=False):
                dve.wait_ge(x_in, 16 * t + 16)
                if not first:
                    dve.wait_ge(h_out, 16 * t)
                for i in range(2):
                    dve.wait_ge(product, 3 * t + 2 + i)
                    pairs = slice(2 * i, 2 * i + 2)
                    V.tensor_tensor(stored(h_t[:])[:, :, pairs], natural(pM[:])[:, :, pairs],
                                    natural(x_t[:])[:, :, pairs], ALU.add).then_inc(summed, 1)

            def norm(t, S, first=False):
                dve.wait_ge(sq, t + 1)
                S.mark(V.tensor_scalar(rec[:], ss[:], 1.0 / D, EPS, ALU.mult, ALU.add))
                S.wait(dve)
                V.reciprocal(rec[:], rec[:]).then_inc(rec_r, 1)
                dve.wait_ge(rstd_r, t + 1)
                if not first:
                    dve.wait_ge(hn_out, 16 * t)
                    dve.wait_ge(turned, 2 * t)
                for h in range(2):
                    last = V.scalar_tensor_tensor(stored(hn_t[:])[:, h], stored(h_t[:])[:, h], rstd[:],
                                                  natural(g_ffn[:])[:, h], ALU.mult, ALU.mult)
                last.then_inc(normed, 1)

            def turned_half(t):
                dve.wait_ge(turned, 2 * t + 2)
                V.tensor_copy(hnT[:, 4:8, :], pX[1][:]).then_inc(x1_read, 1)

            def top(t, S):
                dve.wait_ge(logits_done, t + 1)
                V.tensor_tensor(lg_t[:], pL[:], rb[:], ALU.add).then_inc(l_read, 1)
                hold(dve, l_read, t + 2, passed)
                S.mark(V.max(top_t[:], lg_t[:]))
                S.wait(dve)
                V.tensor_tensor(lg[:, bass.ds(t, 1), :], lg_t[:].unsqueeze(1),
                                B(top_t[:, 0:1].unsqueeze(1), [P, 1, NE]), ALU.subtract).then_inc(e_in, 1)
                S.mark(V.max_index(top_i[:], top_t[:], lg_t[:]))
                S.wait(dve)
                S.mark(V.tensor_copy(top_f[:], top_i[:, 0:TOPK]))
                S.wait(dve)
                S.mark(V.tensor_tensor(hot[:], B(top_f[:].unsqueeze(2), [P, TOPK, NE]),
                                       B(C["iota"][:, 0:NE].unsqueeze(1), [P, TOPK, NE]), ALU.is_equal))
                S.wait(dve)
                S.mark(V.tensor_reduce(took[:, bass.ds(t, 1), :], hot[:].rearrange("p k (a e) -> p a e k", a=1),
                                       AX_X, ALU.add))

            TURN = 6
            S = Steps(own)
            for k in range(KT):
                dve.wait_ge(w_rounded, k + 1)
                V.tensor_tensor(w_lo[k], w_out.rows[k], w_hi[k].bitcast(F32), ALU.subtract).then_inc(w_split, 1)
            residual(0, True)
            dve.wait_ge(rld, 48)
            norm(0, S, True)
            n0 = S.n
            with dve.Fori(1, NT) as t:
                S = Steps(own, (t - 1) * TURN + n0)
                turned_half(t - 1)
                residual(t)
                top(t - 1, S)
                norm(t, S)
            assert S.n == TURN, S.n
            S = Steps(own, (NT - 1) * TURN + n0)
            turned_half(NT - 1)
            V.memset(zeros, 0.0).then_inc(zero, 1)
            top(NT - 1, S)
            S.wait(dve)
            V.tensor_copy(took_b[:], took[:]).then_inc(took_r, 1)
            dve.wait_ge(posd, 1)
            S.mark(V.tensor_copy(cnt[:], pC[:]))
            S.mark(V.scalar_tensor_tensor(W.place[:], pP[:], 1.0, took[:], ALU.add, ALU.mult))
            S.wait(dve)
            S.mark(V.tensor_scalar(W.place[:], W.place[:], -1.0, None, ALU.add))
            S.mark(V.tensor_scalar(more[:], cnt[:], float(CAP), None, ALU.is_gt))
            for j in range(2, MORE + 1):
                S.wait(dve)
                S.mark(V.scalar_tensor_tensor(more[:], cnt[:], float(CAP * j), more[:], ALU.is_gt, ALU.add))
            src, dst, other = more, cum, cum2
            for d in (1, 2, 4, 8, 16):
                S.wait(dve)
                S.mark(V.tensor_copy(dst[:, 0:d], src[:, 0:d]))
                S.mark(V.tensor_tensor(dst[:, d:], src[:, d:], src[:, 0:NE - d], ALU.add))
                src, dst, other = dst, other, dst
            assert src is cum
            S.wait(dve)
            S.mark(V.tensor_copy(W.items[:, 0:NE, 0], C["iota"][:, 0:NE]))
            S.mark(V.tensor_copy(W.items[:, 0:NE, 1], cnt[:]))
            S.mark(V.memset(W.items[:, 0:NE, 3], 0.0))
            S.mark(V.tensor_scalar(W.items[:, 0:NE, 2], B(cum[:, NE - 1:NE], [P, NE]), float(NE), None, ALU.add))
            S.wait(dve)
            S.mark(V.tensor_copy(W.tab_f[:, 0:NE], W.items[:, 0:NE, 3]))
            S.mark(V.tensor_copy(W.tab[:, 0:NE], W.items[:, 0:NE]))
            dve.wait_ge(e_out, 1)
            S.mark(V.tensor_tensor(lg[:], lg[:], took[:], ALU.mult))
            S.wait(dve)
            S.mark(V.tensor_reduce(se[:], lg[:], AX_X, ALU.add))
            S.wait(dve)
            S.mark(V.reciprocal(se[:], se[:]))
            S.wait(dve)
            S.mark(V.tensor_tensor(lg[:], lg[:], B(se[:].unsqueeze(2), [P, NT, NE]), ALU.mult))
            S.wait(dve)
            S.mark(V.tensor_copy(W.facts[:, :, :, 3], lg[:]))
            S.wait(dve)
            S.mark(V.tensor_tensor(rest, lg[:], W.facts[:, :, :, 3], ALU.subtract))
            S.wait(dve)
            S.mark(V.tensor_copy(W.facts[:, :, :, 4], rest))
            S.wait(dve)
            S.mark(V.tensor_tensor(rest, rest, W.facts[:, :, :, 4], ALU.subtract))
            S.wait(dve)
            S.mark(V.tensor_copy(W.facts[:, :, :, 5], rest))
            S.wait(dve)


class Weights:

    def __init__(self, nc, M, room, a):
        self.a = a
        self.w1 = []
        self.rooms(M, FIRST)
        self.w2 = [room] + [M.sb(f"w2_{c}", [P, DFF // P, D // DC]) for c in range(1, DC)]
        self.tab = M.sb("tab", [P, MAX_ITEMS, 4], I32)
        self.tab_f = M.sb("tab_f", [P, MAX_ITEMS])
        self.facts = M.sb("facts", [P, NT, NE, 6], BF16)
        self.place = M.sb("place", [P, NT, NE])
        self.items = M.sb("items", [P, MAX_ITEMS, 4])
        self.cnt, self.cum = M.sb("cnt", [P, NE]), M.sb("cum", [P, NE])
        self.w1_in = [M.sem(f"w1in{c}") for c in range(FC)]
        self.w2_in = [M.sem(f"w2in{c}") for c in range(DC)]
        self.up_done, self.down_done = M.sem("up_done"), M.sem("down_done")

    def rooms(self, M, n):
        self.w1 += [M.sb(f"w1_{len(self.w1) + i}", [P, KT, 2, P]) for i in range(n)]

    def load(self, sp, n, e=0, first=False, chunks=range(FC + DC)):
        w1 = self.a["moe_w1"].rearrange("l e (k p) (two c f) -> c (l e) two p k f", p=P, two=2, f=P)
        w2 = self.a["moe_w2"].rearrange("l e (k p) (c d) -> c (l e) p k d", p=P, c=DC)
        for c in (c for c in chunks if c < FC):
            if not first:
                sp.wait_ge(self.up_done, FC * (n - 1) + c + 1)
            for two in range(2):
                sp.dma_start(self.w1[c][:, :, two, :], w1[c, bass.ds(e, 1), two].rearrange("a p k f -> (a p) k f")
                             ).then_inc(self.w1_in[c], 16)
        for c in (c - FC for c in chunks if c >= FC):
            if not first:
                sp.wait_ge(self.down_done, DC * (n - 1) + c + 1)
            sp.dma_start(self.w2[c][:], w2[c, bass.ds(e, 1)].rearrange("a p k d -> (a p) k d")
                         ).then_inc(self.w2_in[c], 16)


def experts(nc, C, R, W):
    with ExitStack() as ctx:
        M = Mem(nc, ctx, C["sems"])
        W.rooms(M, FC - FIRST)
        place_e, facts_e = M.sb("e_place", [P, NT]), M.sb("e_facts", [P, NT, 6], BF16)
        slots = M.sb("e_slots", [P, 2 * P])
        onehot = M.sb("e_onehot", [P, NT, 2 * P], BF16)
        told = M.sb("e_told", [P, 2, 6])
        tmp = M.sb("e_tmp", [P, 4, 2])
        dump, half = M.sb("e_dump", [P, 2]), M.sb("e_half", [P, 2])
        extra = M.sb("e_extra", [P, 3, EXTRA])
        is_e, sums = M.sb("e_ise", [P, EXTRA, NE]), M.sb("e_sums", [P, EXTRA, NE])
        idx_next, idx = M.sb("e_idxn", [P, 2], I32), M.sb("e_idx", [P, 2], I32)
        gate_next, gate = M.sb("e_gaten", [P, 2]), M.sb("e_gate", [P, 2])
        x0, x1 = M.sb("e_x0", [P, D]), M.sb("e_x1", [P, D // 2])
        xT = M.sb("e_xT", [P, KT, CAP])
        b1, b2 = M.sb("e_b1", [P, 2 * FC]), M.sb("e_b2", [P, KT])
        g1, g2, up = M.sb("e_g1", [P, 2, CAP]), M.sb("e_g2", [P, 2, CAP]), M.sb("e_up", [P, 2, CAP])
        sg = M.sb("e_sg", [P, 2, CAP])
        hT = M.sb("e_hT", [P, FC, CAP])
        yT0, yT1 = M.sb("e_yT0", [P, KT, P]), M.sb("e_yT1", [P, KT, REST])
        y0, y1 = M.sb("e_y0", [P, D]), M.sb("e_y1", [P, D // 2])
        pH = [M.ps(f"e_pH{i}", [P, 2, 256]) for i in range(2)]
        pY = [M.ps(f"e_pY{i}", [P, 2, 256]) for i in range(2)]
        pX = [M.ps(f"e_pX{i}", [P, 4, P]) for i in range(2)]
        pD = M.ps("e_pD", [P, 2, 8])
        s = lambda x: M.sem("e_" + x)
        cleared, cleared_y, picked, told_ready, idx_ready = s("clr"), s("clry"), s("picked"), s("told"), s("idx")
        gathered, cur_ready = [s("ga0"), s("ga1")], s("cur")
        bank_turned, bank_read = [s("bt0"), s("bt1")], [s("br0"), s("br1")]
        h_read, lin_ready, sg_ready, h_ready = s("hread"), s("lin"), s("sg"), s("h")
        yT_ready, scat, scattered = s("yT"), [s("sc0"), s("sc1")], s("scattered")
        own_d, own_a, b_staged, passed = s("od"), s("oa"), s("bst"), s("passed")
        table_ready = s("table")
        block = ctx.enter_context(nc.Block())
        PER, FREE = 4, 1

        def seq_late(n):
            return 2 + PER * n

        def seq_x(n):
            return 3 + PER * n

        def seq_early(n):
            return 5 + PER * n

        half_rows = lambda dram: dram.rearrange("r (h c) -> (r h) c", h=2)

        def n_items(eng):
            return eng.value_load(W.tab[0:1, 0, 2:3], min_val=NE, max_val=NE + SEQ * TOPK // CAP)

        def expert(eng, n):
            return eng.value_load(W.tab[0:1, bass.ds(n, 1), 0:1].rearrange("p a c -> p (a c)"),
                                  min_val=0, max_val=NE - 1)

        @block.sync
        def _(sp):
            for b in range(2):
                sp.wait_ge(gathered[b], 16)
            W.load(sp, 0, first=True, chunks=range(FIRST, FC))
            last = n_items(sp)
            with sp.Fori(1, last) as n:
                W.load(sp, n, expert(sp, n))

        @block.gpsimd
        def _(pool):
            def gather(i):
                hold(pool, idx_ready, i + 1, passed)
                pool.indirect_dma_start(x0[:], None, R["hn"], bass.IndirectOffsetOnAxis(idx_next[:, 0:1], 0)
                                        ).then_inc(gathered[0], 16)
                pool.indirect_dma_start(x1[:], None, half_rows(R["hn"]), bass.IndirectOffsetOnAxis(idx_next[:, 1:2], 0)
                                        ).then_inc(gathered[1], 16)
            last = n_items(pool)
            gather(0)
            for c, t in enumerate((yT0[:, 4:8], yT1[:, 4:8], y0[:], y1[:])):
                pool.memset(t, 0.0).then_inc(cleared_y, 1)
                pool.wait_ge(cleared_y, c + 1)
            def scatter(n):
                for b in range(2):
                    hold(pool, bank_read[b], seq_late(n) + 1 + FREE, passed)
                pool.indirect_dma_start(R["acc"], bass.IndirectOffsetOnAxis(idx[:, 0:1], 0), y0[:], None,
                                        compute_op=ALU.add).then_inc(scat[0], 16)
                pool.indirect_dma_start(half_rows(R["acc"]), bass.IndirectOffsetOnAxis(idx[:, 1:2], 0), y1[:], None,
                                        compute_op=ALU.add).then_inc(scat[1], 16)
                for b in range(2):
                    pool.wait_ge(scat[b], 16 * n + 16)
                pool.sem_inc(scattered, 1)

            with pool.Fori(0, last) as n:
                scatter(n)
                gather(n + 1)
            scatter(last)
            for b in range(2):
                pool.wait_ge(gathered[b], 16)

        @block.tensor
        def _(pe):
            def pick(i):
                pe.wait_ge(picked, i + 1)
                for j in range(2):
                    for t in range(NT):
                        last = nc.tensor.matmul(pD[:, j, 0:6], onehot[:, t, j * P:(j + 1) * P],
                                                facts_e[:, t, :], start=(t == 0), stop=(t == NT - 1))
                last.then_inc(told_ready, 1)

            def turn_x(i, seq, steps):
                for j in steps:
                    pe.wait_ge(bank_read[j % 2], seq + j // 2 + FREE)
                    for m in range(2):
                        c = place_of(2 * j + m)
                        nc.tensor.transpose(pX[j % 2][:, m, :], x0[:, c:c + P], C["ident"][:])
                    last = nc.tensor.transpose(pX[j % 2][:, 2, :], x1[:, j * P:(j + 1) * P], C["ident"][:])
                    last.then_inc(bank_turned[j % 2], 1)

            def turn_y(n, c):
                if c < 2:
                    pe.wait_ge(yT_ready, DC * n + c + 1 + 2)
                    pe.wait_ge(bank_read[c % 2], seq_early(n) + FREE)
                else:
                    pe.wait_ge(yT_ready, DC * n + c + 1 + 2 - DC)
                    pe.wait_ge(bank_read[c % 2], seq_late(n) + FREE)
                for m in range(2):
                    nc.tensor.transpose(pX[c % 2][:, m, :], yT0[:, 2 * c + m, :], C["ident"][:])
                last = nc.tensor.transpose(pX[c % 2][:, 2, :], yT1[:, 2 * c:2 * c + 2, :].rearrange("p m s -> p (m s)"),
                                           C["ident"][:])
                last.then_inc(bank_turned[c % 2], 1)

            def item(n, N):
                for b in range(2):
                    pe.wait_ge(bank_read[b], PER * n + 1 + FREE)
                for c in range(FC):
                    pe.wait_ge(W.w1_in[c], 32 * n + 32)
                    pe.wait_ge(h_read, FC * n + c + 1)
                    for two in range(2):
                        for k in range(KT):
                            last = nc.tensor.matmul(pH[c % 2][:, two, 0:N], W.w1[c][:, k, two, :], xT[:, k, 0:N],
                                                    start=(k == 0), stop=(k == KT - 1))
                    last.then_inc(W.up_done, 1)
                    if c == 0:
                        turn_y(n, 2)
                        turn_y(n, 3)
                    if c == 3:
                        pick(n + 1)
                for c in range(DC):
                    pe.wait_ge(W.w2_in[c], 16 * n + 16)
                    pe.wait_ge(yT_ready, DC * n + c + 1)
                    steps = [(k, m) for m in range(2) for k in range(DFF // P)]
                    if c == 0:
                        steps.sort(key=lambda s: s[0] == DFF // P - 1)
                    for k, m in steps:
                        if c == 0 and m == 0:
                            pe.wait_ge(h_ready, FC * n + k + 1)
                        if c == 0 and m == 1 and k == 0:
                            for b in range(2):
                                pe.wait_ge(gathered[b], 16 * n + 32)
                        last = nc.tensor.matmul(pY[c % 2][:, m, 0:N], W.w2[c][:, k, m * P:(m + 1) * P],
                                                hT[:, k, 0:N], start=(k, m) == steps[0], stop=(k, m) == steps[-1])
                    last.then_inc(W.down_done, 1)
                    if c < 2:
                        turn_x(n + 1, seq_x(n), (2 * c, 2 * c + 1))
                    if c == 2:
                        turn_y(n, 0)
                        turn_y(n, 1)

            def choose(n, left, variants):
                if len(variants) == 1:
                    item(n, variants[0])
                    return
                half = len(variants) // 2
                with pe.If(left <= variants[half - 1]):
                    choose(n, left, variants[:half])
                with pe.Else():
                    choose(n, left, variants[half:])

            for b in range(2):
                pe.sem_inc(bank_read[b], FREE)
            pe.sem_inc(h_read, 2)
            pe.sem_inc(yT_ready, 2)
            last = n_items(pe)
            pick(0)
            for b in range(2):
                pe.wait_ge(gathered[b], 16)
            turn_x(0, 0, range(4))
            for b in range(2):
                pe.wait_ge(bank_read[b], 2 + FREE)
            pe.wait_ge(cleared, 4)
            pe.wait_ge(cleared_y, 4)
            with pe.Fori(0, last) as n:
                left = pe.value_load(W.tab[0:1, bass.ds(n, 1), 1:2].rearrange("p a c -> p (a c)"),
                                     min_val=-SEQ * 64, max_val=SEQ)
                choose(n, left, VARIANTS)
            turn_y(last, 2)
            turn_y(last, 3)

        @block.scalar
        def _(act):
            def stage_b2(i):
                e = expert(act, i)
                nc.scalar.copy(b2[:], C["b2"][:, bass.ds(e * KT, KT)]).then_inc(own_a, 1)

            def read_x(seq, steps=(0, 2)):
                for j in steps:
                    act.wait_ge(bank_turned[0], seq + j // 2 + 1)
                    nc.scalar.copy(xT[:, 2 * j:2 * j + 2, 0:P], pX[0][:, 0:2, :])
                    nc.scalar.copy(xT[:, 2 * j:2 * j + 2, P:], pX[0][:, 2, :].rearrange("p (m s) -> p m s", m=2)
                                   ).then_inc(bank_read[0], 1)

            stage_b2(0)
            last = n_items(act)
            read_x(0)
            def results(n, c):
                seq = seq_early(n) if c < 2 else seq_late(n)
                act.wait_ge(bank_turned[0], seq + 1)
                nc.scalar.activation(stored(y0[:])[:, :, c, :], pX[0][:, 0:2, :], ACT.Copy, scale=gate[:, 0:1])
                nc.scalar.activation(y1[:, c * P:(c + 1) * P], pX[0][:, 2, :], ACT.Copy, scale=gate[:, 1:2]
                                     ).then_inc(bank_read[0], 1)

            with act.Fori(0, last) as n:
                for c in range(FC):
                    act.wait_ge(lin_ready, FC * n + c + 1)
                    nc.scalar.activation(sg[:, c % 2], g1[:, c % 2], ACT.Sigmoid, scale=ALPHA).then_inc(sg_ready, 1)
                    if c == 0:
                        results(n, 2)
                act.wait_ge(own_a, n + 1)
                for c in range(DC):
                    act.wait_ge(W.down_done, DC * n + c + 1)
                    for m in range(2):
                        k = 2 * c + m
                        nc.scalar.activation(yT0[:, k, :], pY[c % 2][:, m, 0:P], ACT.Identity, bias=b2[:, k:k + 1])
                        ins = nc.scalar.activation(yT1[:, k, :], pY[c % 2][:, m, P:CAP], ACT.Identity,
                                                   bias=b2[:, k:k + 1])
                    ins.then_inc(yT_ready, 1)
                    if c < 2:
                        read_x(seq_x(n), (2 * c,))
                    if c == 2:
                        act.wait_ge(cur_ready, n + 1)
                        results(n, 0)
                act.wait_ge(yT_ready, DC * (n + 1) + 2)
                stage_b2(n + 1)
            results(last, 2)

        @block.vector
        def _(dve):
            V = nc.vector
            B = lambda x, n: x.to_broadcast(n)
            OWN = 3 * FC + 2 + 6

            def prepare(i):
                e = expert(dve, i)
                V.tensor_scalar(place_e[:].unsqueeze(2), W.place[:, :, bass.ds(e, 1)],
                                W.tab_f[:, bass.ds(i, 1)], None, ALU.subtract).then_inc(b_staged, 1)
                V.tensor_copy(facts_e[:].unsqueeze(2), W.facts[:, :, bass.ds(e, 1), :])
                dve.wait_ge(b_staged, 2 * i + 1)
                for t in range(NT):
                    ins = V.tensor_scalar(onehot[:, t, :], slots[:], place_e[:, t:t + 1], None, ALU.is_equal)
                ins.then_inc(picked, 1)

            def stage_b1(i):
                e = expert(dve, i)
                V.tensor_copy(b1[:], C["b1"][:, bass.ds(e * (2 * FC), 2 * FC)]).then_inc(b_staged, 1)

            def addresses(i, S):
                dve.wait_ge(told_ready, i + 1)
                S.mark(V.tensor_copy(told[:], pD[:, :, 0:6]))
                S.wait(dve)
                S.mark(V.tensor_scalar(tmp[:, 0], told[:, :, 2], -1.0, 1.0, ALU.mult, ALU.add))
                S.mark(V.scalar_tensor_tensor(tmp[:, 1], told[:, :, 1], float(P), told[:, :, 0], ALU.mult, ALU.add))
                S.mark(V.tensor_tensor(tmp[:, 2], told[:, :, 3], told[:, :, 4], ALU.add))
                S.wait(dve)
                S.mark(V.tensor_tensor(tmp[:, 0], tmp[:, 0], dump[:], ALU.mult))
                V.tensor_tensor(gate_next[:], tmp[:, 2], told[:, :, 5], ALU.add)
                S.wait(dve)
                S.mark(V.tensor_tensor(tmp[:, 1], tmp[:, 0], tmp[:, 1], ALU.add))
                S.wait(dve)
                V.tensor_copy(idx_next[:, 0:1], tmp[:, 1, 0:1])
                V.scalar_tensor_tensor(idx_next[:, 1:2], tmp[:, 1, 1:2], 2.0, half[:, 1:2], ALU.mult, ALU.add
                                       ).then_inc(idx_ready, 1)

            def read_x(seq):
                for j in (1, 3):
                    dve.wait_ge(bank_turned[1], seq + j // 2 + 1)
                    V.tensor_copy(xT[:, 2 * j:2 * j + 2, 0:P], pX[1][:, 0:2, :])
                    V.tensor_copy(xT[:, 2 * j:2 * j + 2, P:], pX[1][:, 2, :].rearrange("p (m s) -> p m s", m=2)
                                  ).then_inc(bank_read[1], 1)

            S = Steps(own_d)
            S.mark(V.memset(gate[:], 0.0))
            S.mark(V.tensor_copy(slots[:, 0:CAP], C["iota"][:]))
            S.mark(V.tensor_copy(slots[:, CAP:], C["iota"][:, P:]))
            S.mark(V.tensor_scalar(dump[:, 0:1], C["iota_p"][:], float(SEQ), None, ALU.add))
            S.mark(V.tensor_scalar(half[:, 1:2], C["iota_p"][:], float(REST), None, ALU.is_ge))
            S.wait(dve)
            S.mark(V.scalar_tensor_tensor(dump[:, 1:2], half[:, 1:2], -float(REST), dump[:, 0:1], ALU.mult, ALU.add))
            S.wait(dve)
            S.mark(V.tensor_scalar(dump[:, 1:2], dump[:, 1:2], float(P), None, ALU.add))
            S.wait(dve)
            prepare(0)
            stage_b1(0)
            addresses(0, S)
            for ps in (*pH, *pY):
                V.memset(ps[:], 0.0).then_inc(cleared, 1)
            S.mark(V.tensor_copy(idx[:, 0:1], dump[:, 0:1]))
            S.mark(V.scalar_tensor_tensor(idx[:, 1:2], dump[:, 1:2], 2.0, half[:, 1:2], ALU.mult, ALU.add))
            S.wait(dve)
            last = n_items(dve)
            read_x(0)
            full = [P, EXTRA, NE]
            x_no, experts_no, items = C["iota"][:, 0:EXTRA], C["iota"][:, 0:NE], W.items
            S.mark(V.tensor_tensor(is_e[:], B(W.cum[:].unsqueeze(1), full), B(x_no.unsqueeze(2), full), ALU.is_le))
            S.mark(V.tensor_copy(items[:, NE:, 2], B(items[:, 0:1, 2], [P, EXTRA])))
            S.wait(dve)
            S.mark(V.tensor_tensor(sums[:], is_e[:], B(W.cum[:].unsqueeze(1), full), ALU.mult))
            S.mark(V.tensor_reduce(items[:, NE:, 0], is_e[:], AX_X, ALU.add))
            S.wait(dve)
            S.mark(V.tensor_reduce(extra[:, 0, :], sums[:], AX_X, ALU.max))
            S.mark(V.tensor_scalar(items[:, NE:, 0], items[:, NE:, 0], float(NE - 1), None, ALU.min))
            S.wait(dve)
            S.mark(V.tensor_tensor(is_e[:], B(experts_no.unsqueeze(1), full), B(items[:, NE:, 0:1], full), ALU.is_equal))
            S.mark(V.tensor_tensor(extra[:, 2, :], x_no, extra[:, 0, :], ALU.subtract))
            S.wait(dve)
            S.mark(V.tensor_tensor(is_e[:], is_e[:], B(W.cnt[:].unsqueeze(1), full), ALU.mult))
            S.mark(V.tensor_scalar(items[:, NE:, 3], extra[:, 2, :], float(CAP), float(CAP), ALU.mult, ALU.add))
            S.wait(dve)
            S.mark(V.tensor_reduce(extra[:, 1, :], is_e[:], AX_X, ALU.add))
            S.wait(dve)
            S.mark(V.tensor_tensor(items[:, NE:, 1], extra[:, 1, :], items[:, NE:, 3], ALU.subtract))
            S.mark(V.tensor_copy(W.tab_f[:, NE:], items[:, NE:, 3]))
            S.wait(dve)
            V.tensor_copy(W.tab[:, NE:], items[:, NE:]).then_inc(table_ready, 1)
            dve.wait_ge(table_ready, 1)

            def results(n, c):
                seq = seq_early(n) if c < 2 else seq_late(n)
                dve.wait_ge(bank_turned[1], seq + 1)
                V.tensor_scalar(stored(y0[:])[:, :, c, :], pX[1][:, 0:2, :], gate[:, 0:1], None, ALU.mult)
                V.tensor_scalar(y1[:, c * P:(c + 1) * P], pX[1][:, 2, :], gate[:, 1:2], None, ALU.mult
                                ).then_inc(bank_read[1], 1)

            n0 = S.n
            with dve.Fori(0, last) as n:
                S = Steps(own_d, n * OWN + n0)
                dve.wait_ge(b_staged, 2 * n + 2)
                for c in range(FC):
                    dve.wait_ge(W.up_done, FC * n + c + 1)
                    S.mark(V.tensor_scalar(g1[:, c % 2], pH[c % 2][:, 0, 0:CAP], b1[:, c:c + 1], LIMIT, ALU.add, ALU.min))
                    V.tensor_scalar(up[:, c % 2], pH[c % 2][:, 1, 0:CAP], b1[:, FC + c:FC + c + 1], LIMIT,
                                    ALU.add, ALU.min).then_inc(h_read, 1)
                    V.drain().then_inc(lin_ready, 1)
                    dve.wait_ge(lin_ready, FC * n + c + 1)
                    S.mark(V.tensor_scalar(up[:, c % 2], up[:, c % 2], -LIMIT, 1.0, ALU.max, ALU.add))
                    dve.wait_ge(sg_ready, FC * n + c + 1)
                    S.mark(V.tensor_tensor(g2[:, c % 2], g1[:, c % 2], sg[:, c % 2], ALU.mult))
                    S.wait(dve)
                    V.tensor_tensor(hT[:, c, :], g2[:, c % 2], up[:, c % 2], ALU.mult).then_inc(h_ready, 1)
                    if c == 0:
                        results(n, 3)
                    if c == 1:
                        prepare(n + 1)
                    if c == 4:
                        dve.wait_ge(scattered, n + 1)
                        dve.wait_ge(bank_read[0], seq_late(n) + 1 + FREE)
                        dve.wait_ge(idx_ready, n + 1)
                        for b in range(2):
                            dve.wait_ge(gathered[b], 16 * n + 16)
                        S.mark(V.tensor_copy(idx[:], idx_next[:]))
                        S.mark(V.tensor_copy(gate[:], gate_next[:]))
                        S.wait(dve)
                        dve.sem_inc(cur_ready, 1)
                        addresses(n + 1, S)
                stage_b1(n + 1)
                read_x(seq_x(n))
                dve.wait_ge(cur_ready, n + 1)
                results(n, 1)
            results(last, 3)
            assert S.n == OWN, S.n


def final(nc, C, R, a, out):
    HALVES = NT // 2
    with ExitStack() as ctx:
        M = Mem(nc, ctx, C["sems"])
        h, o = M.sb("f_h", [P, NT, D]), M.sb("f_o", [P, NT, D])
        g = M.sb("f_g", [P, D])
        junk = M.sb("f_junk", [P, NT, D], BF16)
        ss, rec, rstd = M.sb("f_ss", [P, NT]), M.sb("f_rec", [P, NT]), M.sb("f_rstd", [P, NT])
        h_in = [M.sem(f"f_in{t}") for t in range(NT)]
        g_in, sq, own, rec_r, rstd_r, done, written = (M.sem("f_" + s) for s in ("g", "sq", "own", "rec", "rstd", "done", "st"))
        block = ctx.enter_context(nc.Block())
        acc = R["acc"][0:SEQ].rearrange("(t p) d -> t p d", p=P)
        res = out.rearrange("b (t p) d -> (b t) p d", p=P)

        @block.sync
        def _(sp):
            sp.dma_start(g[:], a["final_norm"].rearrange("(l d) -> l d", l=1).to_broadcast([P, D])).then_inc(g_in, 16)
            for t in range(NT):
                sp.dma_start(h[:, t, :], acc[t]).then_inc(h_in[t], 16)
            for t in range(NT):
                sp.wait_ge(done, t + 1)
                sp.dma_start(res[t], o[:, t, :]).then_inc(written, 16)
            sp.wait_ge(written, 16 * NT)

        @block.scalar
        def _(act):
            for t in range(NT):
                act.wait_ge(h_in[t], 16)
                nc.scalar.activation(junk[:, t], h[:, t, :], ACT.Square, accum_out=ss[:, t:t + 1]).then_inc(sq, 1)
                if t >= 1:
                    act.wait_ge(rec_r, t)
                    nc.scalar.activation(rstd[:, t - 1:t], rec[:, t - 1:t], ACT.Sqrt).then_inc(rstd_r, 1)
            act.wait_ge(rec_r, NT)
            nc.scalar.activation(rstd[:, NT - 1:], rec[:, NT - 1:], ACT.Sqrt).then_inc(rstd_r, 1)

        @block.vector
        def _(dve):
            dve.wait_ge(g_in, 16)
            for t in range(NT + 1):
                if t < NT:
                    dve.wait_ge(sq, t + 1)
                    nc.vector.tensor_scalar(rec[:, t:t + 1], ss[:, t:t + 1], 1.0 / D, EPS, ALU.mult, ALU.add
                                            ).then_inc(own, 1)
                    dve.wait_ge(own, t + 1)
                    nc.vector.reciprocal(rec[:, t:t + 1], rec[:, t:t + 1]).then_inc(rec_r, 1)
                if t >= 1:
                    dve.wait_ge(rstd_r, t)
                    for half in range(2):
                        last = nc.vector.scalar_tensor_tensor(
                            natural(o[:, t - 1, :])[:, half], stored(h[:, t - 1, :])[:, half], rstd[:, t - 1:t],
                            natural(g[:])[:, half], ALU.mult, ALU.mult)
                    last.then_inc(done, 1)


def layer(nc, a, out, upto=None, debug=None):
    R = {k: nc.dram_tensor(k, (SEQ + DUMP, D), F32, kind="Internal").ap() for k in ("acc", "hn")}
    with ExitStack() as whole:
        M = Mem(nc, whole)
        C = {
            "sems": [],
            "ident": M.sb("ident", [P, P]), "ident_b": M.sb("ident_b", [P, P], BF16),
            "causal": M.sb("causal", [P, P], BF16), "far": M.sb("far", [P, P], BF16),
            "cmp_mask": M.sb("cmp_mask", [P, NT, 64], BF16), "before": M.sb("before", [P, P], BF16),
            "ones_b": M.sb("ones_b", [P, P], BF16), "late": M.sb("late", [P, 1]),
            "iota_i": M.sb("iota_i", [P, CAP], I32), "iota": M.sb("iota", [P, CAP]),
            "iota_p_i": M.sb("iota_p_i", [P, 1], I32), "iota_p": M.sb("iota_p", [P, 1]),
            "iota_t_i": M.sb("iota_t_i", [P, NT], I32), "iota_t": M.sb("iota_t", [P, NT]),
            "vec": M.sb("vec", [P, 19]), "b1": M.sb("b1", [P, NE * 2 * FC]), "b2": M.sb("b2", [P, NE * KT]),
            "trig": M.sb("trig", [P, 2, NT + 1, NF]),
        }
        with ExitStack() as early:
            with ExitStack() as heads:
                M = Mem(nc, heads)
                R["latT"] = M.sb("latT", [P, 3, SEQ])
                R["nsaT"] = M.sb("nsaT", [96, 12, SEQ])
                R["v_s"], R["v_w"] = M.sb("v_s", [P, NT, KVW]), M.sb("v_w", [P, NT, KVW])
                R["k_pe"] = M.sb("k_pe", [P, NT, ROPE])
                R["gates"] = M.sb("gates", [P, NT, 3 * H_NSA])
                R["kcT"] = M.sb("kcT", [96, G_NSA, 64])
                R["v_c"] = M.sb("v_c", [64, G_NSA, DH])
                with ExitStack() as blocks:
                    M = Mem(nc, blocks, C["sems"])
                    R["rawT"] = M.sb("rawT", [P, 4, SEQ])
                    F = Ahead(nc, M, a, (R["latT"], R["rawT"]))
                    constants(nc, C, F, a)
                    project(nc, C, R, F, a)
                    compress(nc, C, R, F)
                nc.clear_and_free_semaphores(C["sems"])
                nc.all_engine_barrier()
                C["sems"] = []
                R["mixT"] = early.enter_context(nc.sbuf_tensor("mixT", [P, KT, SEQ], F32, side="right"))
                mla(nc, C, R, a)
                room = early.enter_context(nc.sbuf_tensor("w2_0", [P, DFF // P, D // DC], F32, side="right"))
                w_out = OutWeights(nc, Mem(nc, early, C["sems"]), a)
                w_out.rooms([room])
                nsa(nc, C, R, w_out)
            with ExitStack() as late:
                W = Weights(nc, Mem(nc, late, C["sems"]), room, a)
                w_out.rooms(W.w2[1:])
                route(nc, C, R, W, w_out, a)
                experts(nc, C, R, W)
        final(nc, C, R, a, out)


_INS = ["x", "positions", "attn_norm", "w_in", "mla_q_norm", "mla_w_q_up", "mla_kv_norm", "mla_w_kv_up",
        "nsa_cmp_pos", "nsa_cmp_w1", "nsa_cmp_w2", "w_out", "ffn_norm", "router_w", "router_b",
        "moe_w1", "moe_b1", "moe_w2", "moe_b2", "final_norm"]


def kernel(**inputs):
    import numpy as _np
    import concourse.bacc as _bacc
    from concourse import mybir as _mybir
    from concourse.bass_utils import run_bass_kernel_spmd as _run

    nc = _bacc.Bacc("TRN2", target_bir_lowering=False, num_devices=1)
    arrays, args = {}, {}
    for name in _INS:
        x = _np.ascontiguousarray(inputs[name])
        arrays[f"in_{name}"] = x
        args[name] = nc.dram_tensor(f"in_{name}", x.shape, _mybir.dt.from_np(x.dtype), kind="ExternalInput").ap()
    out = nc.dram_tensor("out_0", (1, SEQ, D), F32, kind="ExternalOutput").ap()
    layer(nc, args, out)
    r = _run(nc, [arrays], core_ids=[0])
    return r.results[0]["out_0"]
```
